# Optimizing a Trainium2 kernel written in Bass

```python
import math
import jax
import jax.numpy as jnp
from jax import lax
import numpy as np

D_MODEL = 1024
BATCH = 1
SEQ = 512
DEPTH = 1

N_BRANCH = 4
BR_WIDTH = 512
CONV_K = 4
NORM_EPS = 1e-6

GDN_HEADS = 4
GDN_DK = 128
GDN_DV = 128
GDN_CHUNK = 64

GLA_HEADS = 4
GLA_DK = 64
GLA_DV = 128
GLA_LOWRANK = 16
GLA_GATE_NORMALIZER = 16.0
GLA_CHUNK = 64

SSD_HEADS = 8
SSD_HEADDIM = 64
SSD_STATE = 128
SSD_GROUPS = 2
SSD_CHUNK = 64

NSA_HEADS = 8
NSA_KV_HEADS = 2
NSA_HEADDIM = 64
CMP_BLOCK = 32
CMP_STRIDE = 16
SEL_BLOCK = 64
SEL_TOPK = 16
WINDOW = 512
NSA_QBLOCK = 64
FORCED_SCORE = 1e4

GDN_QK = GDN_HEADS * GDN_DK
GDN_V = GDN_HEADS * GDN_DV
GLA_K = GLA_HEADS * GLA_DK
GLA_V = GLA_HEADS * GLA_DV
SSD_INNER = SSD_HEADS * SSD_HEADDIM
SSD_BC = SSD_GROUPS * SSD_STATE
NSA_Q = NSA_HEADS * NSA_HEADDIM
NSA_KV = NSA_KV_HEADS * NSA_HEADDIM

IN_SPLITS = (
    ('gdn_q', GDN_QK), ('gdn_k', GDN_QK), ('gdn_v', GDN_V), ('gdn_beta', GDN_HEADS), ('gdn_a', GDN_HEADS), ('gdn_z', BR_WIDTH),
    ('gla_q', GLA_K), ('gla_k', GLA_K), ('gla_v', GLA_V), ('gla_gk', GLA_LOWRANK), ('gla_z', BR_WIDTH),
    ('ssd_x', SSD_INNER), ('ssd_b', SSD_BC), ('ssd_c', SSD_BC), ('ssd_dt', SSD_HEADS), ('ssd_z', BR_WIDTH),
    ('nsa_q', NSA_Q), ('nsa_kc', NSA_KV), ('nsa_vc', NSA_KV), ('nsa_ks', NSA_KV), ('nsa_vs', NSA_KV),
    ('nsa_kw', NSA_KV), ('nsa_vw', NSA_KV), ('nsa_gate', 3 * NSA_HEADS), ('nsa_z', BR_WIDTH),
    ('merge_gate', N_BRANCH * D_MODEL),
)
D_IN = sum(w for _, w in IN_SPLITS)
F32 = jnp.float32


def _in_offsets():
    offs, start = {}, 0
    for name, width in IN_SPLITS:
        offs[name] = (start, start + width)
        start += width
    return offs

def _cols(u, offs, first, last):
    return u[..., offs[first][0]:offs[last][1]]

def rmsnorm(x, gain):
    xf = x.astype(F32)
    y = xf * lax.rsqrt(jnp.mean(xf * xf, axis=-1, keepdims=True) + NORM_EPS)
    return (y * gain.astype(F32)).astype(x.dtype)

def l2norm(x):
    return x * lax.rsqrt(jnp.sum(x * x, axis=-1, keepdims=True) + NORM_EPS)

def causal_conv(x, w):
    k_width, ch = w.shape
    return lax.conv_general_dilated(x, w[:, None, :], window_strides=(1,), padding=((k_width - 1, 0),),
                                    dimension_numbers=('NWC', 'WIO', 'NWC'), feature_group_count=ch)

def masked_softmax(s, mask):
    s = jnp.where(mask, s.astype(F32), -jnp.inf)
    m = jnp.max(s, axis=-1, keepdims=True)
    m = jnp.where(jnp.isfinite(m), m, 0.0)
    e = jnp.exp(s - m)
    return e / jnp.maximum(jnp.sum(e, axis=-1, keepdims=True), 1e-30)

def alibi_slopes(n):
    return 2.0 ** (-8.0 * jnp.arange(1, n + 1, dtype=F32) / n)

def gated_delta_rule(q, k, v, beta, g):
    bsz, nh, s_len, dk = q.shape
    dv = v.shape[-1]
    c = GDN_CHUNK
    n = s_len // c
    ch = lambda t: t.reshape(bsz, nh, n, c, *t.shape[3:])
    q = ch(q * dk ** -0.5)
    k, v, beta = ch(k), ch(v), ch(beta)
    gc = jnp.cumsum(ch(g), axis=-1)
    tri = jnp.tril(jnp.ones((c, c), bool))
    stri = jnp.tril(jnp.ones((c, c), bool), -1)
    decay = jnp.exp(jnp.where(tri, gc[..., :, None] - gc[..., None, :], -jnp.inf))
    kb = k * beta[..., None]
    lower = jnp.where(stri, jnp.einsum('bhnid,bhnjd->bhnij', kb, k) * decay, 0.0)
    rhs = jnp.concatenate([v * beta[..., None], kb * jnp.exp(gc)[..., None]], axis=-1)
    sol = lax.linalg.triangular_solve(lower + jnp.eye(c, dtype=F32), rhs, left_side=True, lower=True,
                                      unit_diagonal=True)
    u_c, w_c = sol[..., :dv], sol[..., dv:]
    attn = jnp.einsum('bhnid,bhnjd->bhnij', q, k) * decay
    qg = q * jnp.exp(gc)[..., None]
    kd = k * jnp.exp(gc[..., -1:] - gc)[..., None]
    dec = jnp.exp(gc[..., -1])

    def step(state, inp):
        u_i, w_i, qg_i, kd_i, a_i, d_i = inp
        v_new = u_i - jnp.einsum('bhcd,bhde->bhce', w_i, state)
        o = jnp.einsum('bhcd,bhde->bhce', qg_i, state) + jnp.einsum('bhij,bhje->bhie', a_i, v_new)
        state = state * d_i[..., None, None] + jnp.einsum('bhcd,bhce->bhde', kd_i, v_new)
        return state, o

    xs = tuple(jnp.moveaxis(t, 2, 0) for t in (u_c, w_c, qg, kd, attn, dec))
    _, o = lax.scan(step, jnp.zeros((bsz, nh, dk, dv), F32), xs)
    return jnp.moveaxis(o, 0, 2).reshape(bsz, nh, s_len, dv)

def gdn_branch(u, offs, conv_w, a_log, dt_bias, onorm):
    bsz, s_len, _ = u.shape
    c = lambda name: _cols(u, offs, name, name).astype(F32)
    qkv = jax.nn.silu(causal_conv(_cols(u, offs, 'gdn_q', 'gdn_v').astype(F32), conv_w.astype(F32)))
    q, k, v = jnp.split(qkv, [GDN_QK, 2 * GDN_QK], axis=-1)
    heads = lambda t, d: t.reshape(bsz, s_len, GDN_HEADS, d).transpose(0, 2, 1, 3)
    q, k, v = l2norm(heads(q, GDN_DK)), l2norm(heads(k, GDN_DK)), heads(v, GDN_DV)
    beta = jax.nn.sigmoid(c('gdn_beta')).transpose(0, 2, 1)
    g = (-jnp.exp(a_log.astype(F32)) * jax.nn.softplus(c('gdn_a') + dt_bias.astype(F32))).transpose(0, 2, 1)
    o = gated_delta_rule(q, k, v, beta, g)
    o = rmsnorm(o, onorm).transpose(0, 2, 1, 3).reshape(bsz, s_len, GDN_V)
    return o * jax.nn.silu(c('gdn_z'))

def gla_chunked(q, k, v, gk):
    bsz, nh, s_len, dk = q.shape
    dv = v.shape[-1]
    c = GLA_CHUNK
    n = s_len // c
    ch = lambda t: t.reshape(bsz, nh, n, c, t.shape[-1])
    q = ch(q * dk ** -0.5)
    k, v = ch(k), ch(v)
    b = jnp.cumsum(ch(gk), axis=3)
    bref = b[:, :, :, c // 2:c // 2 + 1]
    tri = jnp.tril(jnp.ones((c, c), bool))
    a_intra = jnp.where(tri, jnp.einsum('bhnid,bhnjd->bhnij', q * jnp.exp(b - bref), k * jnp.exp(bref - b)), 0.0)
    o_intra = jnp.einsum('bhnij,bhnje->bhnie', a_intra, v)
    qg = q * jnp.exp(b)
    kd = k * jnp.exp(b[:, :, :, -1:] - b)
    dec = jnp.exp(b[:, :, :, -1])

    def step(state, inp):
        qg_i, kd_i, v_i, d_i = inp
        o = jnp.einsum('bhcd,bhde->bhce', qg_i, state)
        state = state * d_i[..., None] + jnp.einsum('bhcd,bhce->bhde', kd_i, v_i)
        return state, o

    xs = tuple(jnp.moveaxis(t, 2, 0) for t in (qg, kd, v, dec))
    _, o_inter = lax.scan(step, jnp.zeros((bsz, nh, dk, dv), F32), xs)
    return (o_intra + jnp.moveaxis(o_inter, 0, 2)).reshape(bsz, nh, s_len, dv)

def gla_branch(u, offs, w_gk, b_gk, onorm):
    bsz, s_len, _ = u.shape
    c = lambda name: _cols(u, offs, name, name).astype(F32)
    gk = jax.nn.log_sigmoid(c('gla_gk') @ w_gk.astype(F32) + b_gk.astype(F32)) / GLA_GATE_NORMALIZER
    heads = lambda t, d: t.reshape(bsz, s_len, GLA_HEADS, d).transpose(0, 2, 1, 3)
    o = gla_chunked(heads(c('gla_q'), GLA_DK), heads(c('gla_k'), GLA_DK), heads(c('gla_v'), GLA_DV), heads(gk, GLA_DK))
    o = rmsnorm(o, onorm).transpose(0, 2, 1, 3).reshape(bsz, s_len, GLA_V)
    return o * jax.nn.silu(c('gla_z'))

def ssd_chunked(x, dt, a_head, bm, cm, d_skip):
    bsz, s_len, ng, hg, p = x.shape
    ns = bm.shape[-1]
    c = SSD_CHUNK
    n = s_len // c
    xc = x.reshape(bsz, n, c, ng, hg, p)
    dtc = dt.reshape(bsz, n, c, ng, hg)
    bc = bm.reshape(bsz, n, c, ng, ns)
    cc = cm.reshape(bsz, n, c, ng, ns)
    acs = jnp.cumsum(dtc * a_head, axis=2)
    xdt = xc * dtc[..., None]
    acs_h = jnp.moveaxis(acs, 2, -1)
    tri = jnp.tril(jnp.ones((c, c), bool))
    lmat = jnp.exp(jnp.where(tri, acs_h[..., :, None] - acs_h[..., None, :], -jnp.inf))
    cb = jnp.einsum('bnigs,bnjgs->bngij', cc, bc)
    y_diag = jnp.einsum('bngij,bnghij,bnjghp->bnighp', cb, lmat, xdt)
    decay_states = jnp.exp(acs[:, :, -1:] - acs)
    states = jnp.einsum('bnjgs,bnjgh,bnjghp->bnghps', bc, decay_states, xdt)
    chunk_decay = jnp.exp(acs[:, :, -1])

    def step(h, inp):
        st, dc = inp
        return h * dc[..., None, None] + st, h

    _, h_prev = lax.scan(step, jnp.zeros((bsz, ng, hg, p, ns), F32),
                         (jnp.moveaxis(states, 1, 0), jnp.moveaxis(chunk_decay, 1, 0)))
    h_prev = jnp.moveaxis(h_prev, 0, 1)
    y_off = jnp.einsum('bnigs,bnghps,bnigh->bnighp', cc, h_prev, jnp.exp(acs))
    y = y_diag + y_off + xc * d_skip[..., None]
    return y.reshape(bsz, s_len, ng, hg, p)

def ssd_branch(u, offs, conv_w, conv_b, a_log, dt_bias, d_skip, onorm):
    bsz, s_len, _ = u.shape
    hg = SSD_HEADS // SSD_GROUPS
    c = lambda name: _cols(u, offs, name, name).astype(F32)
    xbc = jax.nn.silu(causal_conv(_cols(u, offs, 'ssd_x', 'ssd_c').astype(F32), conv_w.astype(F32)) + conv_b.astype(F32))
    xs, bm, cm = jnp.split(xbc, [SSD_INNER, SSD_INNER + SSD_BC], axis=-1)
    xs = xs.reshape(bsz, s_len, SSD_GROUPS, hg, SSD_HEADDIM)
    bm = bm.reshape(bsz, s_len, SSD_GROUPS, SSD_STATE)
    cm = cm.reshape(bsz, s_len, SSD_GROUPS, SSD_STATE)
    dt = jax.nn.softplus(c('ssd_dt') + dt_bias.astype(F32)).reshape(bsz, s_len, SSD_GROUPS, hg)
    a_head = -jnp.exp(a_log.astype(F32)).reshape(SSD_GROUPS, hg)
    y = ssd_chunked(xs, dt, a_head, bm, cm, d_skip.astype(F32).reshape(SSD_GROUPS, hg)).reshape(bsz, s_len, SSD_INNER)
    return rmsnorm(y * jax.nn.silu(c('ssd_z')), onorm)

def compress_tokens(kv, pos_emb, w1, w2):
    bsz, ng, s_len, hd = kv.shape
    r = CMP_BLOCK // CMP_STRIDE
    n_sub = s_len // CMP_STRIDE
    nc = n_sub - r + 1
    sub = kv.reshape(bsz, ng, n_sub, CMP_STRIDE, hd)
    blocks = jnp.concatenate([sub[:, :, i:i + nc] for i in range(r)], axis=3) + pos_emb.astype(F32)
    flat = blocks.reshape(bsz, ng, nc, CMP_BLOCK * hd)
    return jax.nn.silu(flat @ w1.astype(F32)) @ w2.astype(F32)

def nsa_attention(q, kc, vc, ks, vs, kw, vw, gates):
    bsz, ng, hg, s_len, hd = q.shape
    nc = kc.shape[2]
    nsel = s_len // SEL_BLOCK
    topk = min(SEL_TOPK, nsel)
    scale = hd ** -0.5
    slopes = alibi_slopes(ng * hg).reshape(ng, hg, 1, 1)
    cmp_start = jnp.arange(nc) * CMP_STRIDE
    cmp_pos = cmp_start + CMP_BLOCK - 1
    sel_start = jnp.arange(nsel) * SEL_BLOCK
    overlap = ((cmp_start[:, None] <= sel_start[None, :] + SEL_BLOCK - 1)
               & (cmp_pos[:, None] >= sel_start[None, :])).astype(F32)
    ks_blk = ks.reshape(bsz, ng, nsel, SEL_BLOCK, hd)
    vs_blk = vs.reshape(bsz, ng, nsel, SEL_BLOCK, hd)
    kw_pad = jnp.pad(kw, ((0, 0), (0, 0), (WINDOW, 0), (0, 0)))
    vw_pad = jnp.pad(vw, ((0, 0), (0, 0), (WINDOW, 0), (0, 0)))
    bi = jnp.arange(bsz)[:, None, None, None]
    gi = jnp.arange(ng)[None, :, None, None]
    jj = jnp.arange(nsel)
    in_blk = jnp.arange(SEL_BLOCK)

    def block(q0):
        qb = lax.dynamic_slice_in_dim(q, q0, NSA_QBLOCK, axis=3)
        t = q0 + jnp.arange(NSA_QBLOCK)
        s = jnp.einsum('bghqd,bgkd->bghqk', qb, kc) * scale - slopes * (t[:, None] - cmp_pos[None, :]).astype(F32)
        p_c = masked_softmax(s, cmp_pos[None, :] <= t[:, None])
        o_c = jnp.einsum('bghqk,bgkd->bghqd', p_c, vc)
        imp = jnp.einsum('bgqk,kj->bgqj', jnp.sum(p_c, axis=2), overlap)
        cur = t // SEL_BLOCK
        blk_valid = jj[None, :] <= cur[:, None]
        forced = (jj[None, :] == 0) | (jj[None, :] == cur[:, None]) | (jj[None, :] == cur[:, None] - 1)
        imp = jnp.where(blk_valid, jnp.where(forced, FORCED_SCORE, imp), -1.0)
        vals, idx = lax.top_k(imp, topk)
        pos_b = idx[..., None] * SEL_BLOCK + in_blk
        ok = ((vals >= 0.0)[..., None] & (pos_b <= t[:, None, None])).reshape(bsz, ng, NSA_QBLOCK, topk * SEL_BLOCK)
        pos_s = pos_b.reshape(bsz, ng, NSA_QBLOCK, topk * SEL_BLOCK)
        k_g = ks_blk[bi, gi, idx].reshape(bsz, ng, NSA_QBLOCK, topk * SEL_BLOCK, hd)
        v_g = vs_blk[bi, gi, idx].reshape(bsz, ng, NSA_QBLOCK, topk * SEL_BLOCK, hd)
        s = jnp.einsum('bghqd,bgqkd->bghqk', qb, k_g) * scale - slopes * (t[:, None] - pos_s[:, :, None]).astype(F32)
        p_s = masked_softmax(s, ok[:, :, None])
        o_s = jnp.einsum('bghqk,bgqkd->bghqd', p_s, v_g)
        kwb = lax.dynamic_slice_in_dim(kw_pad, q0, WINDOW + NSA_QBLOCK, axis=2)
        vwb = lax.dynamic_slice_in_dim(vw_pad, q0, WINDOW + NSA_QBLOCK, axis=2)
        pos_w = q0 - WINDOW + jnp.arange(WINDOW + NSA_QBLOCK)
        dist = t[:, None] - pos_w[None, :]
        okw = (dist >= 0) & (dist < WINDOW) & (pos_w[None, :] >= 0)
        s = jnp.einsum('bghqd,bgkd->bghqk', qb, kwb) * scale - slopes * dist.astype(F32)
        o_w = jnp.einsum('bghqk,bgkd->bghqd', masked_softmax(s, okw), vwb)
        gb = lax.dynamic_slice_in_dim(gates, q0, NSA_QBLOCK, axis=3)
        return gb[..., 0:1] * o_c + gb[..., 1:2] * o_s + gb[..., 2:3] * o_w

    starts = jnp.arange(s_len // NSA_QBLOCK, dtype=jnp.int32) * NSA_QBLOCK
    out = lax.map(block, starts)
    return jnp.moveaxis(out, 0, 3).reshape(bsz, ng, hg, s_len, hd)

def nsa_branch(u, offs, cmp_pos_k, cmp_pos_v, w_ck1, w_ck2, w_cv1, w_cv2):
    bsz, s_len, _ = u.shape
    ng, hg, hd = NSA_KV_HEADS, NSA_HEADS // NSA_KV_HEADS, NSA_HEADDIM
    c = lambda name: _cols(u, offs, name, name).astype(F32)
    q = c('nsa_q').reshape(bsz, s_len, ng, hg, hd).transpose(0, 2, 3, 1, 4)
    kvh = lambda t: t.reshape(bsz, s_len, ng, hd).transpose(0, 2, 1, 3)
    kc = compress_tokens(kvh(c('nsa_kc')), cmp_pos_k, w_ck1, w_ck2)
    vc = compress_tokens(kvh(c('nsa_vc')), cmp_pos_v, w_cv1, w_cv2)
    gates = jax.nn.sigmoid(c('nsa_gate')).reshape(bsz, s_len, ng, hg, 3).transpose(0, 2, 3, 1, 4)
    o = nsa_attention(q, kc, vc, kvh(c('nsa_ks')), kvh(c('nsa_vs')), kvh(c('nsa_kw')), kvh(c('nsa_vw')), gates)
    o = o.transpose(0, 3, 1, 2, 4).reshape(bsz, s_len, NSA_Q)
    return o * jax.nn.silu(c('nsa_z'))

def _dt_bias(key, n):
    dt = jnp.exp(jax.random.uniform(key, (DEPTH, n), F32, minval=math.log(1e-3), maxval=math.log(1e-1)))
    return dt + jnp.log(-jnp.expm1(-dt))

def first_inputs(seed: int = 0) -> dict:
    key = jax.random.key(seed)
    ks = jax.random.split(key, 32)
    nrm = lambda k, shape, sc: jax.random.normal(k, shape, F32) * sc
    gain = lambda k, n: 1.0 + 0.02 * jax.random.normal(k, (DEPTH, n), F32)
    a_log = lambda k, n: jnp.log(jax.random.uniform(k, (DEPTH, n), F32, minval=1.0, maxval=16.0))
    hd = NSA_HEADDIM
    return {
        'x': jax.random.normal(ks[0], (BATCH, SEQ, D_MODEL), F32),
        'norm_pre': gain(ks[1], D_MODEL),
        'norm_post': gain(ks[2], D_MODEL),
        'w_in': nrm(ks[3], (DEPTH, D_MODEL, D_IN), D_MODEL ** -0.5),
        'conv_a': nrm(ks[4], (DEPTH, CONV_K, 2 * GDN_QK + GDN_V), CONV_K ** -0.5),
        'a_log_a': a_log(ks[5], GDN_HEADS),
        'dt_bias_a': _dt_bias(ks[6], GDN_HEADS),
        'onorm_a': gain(ks[7], GDN_DV),
        'w_gk': nrm(ks[8], (DEPTH, GLA_LOWRANK, GLA_K), GLA_LOWRANK ** -0.5),
        'b_gk': nrm(ks[9], (DEPTH, GLA_K), 0.02),
        'onorm_b': gain(ks[10], GLA_DV),
        'conv_c': nrm(ks[11], (DEPTH, CONV_K, SSD_INNER + 2 * SSD_BC), CONV_K ** -0.5),
        'conv_bias_c': nrm(ks[12], (DEPTH, SSD_INNER + 2 * SSD_BC), 0.02),
        'a_log_c': a_log(ks[13], SSD_HEADS),
        'dt_bias_c': _dt_bias(ks[14], SSD_HEADS),
        'd_skip_c': 1.0 + 0.1 * jax.random.normal(ks[15], (DEPTH, SSD_HEADS), F32),
        'onorm_c': gain(ks[16], SSD_INNER),
        'cmp_pos_k': nrm(ks[17], (DEPTH, CMP_BLOCK, hd), 0.02),
        'cmp_pos_v': nrm(ks[18], (DEPTH, CMP_BLOCK, hd), 0.02),
        'w_ck1': nrm(ks[19], (DEPTH, CMP_BLOCK * hd, hd), (CMP_BLOCK * hd) ** -0.5),
        'w_ck2': nrm(ks[20], (DEPTH, hd, hd), hd ** -0.5),
        'w_cv1': nrm(ks[21], (DEPTH, CMP_BLOCK * hd, hd), (CMP_BLOCK * hd) ** -0.5),
        'w_cv2': nrm(ks[22], (DEPTH, hd, hd), hd ** -0.5),
        'w_br': nrm(ks[23], (DEPTH, N_BRANCH, BR_WIDTH, D_MODEL), BR_WIDTH ** -0.5),
        'w_out': nrm(ks[24], (DEPTH, D_MODEL, D_MODEL), D_MODEL ** -0.5),
    }

def first_block(x, norm_pre, norm_post, w_in, conv_a, a_log_a, dt_bias_a, onorm_a, w_gk, b_gk, onorm_b,
              conv_c, conv_bias_c, a_log_c, dt_bias_c, d_skip_c, onorm_c, cmp_pos_k, cmp_pos_v,
              w_ck1, w_ck2, w_cv1, w_cv2, w_br, w_out):
    offs = _in_offsets()
    bsz, s_len, _ = x.shape
    for l in range(DEPTH):
        h = rmsnorm(x, norm_pre[l])
        u = h @ w_in[l]
        branches = (
            gdn_branch(u, offs, conv_a[l], a_log_a[l], dt_bias_a[l], onorm_a[l]),
            gla_branch(u, offs, w_gk[l], b_gk[l], onorm_b[l]),
            ssd_branch(u, offs, conv_c[l], conv_bias_c[l], a_log_c[l], dt_bias_c[l], d_skip_c[l], onorm_c[l]),
            nsa_branch(u, offs, cmp_pos_k[l], cmp_pos_v[l], w_ck1[l], w_ck2[l], w_cv1[l], w_cv2[l]),
        )
        gates = jax.nn.sigmoid(_cols(u, offs, 'merge_gate', 'merge_gate').astype(F32)).reshape(bsz, s_len, N_BRANCH, D_MODEL)
        merged = jnp.zeros((bsz, s_len, D_MODEL), F32)
        for n, y in enumerate(branches):
            merged = merged + gates[:, :, n] * (y @ w_br[l, n].astype(F32))
        out = merged.astype(x.dtype) @ w_out[l]
        x = x + rmsnorm(out, norm_post[l])
    return x


_first_inputs = first_inputs


def first_inputs(seed=0):
    import zlib

    import numpy as np

    out = dict(_first_inputs(seed))
    spreads = {}
    factors = {'norm_post': 11.246,
     'onorm_a': 41.269,
     'b_gk': 8.0,
     'onorm_b': 36.481,
     'conv_bias_c': 3.915,
     'd_skip_c': 2.99,
     'onorm_c': 24.108,
     'cmp_pos_k': 64.0,
     'cmp_pos_v': 64.0,
     'w_ck1': 13.9,
     'w_ck2': 14.28,
     'w_cv1': 3.065,
     'w_cv2': 2.931}
    for name, (base, spread) in spreads.items():
        noise = np.random.default_rng([zlib.crc32(name.encode()), seed]).standard_normal(out[name].shape)
        drawn = base * np.exp(spread * noise) if base else spread * noise
        out[name] = jnp.asarray(drawn.astype(out[name].dtype))
    for name, factor in factors.items():
        out[name] = (out[name] * factor).astype(out[name].dtype)
    return out


_narrow_inputs = first_inputs


def first_inputs(seed=0):

    out = dict(_narrow_inputs(seed))
    wider = {'norm_post': 3.14, 'onorm_a': 5.27, 'onorm_b': 5.25, 'onorm_c': 5.24}
    for name, times in wider.items():
        mean = out[name].mean()
        out[name] = (mean + times * (out[name] - mean)).astype(out[name].dtype)
    return out


N_MEM = 256
ATTN_HEADS = 8
ATTN_HEAD_DIM = D_MODEL // 16
DILATED_PATTERNS = ((128, 1), (512, 4), (2048, 16))
RET_HEADS = 4
RET_QK_DIM = D_MODEL // 16
RET_V_DIM = D_MODEL // 8
RET_CHUNK = 128
RET_BASE_EXP = 5
ATTN_WIDTH = ATTN_HEADS * ATTN_HEAD_DIM
RET_QK_WIDTH = RET_HEADS * RET_QK_DIM
RET_V_WIDTH = RET_HEADS * RET_V_DIM
MIX_WIDTH = ATTN_WIDTH + RET_V_WIDTH
IN_PROJ_COLS = 3 * ATTN_WIDTH + 2 * RET_QK_WIDTH + 2 * RET_V_WIDTH
MEM_HEADS = 4
MEM_HEAD_DIM = D_MODEL // MEM_HEADS
N_GROUPS = 4
EXPERTS_PER_GROUP = 8
N_EXPERTS = N_GROUPS * EXPERTS_PER_GROUP
EXPERT_TOP_K = 2
EXPERT_FF = D_MODEL // 2
MOE_BLOCK = 128
GN_EPS = 1e-5
NEG_INF = -1e30


def rms_norm(x, w, eps=NORM_EPS):
    xf = x.astype(jnp.float32)
    y = xf * lax.rsqrt(jnp.mean(xf * xf, axis=-1, keepdims=True) + eps)
    return (y * w.astype(jnp.float32)).astype(x.dtype)

def split_heads(t, n_heads, head_dim):
    b, s, _ = t.shape
    return t.reshape(b, s, n_heads, head_dim).transpose(0, 2, 1, 3)

def merge_heads(t):
    b, h, s, d = t.shape
    return t.transpose(0, 2, 1, 3).reshape(b, s, h * d)

def alibi_slopes_2(n_heads):
    exps = jnp.arange(1, n_heads + 1, dtype=jnp.float32)
    return jnp.exp2(-8.0 * exps / n_heads)

def dilated_window_attention(q, k, v, slopes, window, dilation):
    B, H, S, hd = q.shape
    half = window // (2 * dilation)
    L = S // dilation
    nb = -(-L // half)
    Lp = nb * half

    def to_sub(t):
        return t.reshape(B, H, L, dilation, hd).transpose(0, 1, 3, 2, 4)

    qs, ks, vs = to_sub(q), to_sub(k), to_sub(v)
    qb = jnp.pad(qs, ((0, 0), (0, 0), (0, 0), (0, Lp - L), (0, 0))).reshape(B, H, dilation, nb, half, hd)
    kv_pad = ((0, 0), (0, 0), (0, 0), (half, Lp - L + half), (0, 0))
    kp = jnp.pad(ks, kv_pad).reshape(B, H, dilation, nb + 2, half, hd)
    vp = jnp.pad(vs, kv_pad).reshape(B, H, dilation, nb + 2, half, hd)

    def band(t):
        return jnp.concatenate([t[:, :, :, 0:nb], t[:, :, :, 1:nb + 1], t[:, :, :, 2:nb + 2]], axis=4)

    kb, vb = band(kp), band(vp)
    s = jnp.einsum('bhrnqd,bhrnkd->bhrnqk', qb, kb, preferred_element_type=jnp.float32)
    qi = jnp.arange(half)
    kc = jnp.arange(3 * half)
    delta = kc[None, :] - half - qi[:, None]
    key_pos = jnp.arange(nb)[:, None] * half - half + kc[None, :]
    allowed = (jnp.abs(delta) <= half)[None] & ((key_pos >= 0) & (key_pos < L))[:, None, :]
    bias = -slopes[:, None, None] * (dilation * jnp.abs(delta)).astype(jnp.float32)
    s = s + bias[None, :, None, None]
    s = jnp.where(allowed[None, None, None], s, NEG_INF)
    m = jnp.max(s, axis=-1, keepdims=True)
    p = jnp.exp(s - m)
    denom = jnp.sum(p, axis=-1, keepdims=True)
    o = jnp.einsum('bhrnqk,bhrnkd->bhrnqd', p.astype(v.dtype), vb, preferred_element_type=jnp.float32) / denom
    lse = (m + jnp.log(denom))[..., 0]

    def from_sub(t):
        t = t.reshape((B, H, dilation, Lp) + t.shape[5:])[:, :, :, :L]
        t = jnp.moveaxis(t, 2, 3)
        return t.reshape((B, H, S) + t.shape[4:])

    return from_sub(o), from_sub(lse)

def retention_chunkwise(q, k, v, log_gamma, inclusive):
    B, H, S, dk = q.shape
    dv = v.shape[-1]
    C = RET_CHUNK
    nC = S // C
    qc = q.reshape(B, H, nC, C, dk)
    kc = k.reshape(B, H, nC, C, dk)
    vc = v.reshape(B, H, nC, C, dv)
    i = jnp.arange(C)
    lg = log_gamma[:, None]
    diff = i[:, None] - i[None, :]
    mask = diff >= 0 if inclusive else diff > 0
    decay_mat = jnp.where(mask[None], jnp.exp(lg[:, :, None] * jnp.maximum(diff, 0)[None]), 0.0)
    scores = jnp.einsum('bhnid,bhnjd->bhnij', qc, kc) * decay_mat[None, :, None]
    y_intra = jnp.einsum('bhnij,bhnje->bhnie', scores, vc)
    k_dec = jnp.exp(lg * (C - 1 - i)[None])
    chunk_kv = jnp.einsum('bhnjd,hj,bhnje->bhnde', kc, k_dec, vc)
    chunk_decay = jnp.exp(log_gamma * C)[None, :, None, None]

    def step(state, kv_n):
        return state * chunk_decay + kv_n, state

    _, prev = lax.scan(step, jnp.zeros((B, H, dk, dv), q.dtype), jnp.moveaxis(chunk_kv, 2, 0))
    prev = jnp.moveaxis(prev, 0, 2)
    q_dec = jnp.exp(lg * (i + 1)[None])
    y_cross = jnp.einsum('bhnid,hi,bhnde->bhnie', qc, q_dec, prev)
    return (y_intra + y_cross).reshape(B, H, S, dv)

def head_group_norm(y, w, eps=GN_EPS):
    mu = jnp.mean(y, axis=-1, keepdims=True)
    var = jnp.mean(jnp.square(y - mu), axis=-1, keepdims=True)
    return merge_heads((y - mu) * lax.rsqrt(var + eps)) * w.astype(jnp.float32)

def parallel_mixer(h, w_in, q_norm_w, k_norm_w, decay_f, decay_b, gn_w, w_out):
    f32 = jnp.float32
    proj = h @ w_in
    a3 = 3 * ATTN_WIDTH
    cuts = [ATTN_WIDTH, 2 * ATTN_WIDTH, a3, a3 + RET_QK_WIDTH, a3 + 2 * RET_QK_WIDTH,
            a3 + 2 * RET_QK_WIDTH + RET_V_WIDTH]
    aq, ak, av, rq, rk, rv, rg = jnp.split(proj, cuts, axis=-1)
    q = rms_norm(split_heads(aq, ATTN_HEADS, ATTN_HEAD_DIM), q_norm_w) * (ATTN_HEAD_DIM ** -0.5)
    k = rms_norm(split_heads(ak, ATTN_HEADS, ATTN_HEAD_DIM), k_norm_w)
    v = split_heads(av, ATTN_HEADS, ATTN_HEAD_DIM)
    slopes = alibi_slopes_2(ATTN_HEADS)
    outs, lses = [], []
    for window, dilation in DILATED_PATTERNS:
        o, lse = dilated_window_attention(q, k, v, slopes, window, dilation)
        outs.append(o)
        lses.append(lse)
    mix_w = jax.nn.softmax(jnp.stack(lses), axis=0)
    attn = jnp.einsum('pbhs,pbhsd->bhsd', mix_w, jnp.stack(outs))
    attn = merge_heads(attn).astype(h.dtype)
    qr = split_heads(rq, RET_HEADS, RET_QK_DIM).astype(f32)
    kr = split_heads(rk, RET_HEADS, RET_QK_DIM).astype(f32) * (RET_QK_DIM ** -0.5)
    vr = split_heads(rv, RET_HEADS, RET_V_DIM).astype(f32)
    lg_f = jax.nn.log_sigmoid(decay_f.astype(f32))
    lg_b = jax.nn.log_sigmoid(decay_b.astype(f32))
    y_f = retention_chunkwise(qr, kr, vr, lg_f, inclusive=True)
    flip = lambda t: jnp.flip(t, axis=2)
    y_b = flip(retention_chunkwise(flip(qr), flip(kr), flip(vr), lg_b, inclusive=False))
    ret = head_group_norm(y_f + y_b, gn_w)
    ret = (jax.nn.silu(rg.astype(f32)) * ret).astype(h.dtype)
    return jnp.concatenate([attn, ret], axis=-1) @ w_out

def memory_cross_attention(h, mem_h, w_mq, w_mkv, q_norm_w, k_norm_w, w_mo):
    q = rms_norm(split_heads(h @ w_mq, MEM_HEADS, MEM_HEAD_DIM), q_norm_w) * (MEM_HEAD_DIM ** -0.5)
    mk, mv = jnp.split(mem_h @ w_mkv, 2, axis=-1)
    k = rms_norm(split_heads(mk, MEM_HEADS, MEM_HEAD_DIM), k_norm_w)
    v = split_heads(mv, MEM_HEADS, MEM_HEAD_DIM)
    s = jnp.einsum('bhsd,bhmd->bhsm', q, k, preferred_element_type=jnp.float32)
    p = jax.nn.softmax(s, axis=-1)
    o = jnp.einsum('bhsm,bhmd->bhsd', p.astype(v.dtype), v)
    return merge_heads(o) @ w_mo

def hierarchical_moe(h, w_group, w_router, w1, w3, w2):
    B, S, D = h.shape
    N = B * S
    t = h.reshape(N, D)
    g_logits = jnp.einsum('nd,dg->ng', t, w_group, preferred_element_type=jnp.float32)
    g_prob = jax.nn.softmax(g_logits, axis=-1)
    grp = jnp.argmax(g_logits, axis=-1)
    g_gate = jnp.take_along_axis(g_prob, grp[:, None], axis=-1)
    e_logits = jnp.einsum('nd,gde->nge', t, w_router, preferred_element_type=jnp.float32)
    e_logits = jnp.take_along_axis(e_logits, grp[:, None, None], axis=1)[:, 0]
    top_vals, top_idx = lax.top_k(e_logits, EXPERT_TOP_K)
    gates = g_gate * jax.nn.softmax(top_vals, axis=-1)
    expert_id = grp[:, None] * EXPERTS_PER_GROUP + top_idx
    A = N * EXPERT_TOP_K
    e_flat = expert_id.reshape(A)
    tok_flat = jnp.repeat(jnp.arange(N, dtype=jnp.int32), EXPERT_TOP_K)
    gate_flat = gates.reshape(A)
    order = jnp.argsort(e_flat)
    e_sorted = e_flat[order]
    counts = jnp.bincount(e_flat, length=N_EXPERTS)
    starts = jnp.cumsum(counts) - counts
    pcounts = (counts + MOE_BLOCK - 1) // MOE_BLOCK * MOE_BLOCK
    pends = jnp.cumsum(pcounts)
    pstarts = pends - pcounts
    dest = pstarts[e_sorted] + jnp.arange(A) - starts[e_sorted]
    n_blocks = -(-(A + N_EXPERTS * MOE_BLOCK) // MOE_BLOCK)
    n_slots = n_blocks * MOE_BLOCK
    slot_tok = jnp.full((n_slots,), N, dtype=jnp.int32).at[dest].set(tok_flat[order])
    slot_gate = jnp.zeros((n_slots,), jnp.float32).at[dest].set(gate_flat[order])
    block_expert = jnp.clip(jnp.searchsorted(pends, jnp.arange(n_blocks) * MOE_BLOCK, side='right'),
                            0, N_EXPERTS - 1)
    t_pad = jnp.concatenate([t, jnp.zeros((1, D), t.dtype)], axis=0)

    def expert_block(args):
        toks, e = args
        xb = t_pad[toks]
        return (jax.nn.silu(xb @ w1[e]) * (xb @ w3[e])) @ w2[e]

    y_slots = lax.map(expert_block, (slot_tok.reshape(n_blocks, MOE_BLOCK), block_expert))
    y_slots = y_slots.reshape(n_slots, D) * slot_gate[:, None]
    y = jax.ops.segment_sum(y_slots, slot_tok, num_segments=N + 1)[:N]
    return y.astype(h.dtype).reshape(B, S, D)

def second_inputs(seed: int = 0) -> dict:
    key = jax.random.key(seed)
    ks = jax.random.split(key, 24)
    f32 = jnp.float32

    def normal(k, shape, scale):
        return jax.random.normal(k, shape, f32) * scale

    def gain(k, shape):
        return 1.0 + 0.05 * jax.random.normal(k, shape, f32)

    base_logit = jnp.log(jnp.exp2(RET_BASE_EXP + jnp.arange(RET_HEADS, dtype=f32)) - 1.0)
    return {
        'x': normal(ks[0], (BATCH, SEQ, D_MODEL), 1.0),
        'mem': normal(ks[1], (BATCH, N_MEM, D_MODEL), 1.0),
        'norm_mix_w': gain(ks[2], (DEPTH, D_MODEL)),
        'w_in': normal(ks[3], (DEPTH, D_MODEL, IN_PROJ_COLS), D_MODEL ** -0.5),
        'attn_q_norm_w': gain(ks[4], (DEPTH, ATTN_HEAD_DIM)),
        'attn_k_norm_w': gain(ks[5], (DEPTH, ATTN_HEAD_DIM)),
        'ret_decay_f': base_logit + 0.1 * jax.random.normal(ks[6], (DEPTH, RET_HEADS), f32),
        'ret_decay_b': base_logit + 0.1 * jax.random.normal(ks[7], (DEPTH, RET_HEADS), f32),
        'ret_gn_w': gain(ks[8], (DEPTH, RET_V_WIDTH)),
        'w_out': normal(ks[9], (DEPTH, MIX_WIDTH, D_MODEL), MIX_WIDTH ** -0.5),
        'norm_mem_w': gain(ks[10], (DEPTH, D_MODEL)),
        'norm_memkv_w': gain(ks[11], (DEPTH, D_MODEL)),
        'w_mq': normal(ks[12], (DEPTH, D_MODEL, D_MODEL), D_MODEL ** -0.5),
        'w_mkv': normal(ks[13], (DEPTH, D_MODEL, 2 * D_MODEL), D_MODEL ** -0.5),
        'mem_q_norm_w': gain(ks[14], (DEPTH, MEM_HEAD_DIM)),
        'mem_k_norm_w': gain(ks[15], (DEPTH, MEM_HEAD_DIM)),
        'w_mo': normal(ks[16], (DEPTH, D_MODEL, D_MODEL), D_MODEL ** -0.5),
        'norm_moe_w': gain(ks[17], (DEPTH, D_MODEL)),
        'w_group': normal(ks[18], (DEPTH, D_MODEL, N_GROUPS), D_MODEL ** -0.5),
        'w_router': normal(ks[19], (DEPTH, N_GROUPS, D_MODEL, EXPERTS_PER_GROUP), D_MODEL ** -0.5),
        'w_exp_gate': normal(ks[20], (DEPTH, N_EXPERTS, D_MODEL, EXPERT_FF), D_MODEL ** -0.5),
        'w_exp_up': normal(ks[21], (DEPTH, N_EXPERTS, D_MODEL, EXPERT_FF), D_MODEL ** -0.5),
        'w_exp_down': normal(ks[22], (DEPTH, N_EXPERTS, EXPERT_FF, D_MODEL), EXPERT_FF ** -0.5),
    }

def second_block(x, mem, norm_mix_w, w_in, attn_q_norm_w, attn_k_norm_w, ret_decay_f, ret_decay_b,
              ret_gn_w, w_out, norm_mem_w, norm_memkv_w, w_mq, w_mkv, mem_q_norm_w, mem_k_norm_w,
              w_mo, norm_moe_w, w_group, w_router, w_exp_gate, w_exp_up, w_exp_down):
    for l in range(DEPTH):
        x = x + parallel_mixer(rms_norm(x, norm_mix_w[l]), w_in[l], attn_q_norm_w[l], attn_k_norm_w[l],
                               ret_decay_f[l], ret_decay_b[l], ret_gn_w[l], w_out[l])
        x = x + memory_cross_attention(rms_norm(x, norm_mem_w[l]), rms_norm(mem, norm_memkv_w[l]),
                                       w_mq[l], w_mkv[l], mem_q_norm_w[l], mem_k_norm_w[l], w_mo[l])
        x = x + hierarchical_moe(rms_norm(x, norm_moe_w[l]), w_group[l], w_router[l],
                                 w_exp_gate[l], w_exp_up[l], w_exp_down[l])
    return x


def setup_inputs(seed=0):
    out = dict(first_inputs(seed))
    for name, value in second_inputs(seed + 1).items():
        if name != "x":
            out[name + "_2"] = value
    return out


def reference(
    x, norm_pre, norm_post, w_in, conv_a, a_log_a, dt_bias_a, onorm_a, w_gk, b_gk, onorm_b,
    conv_c, conv_bias_c, a_log_c, dt_bias_c, d_skip_c, onorm_c, cmp_pos_k, cmp_pos_v, w_ck1,
    w_ck2, w_cv1, w_cv2, w_br, w_out, mem_2, norm_mix_w_2, w_in_2, attn_q_norm_w_2,
    attn_k_norm_w_2, ret_decay_f_2, ret_decay_b_2, ret_gn_w_2, w_out_2, norm_mem_w_2,
    norm_memkv_w_2, w_mq_2, w_mkv_2, mem_q_norm_w_2, mem_k_norm_w_2, w_mo_2, norm_moe_w_2,
    w_group_2, w_router_2, w_exp_gate_2, w_exp_up_2, w_exp_down_2,
):
    x = first_block(
        x, norm_pre, norm_post, w_in, conv_a, a_log_a, dt_bias_a, onorm_a, w_gk, b_gk, onorm_b,
        conv_c, conv_bias_c, a_log_c, dt_bias_c, d_skip_c, onorm_c, cmp_pos_k, cmp_pos_v, w_ck1,
        w_ck2, w_cv1, w_cv2, w_br, w_out,
    )
    return second_block(
        x, mem_2, norm_mix_w_2, w_in_2, attn_q_norm_w_2, attn_k_norm_w_2, ret_decay_f_2,
        ret_decay_b_2, ret_gn_w_2, w_out_2, norm_mem_w_2, norm_memkv_w_2, w_mq_2, w_mkv_2,
        mem_q_norm_w_2, mem_k_norm_w_2, w_mo_2, norm_moe_w_2, w_group_2, w_router_2,
        w_exp_gate_2, w_exp_up_2, w_exp_down_2,
    )


_drawn_inputs = setup_inputs


def setup_inputs(seed=0):
    import zlib

    import numpy as np

    out = dict(_drawn_inputs(seed))
    spreads = {}
    factors = {'mem_2': 6.192,
     'norm_mix_w_2': 8.0,
     'attn_q_norm_w_2': 8.0,
     'attn_k_norm_w_2': 8.0,
     'ret_decay_f_2': 47.648,
     'ret_decay_b_2': 47.968,
     'ret_gn_w_2': 8.0,
     'norm_mem_w_2': 8.0,
     'norm_memkv_w_2': 8.0,
     'w_mq_2': 7.453,
     'w_mkv_2': 5.737,
     'mem_q_norm_w_2': 8.0,
     'mem_k_norm_w_2': 8.0,
     'w_mo_2': 5.932,
     'norm_moe_w_2': 8.0,
     'w_group_2': 3.023,
     'w_router_2': 2.929,
     'w_exp_gate_2': 2.768}
    for name, (base, spread) in spreads.items():
        noise = np.random.default_rng([zlib.crc32(name.encode()), seed]).standard_normal(out[name].shape)
        drawn = base * np.exp(spread * noise) if base else spread * noise
        out[name] = jnp.asarray(drawn.astype(out[name].dtype))
    for name, factor in factors.items():
        out[name] = (out[name] * factor).astype(out[name].dtype)
    return out
```

```python
import math
from contextlib import ExitStack

import numpy as np

import concourse.bass as bass
from concourse import mybir

F32 = mybir.dt.float32
I32 = mybir.dt.int32
U32 = mybir.dt.uint32
ALU = mybir.AluOpType
ACT = mybir.ActivationFunctionType
AX = mybir.AxisListType

P = 128
D = 1024
KD = D // P
SEQ = 512
NT = SEQ // P
EPS = 1e-6
GN_EPS = 1e-5
MASKED = -1e30
ALIBI_HEADS = 8

W_IN_COLS = (
    ("gdn_q", 512), ("gdn_k", 512), ("gdn_v", 512), ("gdn_beta", 4), ("gdn_a", 4), ("gdn_z", 512),
    ("gla_q", 256), ("gla_k", 256), ("gla_v", 512), ("gla_gk", 16), ("gla_z", 512),
    ("ssd_x", 512), ("ssd_b", 256), ("ssd_c", 256), ("ssd_dt", 8), ("ssd_z", 512),
    ("nsa_q", 512), ("nsa_kc", 128), ("nsa_vc", 128), ("nsa_ks", 128), ("nsa_vs", 128),
    ("nsa_kw", 128), ("nsa_vw", 128), ("nsa_gate", 24), ("nsa_z", 512), ("merge_gate", 4096),
)
AT = {}
_at = 0
for _name, _width in W_IN_COLS:
    AT[_name] = _at
    _at += _width
D_IN = _at

N_MEM = 256
N_EXPERTS = 32
N_GROUPS = 4
FF = 512
SLOTS = 64
N_OVER = -(-((2 * SEQ - N_EXPERTS) // SLOTS) // 2) * 2
N_BLOCKS = N_EXPERTS + N_OVER
N_CMP = 31

SLOPES = [2.0 ** (-8.0 * (h + 1) / ALIBI_HEADS) for h in range(ALIBI_HEADS)]
BAND = SEQ + (NT - 1) * P


def shape_constants():
    p = np.arange(P)[:, None].astype(np.float64)
    c = np.arange(P)[None, :].astype(np.float64)
    band = np.arange(BAND)[None, :]
    t = {}
    t["ident"] = p == c
    t["ones"] = np.ones((P, P))
    t["upto"] = p <= c
    t["below"] = p < c
    t["half_ones"] = (p // 64) == (c // 64)
    t["strict_bias"] = np.where(c < p, 0.0, MASKED)
    t["causal_biasT"] = np.where(p <= c, 0.0, MASKED)
    for lvl in range(7):
        b = 2**lvl
        t[f"level{lvl}"] = ((p // (2 * b)) == (c // (2 * b))) & ((p // b) % 2 == 1) & ((c // b) % 2 == 0)
    same = (p // 64) == (c // 64)
    within = same & (p <= c)
    mid = same & ((p % 64) <= 32)
    t["gla_from_mid"] = within.astype(float) - mid
    t["gla_within"] = within
    t["gla_to_half_end"] = same.astype(float) - within
    t["gla_to_end"] = 1.0 - (p <= c)
    t["gla_near"] = within
    t["gla_far"] = (p < 64) & (c >= 64)
    dist = p + (NT - 1) * P - band
    t["causal_dist"] = np.where(dist >= 0, -dist, MASKED)
    a = np.abs(dist)
    count = (a <= 64) * 1.0 + ((a % 4 == 0) & (a <= 256)) + (a % 16 == 0)
    t["mix_dist"] = -a
    t["mix_log"] = np.where(count > 0, np.log(np.maximum(count, 1)), MASKED)
    t["ahead"] = np.maximum(-dist, 0)
    t["ahead"] = np.maximum((band - (NT - 1) * P) - p, 0)
    t["behind"] = np.maximum(p - (band - (NT - 1) * P), 0)
    cmp_pos = np.arange(32)[None, None, :] * 16 + 31
    tok = np.arange(P)[:, None, None] + P * np.arange(NT)[None, :, None]
    cmp = np.where((cmp_pos <= tok) & (np.arange(32) < N_CMP), -(tok - cmp_pos), MASKED)
    t["cmp_dist"] = cmp.reshape(P, NT * 32)
    t["iota"] = c + 0 * p
    names = {}
    at = 0
    cols = []
    for k, v in t.items():
        v = np.broadcast_to(np.asarray(v, np.float64), (P, v.shape[1])).astype(np.float32)
        names[k] = (at, v.shape[1])
        at += v.shape[1]
        cols.append(v)
    return names, np.ascontiguousarray(np.concatenate(cols, axis=1))


class Signal:

    def __init__(self, sem):
        self.sem, self.n, self.base = sem, 0, 0

    def up(self, by=1):
        self.n += by
        return self.sem, by

    def at(self, k):
        return self.sem, self.base + k

    def now(self):
        return self.sem, self.n


class Core:

    def __init__(self, nc, ins, out, dbg=None):
        self.nc, self.ins, self.out, self.dbg = nc, ins, out, dbg or {}
        self.stack = ExitStack()
        self.counters = []
        self.names = {}
        n = self.new_counter
        self.dma = n("loads_landed")
        self.stored = n("stores_landed")
        self.vchain = n("vector_step")
        self.achain = n("scalar_step")
        self.gchain = n("gpsimd_step")
        self.ready = n("product_ready")
        self.vfree = n("bank_read_by_vector")
        self.afree = n("bank_read_by_scalar")
        self.uid = 0

    def new_counter(self, name):
        s = Signal(self.stack.enter_context(self.nc.semaphore(name)))
        self.counters.append(s)
        self.names[name] = s
        return s

    def sig(self, name):
        return self.names[name] if name in self.names else self.new_counter(name)

    def sb(self, stack, name, shape, dt=F32):
        self.uid += 1
        return stack.enter_context(self.nc.sbuf_tensor(f"{name}_{self.uid}", shape, dt))

    def ps(self, stack, name, shape=(P, SEQ), dt=F32):
        self.uid += 1
        return stack.enter_context(self.nc.psum_tensor(f"{name}_{self.uid}", list(shape), dt))

    def block(self):
        for s in self.counters:
            s.base = s.n
        return self.nc.Block()

    def const(self, name):
        at, n = self.const_at[name]
        return self.ins["shape_constants"][:, at:at + n]


def linker(eng, sig):
    def link(ins):
        ins.then_inc(*sig.up())
        eng.wait_ge(*sig.now())
        return ins
    return link


class Stream:
    def __init__(self, core, stack, slots, items):
        self.core, self.slots, self.items = core, slots, items
        self.ring = core.sb(stack, "weight_ring", [P, slots, 4096])
        self.at = {key: n for n, (key, _, _, _) in enumerate(items)}
        self.landed = [core.new_counter(f"weights_in_slot{s}") for s in range(slots)]
        self.issued = 0

    def view(self, key):
        n = self.at[key]
        _, _, a, b = self.items[n]
        return self.ring[:, n % self.slots, 0:a * b].rearrange("p (a b) -> p a b", a=a)

    def load(self, sp):
        n = self.issued
        key, src, _, _ = self.items[n]
        sp.dma_start(self.view(key), src).then_inc(*self.landed[n % self.slots].up(16))
        self.issued += 1

    def arrived(self, eng, key):
        n = self.at[key]
        eng.wait_ge(self.landed[n % self.slots].sem, 16 * (n // self.slots + 1))

    def refill(self, sp, key, wait=None):
        assert self.at[key] + self.slots == self.issued or self.issued >= len(self.items), key
        if self.issued < len(self.items):
            if wait:
                sp.wait_ge(*wait)
            self.load(sp)


def product_block(core, jobs, stream=None, loads=(), banks=6):
    nc = core.nc
    st = ExitStack()
    bank = [core.ps(st, f"bank{b}") for b in range(banks)]
    free = {"v": core.vfree, "a": core.afree}
    nth = []
    seen = {"v": 0, "a": 0}
    for job in jobs:
        seen[job[2]] += 1
        nth.append(seen[job[2]])
    last_of = {}
    for j, job in enumerate(jobs):
        if job[0] is not None:
            last_of[job[0]] = j
    with core.block() as block:
        @block.sync
        def _(sp):
            for dst, src in loads:
                sp.dma_start(dst, src).then_inc(*core.dma.up(16))
            for key in sorted(last_of, key=lambda k: last_of[k]):
                stream.refill(sp, key, core.ready.at(last_of[key] + 1))

        @block.tensor
        def _(pe):
            if loads:
                pe.wait_ge(*core.dma.at(16 * len(loads)))
            waited = set()
            for j, (item, fill, _, _) in enumerate(jobs):
                if item is not None and item not in waited:
                    waited.add(item)
                    stream.arrived(pe, item)
                if j >= banks:
                    pe.wait_ge(*free[jobs[j - banks][2]].at(nth[j - banks]))
                fill(bank[j % banks]).then_inc(*core.ready.up())

        def reader(eng, which, chain):
            link = linker(eng, chain)
            if loads:
                eng.wait_ge(*core.dma.at(16 * len(loads)))
            for j, (_, _, e, read) in enumerate(jobs):
                if e == which:
                    eng.wait_ge(*core.ready.at(j + 1))
                    read(link, bank[j % banks]).then_inc(*free[which].up())

        @block.vector
        def _(dve):
            reader(dve, "v", core.vchain)

        @block.scalar
        def _(act):
            reader(act, "a", core.achain)
    st.close()


def sum_of(nc, out, pairs):
    for n, (lhsT, rhs) in enumerate(pairs):
        last = nc.tensor.matmul(out, lhsT, rhs, start=(n == 0), stop=(n == len(pairs) - 1))
    return last


def copy_on(nc, which, out, in_):
    return nc.vector.tensor_copy(out, in_) if which == "v" else nc.scalar.copy(out, in_)


def transpose_job(core, srcs, dst, which, gain=None, item=None):
    nc = core.nc
    n = srcs[0].shape[-1]
    m = srcs[0].shape[0]

    def fill(bank):
        for i, s in enumerate(srcs):
            last = nc.tensor.transpose(bank[0:n, i * m:(i + 1) * m], s, core.ident[0:m, 0:m])
        return last

    def read(link, bank):
        src = bank[0:n, 0:m * len(srcs)]
        if len(dst.shape) == 3:
            src = src.rearrange("p (a b) -> p a b", b=dst.shape[-1])
        if gain is None:
            return copy_on(nc, which, dst, src)
        if which == "v":
            return nc.vector.tensor_scalar(dst, src, gain, None, ALU.mult)
        return nc.scalar.mul(dst, src, gain)
    return (item, fill, which, read)


def channel_major(core, stream, src, item, cols, m, ntok=SEQ, kd=KD):
    w = stream.view(item)

    def fill(bank):
        return sum_of(core.nc, bank[0:m, 0:ntok],
                      [(w[:, k, cols:cols + m], src[:, k, 0:ntok]) for k in range(kd)])
    return fill


def token_major(core, stream, src, item, tile, cols, n, kd=KD):
    w = stream.view(item)

    def fill(bank):
        return sum_of(core.nc, bank[:, 0:n],
                      [(src[:, k, tile * P:(tile + 1) * P], w[:, k, cols:cols + n]) for k in range(kd)])
    return fill


def rms_rows(core, src, tiles, dst):
    nc = core.nc
    st = ExitStack()
    sq = core.sb(st, "squares", [P, D])
    ss = core.sb(st, "sum_squares", [P, tiles])
    rs = core.sb(st, "rms", [P, tiles])
    summed = core.sig("squares_summed")
    rooted = core.sig("rms_rooted")
    with core.block() as block:
        @block.scalar
        def _(act):
            link = linker(act, core.achain)
            for t in range(tiles):
                link(nc.scalar.activation(sq[:], src[:, t, :], ACT.Square, accum_out=ss[:, t:t + 1]))
            nc.scalar.activation(rs[:], ss[:], ACT.Sqrt, scale=1.0 / D, bias=core.eps[:, 0:1]).then_inc(*rooted.up())

        @block.vector
        def _(dve):
            link = linker(dve, core.vchain)
            dve.wait_ge(*rooted.at(1))
            link(nc.vector.reciprocal(rs[:], rs[:]))
            for t in range(tiles):
                nc.vector.tensor_scalar(dst[:, t, :], src[:, t, :], rs[:, t:t + 1], None, ALU.mult)
    st.close()


def norm_to_channels(core, src, tiles, gain, hT, keep=None):
    st = ExitStack()
    xn = keep if keep is not None else core.sb(st, "normed", [P, tiles, D])
    rms_rows(core, src, tiles, xn)
    jobs = [transpose_job(core, [xn[:, t, k * P:(k + 1) * P] for t in range(tiles)],
                          hT[:, k, 0:tiles * P], "va"[k % 2], gain=gain[:, k:k + 1])
            for k in range(KD)]
    product_block(core, jobs)
    st.close()


def norm_channels(core, chunks, group, eps, gains, per_head, ntok=SEQ, mean=True):
    nc = core.nc
    st = ExitStack()
    flat = [(g, c) for g, cs in enumerate(chunks) for c in cs]
    most = max(len(cs) for cs in chunks)
    sq = core.sb(st, "squares", [P, 2, most, ntok])
    root = core.sb(st, "roots", [P, 2, ntok])
    inv = core.sb(st, "inverses", [P, 2, ntok])
    bank = [core.ps(st, f"sums{b}") for b in range(2)]
    squared, summed, rooted, scaled = (core.sig(x) for x in ("ch_squared", "ch_summed", "ch_rooted", "ch_scaled"))
    n = len(chunks)
    done = [sum(len(cs) for cs in chunks[:g + 1]) for g in range(n)]
    with core.block() as block:
        @block.scalar
        def _(act):
            def square(g):
                if g >= 2:
                    act.wait_ge(*summed.at(g - 1))
                for i, c in enumerate(chunks[g]):
                    nc.scalar.activation(sq[:, g % 2, i, :], c, ACT.Square).then_inc(*squared.up())

            def take_root(g):
                act.wait_ge(*summed.at(g + 1))
                if g >= 2:
                    act.wait_ge(*scaled.at(done[g - 2]))
                nc.scalar.activation(root[:, g % 2, :], bank[g % 2][:, 0:ntok], ACT.Sqrt,
                                     scale=1.0 / per_head if mean else 1.0, bias=eps).then_inc(*rooted.up())
            square(0)
            for g in range(n):
                if g + 1 < n:
                    square(g + 1)
                take_root(g)

        @block.tensor
        def _(pe):
            for g in range(n):
                pe.wait_ge(*squared.at(done[g]))
                if g >= 2:
                    pe.wait_ge(*rooted.at(g - 1))
                sum_of(nc, bank[g % 2][:, 0:ntok], [(group, sq[:, g % 2, i, :]) for i in range(len(chunks[g]))]
                       ).then_inc(*summed.up())

        @block.vector
        def _(dve):
            link = linker(dve, core.vchain)
            k = 0
            for g in range(n):
                dve.wait_ge(*rooted.at(g + 1))
                link(nc.vector.reciprocal(inv[:, g % 2, :], root[:, g % 2, :]))
                for c in chunks[g]:
                    nc.vector.scalar_tensor_tensor(out=c, in0=c, scalar=gains[k], in1=inv[:, g % 2, :],
                                                   op0=ALU.mult, op1=ALU.mult).then_inc(*scaled.up())
                    k += 1
    st.close()


def conv_block(core, stream, src, chunks, taps, bias):
    nc = core.nc
    st = ExitStack()
    bank = [core.ps(st, f"raw{b}") for b in range(4)]
    acc = core.sb(st, "convolved", [P, 3, SEQ])
    convolved, activated = core.sig("chunk_convolved"), core.sig("chunk_activated")
    n = len(chunks)
    last_of = {c[0]: j for j, c in enumerate(chunks)}
    with core.block() as block:
        @block.sync
        def _(sp):
            for key in sorted(last_of, key=lambda k: last_of[k]):
                stream.refill(sp, key, core.ready.at(last_of[key] + 1))

        @block.tensor
        def _(pe):
            for j, (item, col, _, _) in enumerate(chunks):
                stream.arrived(pe, item)
                if j >= 4:
                    pe.wait_ge(*convolved.at(j - 3))
                channel_major(core, stream, src, item, col, P)(bank[j % 4]).then_inc(*core.ready.up())

        @block.vector
        def _(dve):
            link = linker(dve, core.vchain)
            for j, (_, _, _, w) in enumerate(chunks):
                dve.wait_ge(*core.ready.at(j + 1))
                if j >= 3:
                    dve.wait_ge(*activated.at(j - 2))
                a, raw = acc[:, j % 3, :], bank[j % 4]
                link(nc.vector.tensor_scalar(a, raw[:], taps[:, w, 3:4], None, ALU.mult))
                for back in (1, 2, 3):
                    ins = nc.vector.scalar_tensor_tensor(
                        out=acc[:, j % 3, back:], in0=raw[:, 0:SEQ - back], scalar=taps[:, w, 3 - back:4 - back],
                        in1=acc[:, j % 3, back:], op0=ALU.mult, op1=ALU.add)
                    if back < 3:
                        link(ins)
                ins.then_inc(*convolved.up())

        @block.scalar
        def _(act):
            for j, (_, _, dst, w) in enumerate(chunks):
                act.wait_ge(*convolved.at(j + 1))
                nc.scalar.activation(dst, acc[:, j % 3, :], ACT.Silu,
                                     bias=bias[:, w:w + 1] if bias is not None else 0.0).then_inc(*activated.up())
    st.close()


def merge_branch(core, stream, hT, yT, n, merged):
    nc = core.nc
    st = ExitStack()
    gate_bank = [core.ps(st, f"gate{b}") for b in range(3)]
    proj_bank = [core.ps(st, f"proj{b}") for b in range(3)]
    gate = core.sb(st, "gate", [P, 3, SEQ])
    part = core.sb(st, "part", [P, 3, SEQ])
    gated, multiplied, added = core.sig("gate_ready"), core.sig("branch_gated"), core.sig("branch_added")
    jobs = [(half, t) for half in range(2) for t in range(NT)]
    w_br = stream.view(f"w_br{n}")
    with core.block() as block:
        @block.sync
        def _(sp):
            stream.refill(sp, f"merge{n}_0", core.ready.at(NT))
            stream.refill(sp, f"merge{n}_1", core.ready.at(2 * NT))
            stream.refill(sp, f"w_br{n}", None)

        @block.tensor
        def _(pe):
            stream.arrived(pe, f"w_br{n}")
            for j, (half, t) in enumerate(jobs):
                stream.arrived(pe, f"merge{n}_{half}")
                if j >= 3:
                    pe.wait_ge(*gated.at(j - 2))
                    pe.wait_ge(*multiplied.at(j - 2))
                token_major(core, stream, hT, f"merge{n}_{half}", t, 0, SEQ)(gate_bank[j % 3])
                sum_of(nc, proj_bank[j % 3][:], [(yT[:, c, t * P:(t + 1) * P], w_br[:, c, half * SEQ:(half + 1) * SEQ])
                                                 for c in range(4)]).then_inc(*core.ready.up())

        @block.scalar
        def _(act):
            for j in range(len(jobs)):
                act.wait_ge(*core.ready.at(j + 1))
                if j >= 3:
                    act.wait_ge(*multiplied.at(j - 2))
                nc.scalar.activation(gate[:, j % 3, :], gate_bank[j % 3][:], ACT.Sigmoid).then_inc(*gated.up())

        @block.vector
        def _(dve):
            for j, (half, t) in enumerate(jobs):
                dve.wait_ge(*gated.at(j + 1))
                m = merged[:, t, half * SEQ:(half + 1) * SEQ]
                if n == 0:
                    nc.vector.tensor_tensor(m, proj_bank[j % 3][:], gate[:, j % 3, :], ALU.mult
                                            ).then_inc(*multiplied.up())
                    continue
                if j >= 3:
                    dve.wait_ge(*added.at(j - 2))
                nc.vector.tensor_tensor(part[:, j % 3, :], proj_bank[j % 3][:], gate[:, j % 3, :], ALU.mult
                                        ).then_inc(*multiplied.up())
                dve.wait_ge(*multiplied.at(j + 1))
                nc.vector.tensor_tensor(m, m, part[:, j % 3, :], ALU.add).then_inc(*added.up())
    st.close()


def gate_with_z(core, stream, hT, item, y, out=None):
    nc = core.nc
    st = ExitStack()
    bank = [core.ps(st, f"z{b}") for b in range(4)]
    z = core.sb(st, "z", [P, 2, SEQ])
    gated, used = core.sig("z_ready"), core.sig("z_used")
    with core.block() as block:
        @block.sync
        def _(sp):
            stream.refill(sp, item, core.ready.at(NT))

        @block.tensor
        def _(pe):
            stream.arrived(pe, item)
            for t in range(NT):
                token_major(core, stream, hT, item, t, 0, SEQ)(bank[t]).then_inc(*core.ready.up())

        @block.scalar
        def _(act):
            for t in range(NT):
                act.wait_ge(*core.ready.at(t + 1))
                if t >= 2:
                    act.wait_ge(*used.at(t - 1))
                nc.scalar.activation(z[:, t % 2, :], bank[t][:], ACT.Silu).then_inc(*gated.up())

        @block.vector
        def _(dve):
            for t in range(NT):
                dve.wait_ge(*gated.at(t + 1))
                nc.vector.tensor_tensor(y[:, t, :], y[:, t, :], z[:, t % 2, :], ALU.mult).then_inc(*used.up())
    st.close()


def to_channels(core, y, yT, chunks):
    product_block(core, [transpose_job(core, [y[:, t, c * P:(c + 1) * P] for t in range(NT)],
                                       yT[:, c, :], "va"[c % 2]) for c in range(chunks)])


def head_rms(core, y, heads, width, gain):
    nc = core.nc
    st = ExitStack()
    sq = core.sb(st, "squares", [P, NT, heads, width])
    ss = core.sb(st, "sum_squares", [P, NT, heads])
    each = gain if len(gain.shape) == 3 else gain.unsqueeze(1).to_broadcast([P, heads, width])
    squared, summed, rooted = core.sig("heads_squared"), core.sig("heads_summed"), core.sig("heads_rooted")
    with core.block() as block:
        @block.scalar
        def _(act):
            for t in range(NT):
                nc.scalar.activation(sq[:, t], y[:, t, :].rearrange("p (h w) -> p h w", h=heads), ACT.Square
                                     ).then_inc(*squared.up())
            act.wait_ge(*summed.at(1))
            nc.scalar.activation(ss[:], ss[:], ACT.Sqrt, scale=1.0 / width, bias=core.eps[:, 0:1]).then_inc(*rooted.up())

        @block.vector
        def _(dve):
            link = linker(dve, core.vchain)
            dve.wait_ge(*squared.at(NT))
            nc.vector.tensor_reduce(ss[:], sq[:], AX.X, ALU.add).then_inc(*summed.up())
            dve.wait_ge(*rooted.at(1))
            link(nc.vector.reciprocal(ss[:], ss[:]))
            for t in range(NT):
                yt = y[:, t, :].rearrange("p (h w) -> p h w", h=heads)
                link(nc.vector.tensor_tensor(yt, yt, ss[:, t, :].unsqueeze(2).to_broadcast([P, heads, width]), ALU.mult))
                nc.vector.tensor_tensor(yt, yt, each, ALU.mult)
    st.close()


def small_products(core, stream, hT, w_small, small, gkT):
    nc = core.nc
    jobs = []
    for t in range(NT):
        def fill(bank, t=t):
            return sum_of(nc, bank[:, 0:40], [(hT[:, k, t * P:(t + 1) * P], w_small[:, k, 0:40]) for k in range(KD)])
        jobs.append((None, fill, "v", lambda link, bank, t=t: nc.vector.tensor_copy(small[:, t, :], bank[:, 0:40])))

    def fill_gk(bank):
        return sum_of(nc, bank[0:16, :], [(w_small[:, k, 40:56], hT[:, k, :]) for k in range(KD)])
    jobs.append((None, fill_gk, "v", lambda link, bank: nc.vector.tensor_copy(gkT[:], bank[0:16, :])))
    product_block(core, jobs)




def decay_rates(core, small, head_par, rate, dt, gates, beta):
    nc = core.nc
    st = ExitStack()
    x = core.sb(st, "x", [P, NT, 12])
    e = core.sb(st, "e", [P, NT, 12])
    a = core.sb(st, "a", [P, 12])
    shifted, logged, ready = core.sig("dt_shifted"), core.sig("dt_logged"), core.sig("a_exped")
    with core.block() as block:
        @block.vector
        def _(dve):
            link = linker(dve, core.vchain)
            nc.vector.tensor_tensor(x[:], small[:, :, 4:16], head_par[:, 12:24].unsqueeze(1).to_broadcast([P, NT, 12]), ALU.add
                                    ).then_inc(*shifted.up())
            dve.wait_ge(*logged.at(1))
            link(nc.vector.scalar_tensor_tensor(out=dt[:], in0=x[:], scalar=0.0, in1=e[:], op0=ALU.max, op1=ALU.add))
            dve.wait_ge(*ready.at(1))
            link(nc.vector.tensor_tensor(rate[:], dt[:], a[:].unsqueeze(1).to_broadcast([P, NT, 12]), ALU.mult))
            nc.vector.tensor_scalar(rate[:], rate[:], -1.0, None, ALU.mult)

        @block.scalar
        def _(act):
            link = linker(act, core.achain)
            act.wait_ge(*shifted.at(1))
            link(nc.scalar.activation(e[:], x[:], ACT.Abs))
            link(nc.scalar.activation(e[:], e[:], ACT.Exp, scale=-1.0))
            nc.scalar.activation(a[:], head_par[:, 0:12], ACT.Exp).then_inc(*ready.up())
            nc.scalar.activation(e[:], e[:], ACT.Ln, bias=core.one[:, 0:1]).then_inc(*logged.up())
            nc.scalar.activation(beta[:], small[:, :, 0:4], ACT.Sigmoid)
            nc.scalar.activation(gates[:], small[:, :, 16:40], ACT.Sigmoid)
    st.close()


def decay_sums(core, rate, upto, cum, e_cum, e_rest, e_total):
    nc = core.nc
    st = ExitStack()
    bank = core.ps(st, "sums")
    tot = core.sb(st, "total", [P, NT, 12])
    summed, split = core.sig("rates_summed"), core.sig("rates_split")
    n = NT * 12
    with core.block() as block:
        @block.tensor
        def _(pe):
            nc.tensor.matmul(bank[:, 0:n], upto, rate[:].rearrange("p t h -> p (t h)"), start=True, stop=True)
            nc.tensor.matmul(bank[:, n:2 * n], core.ones, rate[:].rearrange("p t h -> p (t h)"), start=True, stop=True
                             ).then_inc(*summed.up())

        @block.vector
        def _(dve):
            link = linker(dve, core.vchain)
            dve.wait_ge(*summed.at(1))
            link(nc.vector.tensor_copy(cum[:].rearrange("p t h -> p (t h)"), bank[:, 0:n]))
            nc.vector.tensor_tensor(tot[:].rearrange("p t h -> p (t h)"), bank[:, n:2 * n],
                                    cum[:].rearrange("p t h -> p (t h)"), ALU.subtract).then_inc(*split.up())

        @block.scalar
        def _(act):
            act.wait_ge(*split.at(1))
            nc.scalar.activation(e_rest[:], tot[:], ACT.Exp)
            nc.scalar.activation(e_cum[:], cum[:], ACT.Exp)
            nc.scalar.activation(e_total[:].rearrange("p t h -> p (t h)"), bank[:, n:2 * n], ACT.Exp)
    st.close()


def gdn(core, stream, hT, dec, y):
    nc, ins = core.nc, core.ins
    st = ExitStack()
    H = 4
    qT = core.sb(st, "qT", [P, H, SEQ])
    kT = core.sb(st, "kT", [P, H, SEQ])
    k = core.sb(st, "k", [P, NT, SEQ])
    v = core.sb(st, "v", [P, NT, SEQ])
    lower = core.sb(st, "lower", [P, NT, SEQ])
    inner = ExitStack()
    vT = core.sb(inner, "vT", [P, H, SEQ])
    taps = core.sb(inner, "taps", [P, 12, 4])
    with core.block() as block:
        @block.sync
        def _(sp):
            sp.dma_start(taps[:], ins["conv_a"]).then_inc(*core.dma.up(16))
            sp.wait_ge(*core.dma.at(16))
    conv_block(core, stream, hT, [(f"gdn{w}", c * P, dst[:, c, :], 4 * i + c)
                                  for i, (w, dst) in enumerate((("_q", qT), ("_k", kT), ("_v", vT))) for c in range(4)],
               taps, None)
    norm_channels(core, [[qT[:, h, :]] for h in range(H)] + [[kT[:, h, :]] for h in range(H)], core.ones,
                  core.eps[:, 0:1], [P ** -0.5] * H + [1.0] * H, P, mean=False)
    product_block(core, [transpose_job(core, [s[:, h, t * P:(t + 1) * P] for t in range(NT)],
                                       d[:, :, h * P:(h + 1) * P], "va"[h % 2])
                         for s, d in ((kT, k), (vT, v)) for h in range(H)])
    inner.close()
    attnT = core.sb(st, "attnT", [P, NT, SEQ])
    cum, e_cum, e_rest, e_total = (dec[x] for x in ("cum", "e_cum", "e_rest", "e_total"))
    rate, beta = dec["rate"], dec["beta"]

    inner = ExitStack()
    rows = [core.ps(inner, f"rows{b}") for b in range(2)]
    kk = [core.ps(inner, f"kk{b}") for b in range(2)]
    qk = [core.ps(inner, f"qk{b}") for b in range(2)]
    strict = core.sb(inner, "strict", [P, P])
    causal = core.sb(inner, "causal", [P, P])
    dl = core.sb(inner, "decay_lower", [P, 2, SEQ])
    da = core.sb(inner, "decay_attn", [P, 2, SEQ])
    dq = core.sb(inner, "decay_q", [P, 2, SEQ])
    spread, exped, used = core.sig("tile_exponents"), core.sig("tile_exped"), core.sig("tile_decays_used")
    hb = lambda ap, t: ap[:, t, 0:H].unsqueeze(2).to_broadcast([P, H, P])
    four = lambda ap: ap.rearrange("p (h c) -> p h c", h=H)
    with core.block() as block:
        @block.sync
        def _(sp):
            sp.dma_start(strict[:], core.const("strict_bias")).then_inc(*core.dma.up(16))
            sp.dma_start(causal[:], core.const("causal_biasT")).then_inc(*core.dma.up(16))

        @block.tensor
        def _(pe):
            for t in range(NT):
                if t >= 2:
                    pe.wait_ge(*used.at(t - 1))
                    pe.wait_ge(*exped.at(t - 1))
                tile = slice(t * P, (t + 1) * P)
                for h in range(H):
                    nc.tensor.matmul(rows[t % 2][:, h * P:(h + 1) * P], rate[:, t, h:h + 1].to_broadcast([P, P]),
                                     core.upto, start=True, stop=True)
                for h in range(H):
                    nc.tensor.matmul(kk[t % 2][:, h * P:(h + 1) * P], kT[:, h, tile], kT[:, h, tile], start=True, stop=True)
                for h in range(H):
                    last = nc.tensor.matmul(qk[t % 2][:, h * P:(h + 1) * P], kT[:, h, tile], qT[:, h, tile],
                                            start=True, stop=True)
                last.then_inc(*core.ready.up())

        @block.vector
        def _(dve):
            link = linker(dve, core.vchain)
            dve.wait_ge(*core.dma.at(32))

            def exponents(t):
                dve.wait_ge(*core.ready.at(t + 1))
                r = four(rows[t % 2][:])
                l, a = four(dl[:, t % 2, :]), four(da[:, t % 2, :])
                link(nc.vector.tensor_tensor(l, strict[:].unsqueeze(1).to_broadcast([P, H, P]), r, ALU.subtract))
                link(nc.vector.tensor_tensor(a, causal[:].unsqueeze(1).to_broadcast([P, H, P]), r, ALU.add))
                link(nc.vector.tensor_tensor(l, l, hb(cum, t), ALU.add))
                nc.vector.tensor_tensor(a, a, hb(cum, t), ALU.subtract).then_inc(*spread.up())

            def scores(t):
                dve.wait_ge(*exped.at(t + 1))
                lo = lower[:, t, :]
                q = qT[:, :, t * P:(t + 1) * P]
                link(nc.vector.tensor_tensor(lo, kk[t % 2][:], dl[:, t % 2, :], ALU.mult))
                nc.vector.tensor_tensor(attnT[:, t, :], qk[t % 2][:], da[:, t % 2, :], ALU.mult)
                nc.vector.tensor_tensor(q, q, four(dq[:, t % 2, :]), ALU.mult)
                nc.vector.tensor_tensor(four(lo), four(lo), hb(beta, t), ALU.mult).then_inc(*used.up())
            exponents(0)
            for t in range(NT):
                if t + 1 < NT:
                    exponents(t + 1)
                scores(t)

        @block.scalar
        def _(act):
            for t in range(NT):
                act.wait_ge(*spread.at(t + 1))
                if t >= 2:
                    act.wait_ge(*used.at(t - 1))
                nc.scalar.activation(dl[:, t % 2, :], dl[:, t % 2, :], ACT.Exp)
                nc.scalar.activation(da[:, t % 2, :], da[:, t % 2, :], ACT.Exp)
                nc.scalar.activation(dq[:, t % 2, :], rows[t % 2][:], ACT.Exp).then_inc(*exped.up())
    inner.close()

    inner = ExitStack()
    inv = core.sb(inner, "inv", [P, NT, SEQ])
    invT = core.sb(inner, "invT", [P, NT, SEQ])
    level = core.sb(inner, "levels", [P, 7, P])
    pair = core.sb(inner, "pair_blocks", [P, 2, SEQ])
    mid = core.sb(inner, "pair_times_inv", [P, 2, SEQ])
    psum_in = ExitStack()
    first = [core.ps(psum_in, f"first{b}") for b in range(2)]
    second = [core.ps(psum_in, f"second{b}") for b in range(2)]
    third = [core.ps(psum_in, f"third{b}") for b in range(2)]
    masked, halfway, copied, twice, updated = (core.sig(x) for x in (
        "pair_masked", "pair_inv_product", "pair_inv_copied", "inverse_products", "inverse_updated"))
    jobs = [(lvl, t) for lvl in range(7) for t in range(NT)]
    n = len(jobs)
    with core.block() as block:
        @block.sync
        def _(sp):
            for lvl in range(7):
                sp.dma_start(level[:, lvl, :], core.const(f"level{lvl}")).then_inc(*core.dma.up(16))
            sp.wait_ge(*core.dma.at(16 * 7))

        @block.vector
        def _(dve):
            for t in range(NT):
                nc.vector.tensor_copy(four(inv[:, t, :]), core.ident.unsqueeze(1).to_broadcast([P, H, P]))
                nc.vector.tensor_copy(four(invT[:, t, :]), core.ident.unsqueeze(1).to_broadcast([P, H, P]))
    with core.block() as block:
        @block.tensor
        def _(pe):
            def one(j):
                lvl, t = jobs[j]
                pe.wait_ge(*masked.at(j + 1))
                if j >= NT:
                    pe.wait_ge(*updated.at(j - NT + 1))
                if j >= 2:
                    pe.wait_ge(*copied.at(j - 1))
                for h in range(H):
                    s = slice(h * P, (h + 1) * P)
                    last = nc.tensor.matmul(first[j % 2][:, s], pair[:, j % 2, s], invT[:, t, s], start=True, stop=True)
                last.then_inc(*halfway.up())

            def two(j):
                lvl, t = jobs[j]
                pe.wait_ge(*copied.at(j + 1))
                if j >= 2:
                    pe.wait_ge(*updated.at(j - 1))
                for h in range(H):
                    s = slice(h * P, (h + 1) * P)
                    nc.tensor.matmul(second[j % 2][:, s], inv[:, t, s], mid[:, j % 2, s], start=True, stop=True)
                    last = nc.tensor.matmul(third[j % 2][:, s], mid[:, j % 2, s], inv[:, t, s], start=True, stop=True)
                last.then_inc(*twice.up())
            one(0)
            for j in range(n):
                if j + 1 < n:
                    one(j + 1)
                two(j)

        @block.scalar
        def _(act):
            for j in range(n):
                act.wait_ge(*halfway.at(j + 1))
                if j >= 2:
                    act.wait_ge(*twice.at(j - 1))
                nc.scalar.copy(mid[:, j % 2, :], first[j % 2][:]).then_inc(*copied.up())

        @block.vector
        def _(dve):
            def mask(j):
                lvl, t = jobs[j]
                if j >= 2:
                    dve.wait_ge(*halfway.at(j - 1))
                nc.vector.tensor_tensor(four(pair[:, j % 2, :]), four(lower[:, t, :]),
                                        level[:, lvl, :].unsqueeze(1).to_broadcast([P, H, P]), ALU.mult).then_inc(*masked.up())

            def update(j):
                lvl, t = jobs[j]
                dve.wait_ge(*twice.at(j + 1))
                if j >= NT:
                    dve.wait_ge(*updated.at(j - NT + 1))
                nc.vector.tensor_tensor(invT[:, t, :], invT[:, t, :], second[j % 2][:], ALU.subtract)
                nc.vector.tensor_tensor(inv[:, t, :], inv[:, t, :], third[j % 2][:], ALU.subtract).then_inc(*updated.up())
            mask(0)
            for j in range(n):
                if j + 1 < n:
                    mask(j + 1)
                update(j)
    psum_in.close()

    u, wT = lower, inv
    kb = pair
    psum_in = ExitStack()
    u_bank = [core.ps(psum_in, f"u{b}") for b in range(2)]
    w_bank = [core.ps(psum_in, f"w{b}") for b in range(2)]
    scaled, solved, kept = core.sig("kv_scaled"), core.sig("kv_solved"), core.sig("kv_kept")
    with core.block() as block:
        @block.vector
        def _(dve):
            link = linker(dve, core.vchain)
            for t in range(NT):
                if t >= 2:
                    dve.wait_ge(*solved.at(t - 1))
                k4, v4, b4 = four(k[:, t, :]), four(v[:, t, :]), four(kb[:, t % 2, :])
                link(nc.vector.tensor_tensor(b4, k4, hb(beta, t), ALU.mult))
                nc.vector.tensor_tensor(v4, v4, hb(beta, t), ALU.mult)
                nc.vector.tensor_tensor(k4, k4, hb(e_rest, t), ALU.mult)
                nc.vector.tensor_tensor(b4, b4, hb(e_cum, t), ALU.mult).then_inc(*scaled.up())

        @block.tensor
        def _(pe):
            for t in range(NT):
                pe.wait_ge(*scaled.at(t + 1))
                if t >= 2:
                    pe.wait_ge(*kept.at(t - 1))
                for h in range(H):
                    s = slice(h * P, (h + 1) * P)
                    nc.tensor.matmul(u_bank[t % 2][:, s], invT[:, t, s], v[:, t, s], start=True, stop=True)
                    last = nc.tensor.matmul(w_bank[t % 2][:, s], kb[:, t % 2, s], invT[:, t, s], start=True, stop=True)
                last.then_inc(*solved.up())

        @block.scalar
        def _(act):
            for t in range(NT):
                act.wait_ge(*solved.at(t + 1))
                nc.scalar.copy(u[:, t, :], u_bank[t % 2][:])
                nc.scalar.copy(wT[:, t, :], w_bank[t % 2][:]).then_inc(*kept.up())
    psum_in.close()

    state = core.sb(inner, "state", [P, SEQ])
    new = mid
    psum_in = ExitStack()
    ws_bank = core.ps(psum_in, "ws")
    y_bank = [core.ps(psum_in, f"y{b}") for b in range(2)]
    s_bank = core.ps(psum_in, "ds")
    from_state, renewed, stepped, moved, written = (core.sig(x) for x in (
        "state_read", "values_renewed", "state_step_ready", "state_updated", "scan_written"))
    with core.block() as block:
        @block.vector
        def _(dve):
            link = linker(dve, core.vchain)
            nc.vector.memset(state[:], 0.0).then_inc(*moved.up())
            for t in range(NT):
                dve.wait_ge(*from_state.at(t + 1))
                nc.vector.tensor_tensor(new[:, t % 2, :], u[:, t, :], ws_bank[:], ALU.subtract).then_inc(*renewed.up())
                dve.wait_ge(*stepped.at(t + 1))
                if t == 0:
                    dve.wait_ge(*moved.at(1))
                link(nc.vector.tensor_tensor(four(state[:]), four(state[:]), hb(e_total, t), ALU.mult))
                nc.vector.tensor_tensor(state[:], state[:], s_bank[:], ALU.add).then_inc(*moved.up())
                if t < NT - 1:
                    dve.wait_ge(*moved.at(t + 2))

        @block.tensor
        def _(pe):
            for t in range(NT):
                tile = slice(t * P, (t + 1) * P)
                pe.wait_ge(*moved.at(t + 1))
                for h in range(H):
                    s = slice(h * P, (h + 1) * P)
                    last = nc.tensor.matmul(ws_bank[:, s], wT[:, t, s], state[:, s], start=True, stop=True)
                last.then_inc(*from_state.up())
                pe.wait_ge(*renewed.at(t + 1))
                if t >= 2:
                    pe.wait_ge(*written.at(t - 1))
                for h in range(H):
                    s = slice(h * P, (h + 1) * P)
                    sum_of(nc, y_bank[t % 2][:, s], [(qT[:, h, tile], state[:, s]), (attnT[:, t, s], new[:, t % 2, s])])
                for h in range(H):
                    s = slice(h * P, (h + 1) * P)
                    last = nc.tensor.matmul(s_bank[:, s], k[:, t, s], new[:, t % 2, s], start=True, stop=True)
                last.then_inc(*stepped.up())

        @block.scalar
        def _(act):
            for t in range(NT):
                act.wait_ge(*stepped.at(t + 1))
                nc.scalar.copy(y[:, t, :], y_bank[t % 2][:]).then_inc(*written.up())
    psum_in.close()
    inner.close()
    st.close()


def gla(core, stream, hT, gkT, y):
    nc, ins = core.nc, core.ins
    st = ExitStack()
    H, DK, DV = 4, 64, 128
    qk = core.sb(st, "qk", [P, NT, SEQ])
    v = core.sb(st, "v", [P, NT, SEQ])
    gk = core.sb(st, "gk", [P, NT, 256])
    w_gk = core.sb(st, "w_gk", [16, 256])
    b_gk = core.sb(st, "b_gk", [P, 256])
    mats = core.sb(st, "sum_matrices", [P, 7, P])
    names = ("gla_from_mid", "gla_within", "gla_to_half_end", "upto", "gla_to_end", "gla_near", "gla_far")
    jobs = []
    for t in range(NT):
        fill = token_major(core, stream, hT, "gla_qk", t, 0, SEQ)

        def read(link, bank, t=t):
            link(nc.vector.tensor_scalar(qk[:, t, 0:256], bank[:, 0:256], DK ** -0.5, None, ALU.mult))
            return nc.vector.tensor_copy(qk[:, t, 256:512], bank[:, 256:512])
        jobs.append(("gla_qk", fill, "v", read))
    for t in range(NT):
        jobs.append(("gla_v", token_major(core, stream, hT, "gla_v", t, 0, SEQ), "a",
                     lambda link, bank, t=t: nc.scalar.copy(v[:, t, :], bank[:])))
    for t in range(NT):
        jobs.append((None, lambda bank, t=t: nc.tensor.matmul(bank[:, 0:256], gkT[:, t * P:(t + 1) * P], w_gk[:],
                                                              start=True, stop=True), "v",
                     lambda link, bank, t=t: nc.vector.tensor_tensor(gk[:, t, :], bank[:, 0:256], b_gk[:], ALU.add)))
    product_block(core, jobs, stream, loads=[(w_gk[:], ins["w_gk"][0]), (b_gk[:], ins["b_gk"].to_broadcast([P, 256]))]
                  + [(mats[:, i, :], core.const(x)) for i, x in enumerate(names)])

    inner = ExitStack()
    mag = core.sb(inner, "mag", [P, NT, 256])
    logged = core.sig("gk_logged")
    with core.block() as block:
        @block.vector
        def _(dve):
            link = linker(dve, core.vchain)
            dve.wait_ge(*logged.at(1))
            link(nc.vector.scalar_tensor_tensor(out=gk[:], in0=gk[:], scalar=0.0, in1=mag[:], op0=ALU.min, op1=ALU.subtract))
            nc.vector.tensor_scalar(gk[:], gk[:], 1.0 / 16.0, None, ALU.mult)

        @block.scalar
        def _(act):
            link = linker(act, core.achain)
            link(nc.scalar.activation(mag[:], gk[:], ACT.Abs))
            link(nc.scalar.activation(mag[:], mag[:], ACT.Exp, scale=-1.0))
            nc.scalar.activation(mag[:], mag[:], ACT.Ln, bias=core.one[:, 0:1]).then_inc(*logged.up())
    inner.close()

    inner = ExitStack()
    state = core.sb(inner, "state", [DK, H * DV])
    dec = core.sb(inner, "state_decay", [DK, NT * H])
    ex = core.sb(inner, "exps", [P, 6, 256])
    fac = core.sb(inner, "factors", [P, 6, 256])
    facT = core.sb(inner, "factorsT", [DK, 5, H * P])
    aT = core.sb(inner, "aT", [P, 2, H * P])
    summed, exped, moved = core.sig("gk_summed"), core.sig("gk_exped"), core.sig("gla_state")
    tot = core.ps(inner, "totals")
    with core.block() as block:
        @block.tensor
        def _(pe):
            for t in range(NT):
                for h in range(H):
                    i = t * H + h
                    last = nc.tensor.matmul(tot[0:DK, i:i + 1], gk[:, t, h * DK:(h + 1) * DK], core.ones[:, 0:1],
                                            start=True, stop=True)
            last.then_inc(*summed.up())

        @block.scalar
        def _(act):
            act.wait_ge(*summed.at(1))
            nc.scalar.activation(dec[:], tot[0:DK, 0:NT * H], ACT.Exp)

        @block.vector
        def _(dve):
            nc.vector.memset(state[:], 0.0)
    sums = [core.ps(inner, f"sums{b}") for b in range(3)]
    for t in range(NT):
        with core.block() as block:
            @block.tensor
            def _(pe):
                for i in range(5):
                    last = nc.tensor.matmul(sums[i // 2][:, (i % 2) * 256:(i % 2) * 256 + 256], mats[:, i, :], gk[:, t, :],
                                            start=True, stop=True)
                last.then_inc(*summed.up())

            @block.scalar
            def _(act):
                act.wait_ge(*summed.at(1))
                for i in range(6):
                    src = 0 if i == 5 else i
                    nc.scalar.activation(ex[:, i, :], sums[src // 2][:, (src % 2) * 256:(src % 2) * 256 + 256], ACT.Exp,
                                         scale=-1.0 if i == 5 else 1.0).then_inc(*exped.up())

            @block.vector
            def _(dve):
                for i in range(6):
                    dve.wait_ge(*exped.at(i + 1))
                    src = qk[:, t, 0:256] if i in (0, 1, 3) else qk[:, t, 256:512]
                    nc.vector.tensor_tensor(fac[:, i, :], ex[:, i, :], src, ALU.mult)
        order = (0, 1, 3, 5, 2)
        product_block(core, [transpose_job(core, [fac[:, i, h * DK:(h + 1) * DK] for h in range(H)],
                                           facT[:, n, :], "va"[n % 2]) for n, i in enumerate(order)], banks=4)
        q_near, q_far, q_state, k_near, k_far = (facT[:, n, :] for n in range(5))
        k_end = fac[:, 4, :]
        psum_in = ExitStack()
        near, far, y_bank, s_bank = (core.ps(psum_in, x) for x in ("near", "far", "y", "ds"))
        scored, masked, stepped = core.sig("gla_scored"), core.sig("gla_masked"), core.sig("gla_stepped")
        with core.block() as block:
            @block.tensor
            def _(pe):
                for h in range(H):
                    s = slice(h * P, (h + 1) * P)
                    nc.tensor.matmul(near[:, s], k_near[:, s], q_near[:, s], start=True, stop=True)
                for h in range(H):
                    s = slice(h * P, (h + 1) * P)
                    last = nc.tensor.matmul(far[:, s], k_far[:, s], q_far[:, s], start=True, stop=True)
                last.then_inc(*scored.up())
                pe.wait_ge(*masked.at(1))
                for h in range(H):
                    s = slice(h * P, (h + 1) * P)
                    sum_of(nc, y_bank[:, s], [(q_state[:, s], state[:, s]), (aT[:, 0, s], v[:, t, s])])
                for h in range(H):
                    s = slice(h * P, (h + 1) * P)
                    last = nc.tensor.matmul(s_bank[0:DK, s], k_end[:, h * DK:(h + 1) * DK], v[:, t, s], start=True, stop=True)
                last.then_inc(*stepped.up())

            @block.vector
            def _(dve):
                link = linker(dve, core.vchain)
                four = lambda ap: ap.rearrange("p (h c) -> p h c", h=H)
                m = lambda i: mats[:, i, :].unsqueeze(1).to_broadcast([P, H, P])
                dve.wait_ge(*scored.at(1))
                link(nc.vector.scalar_tensor_tensor(out=four(aT[:, 0, :]), in0=four(near[:]), scalar=3e38, in1=m(5),
                                                    op0=ALU.min, op1=ALU.mult))
                link(nc.vector.tensor_tensor(four(aT[:, 1, :]), four(far[:]), m(6), ALU.mult))
                nc.vector.tensor_tensor(aT[:, 0, :], aT[:, 0, :], aT[:, 1, :], ALU.add).then_inc(*masked.up())
                dve.wait_ge(*stepped.at(1))
                for h in range(H):
                    s = slice(h * P, (h + 1) * P)
                    i = t * H + h
                    nc.vector.scalar_tensor_tensor(out=state[:, s], in0=state[:, s], scalar=dec[:, i:i + 1],
                                                   in1=s_bank[0:DK, s], op0=ALU.mult, op1=ALU.add)

            @block.scalar
            def _(act):
                act.wait_ge(*stepped.at(1))
                nc.scalar.copy(y[:, t, :], y_bank[:])
        psum_in.close()
    inner.close()
    st.close()


def ssd(core, stream, hT, dec, y):
    nc, ins = core.nc, core.ins
    st = ExitStack()
    H, HD = 8, 64
    x = core.sb(st, "x", [P, NT, SEQ])
    Bt = core.sb(st, "B", [P, NT, 256])
    bT = core.sb(st, "BT", [P, 2, SEQ])
    cT = core.sb(st, "CT", [P, 2, SEQ])
    skip = core.sb(st, "skip", [P, H])
    inner = ExitStack()
    xT = core.sb(inner, "xT", [P, 4, SEQ])
    taps = core.sb(inner, "taps", [P, 8, 4])
    bias = core.sb(inner, "bias", [P, 8])
    with core.block() as block:
        @block.sync
        def _(sp):
            sp.dma_start(taps[:], ins["conv_c"]).then_inc(*core.dma.up(16))
            sp.dma_start(bias[:], ins["conv_bias_c"]).then_inc(*core.dma.up(16))
            sp.dma_start(skip[:], ins["d_skip_c"].to_broadcast([P, H])).then_inc(*core.dma.up(16))
            sp.wait_ge(*core.dma.at(48))
    conv_block(core, stream, hT, [("ssd_x", c * P, xT[:, c, :], c) for c in range(4)]
               + [("ssd_bc", c * P, (bT if c < 2 else cT)[:, c % 2, :], 4 + c) for c in range(4)], taps, bias)
    product_block(core, [transpose_job(core, [s[:, c, t * P:(t + 1) * P] for t in range(NT)],
                                       d[:, :, c * P:(c + 1) * P], "va"[c % 2])
                         for s, d, n in ((xT, x, 4), (bT, Bt, 2)) for c in range(n)])
    inner.close()

    inner = ExitStack()
    causal = core.sb(inner, "causal", [P, P])
    decay = core.sb(inner, "decay", [P, 2, H, P])
    xdt = core.sb(inner, "x_dt", [P, 2, SEQ])
    xend = core.sb(inner, "x_end", [P, 2, SEQ])
    state = core.sb(inner, "state", [P, SEQ])
    part = core.sb(inner, "part", [P, SEQ])
    rows = [core.ps(inner, f"rows{b}") for b in range(2)]
    cb, y_in, y_off, s_bank = (core.ps(inner, n) for n in ("cb", "y_in", "y_off", "ds"))
    cum, e_cum, e_rest, e_total, rate, dt = (dec[k] for k in ("cum", "e_cum", "e_rest", "e_total", "rate", "dt"))
    hb = lambda ap, t, w: ap[:, t, 4:12].unsqueeze(2).to_broadcast([P, H, w])
    per = lambda ap: ap.rearrange("p (h c) -> p h c", h=H)
    spread, exped, scaled, stepped, moved, used = (core.sig(n) for n in (
        "ssd_exponents", "ssd_exped", "ssd_scaled", "ssd_stepped", "ssd_state", "ssd_rows_read"))
    with core.block() as block:
        @block.sync
        def _(sp):
            sp.dma_start(causal[:], core.const("causal_biasT")).then_inc(*core.dma.up(16))

        @block.tensor
        def _(pe):
            def scores(t):
                tile = slice(t * P, (t + 1) * P)
                if t >= 1:
                    pe.wait_ge(*used.at(t))
                    pe.wait_ge(*scaled.at(t))
                for h in range(H):
                    nc.tensor.matmul(rows[h // 4][:, (h % 4) * P:(h % 4 + 1) * P],
                                     rate[:, t, 4 + h:5 + h].to_broadcast([P, P]), core.upto, start=True, stop=True)
                for g in range(2):
                    last = nc.tensor.matmul(cb[:, g * P:(g + 1) * P], bT[:, g, tile], cT[:, g, tile], start=True, stop=True)
                last.then_inc(*core.ready.up())

            def outputs(t):
                tile = slice(t * P, (t + 1) * P)
                pe.wait_ge(*scaled.at(t + 1))
                pe.wait_ge(*moved.at(t + 1))
                for h in range(H):
                    s = slice(h * HD, (h + 1) * HD)
                    nc.tensor.matmul(y_in[:, s], decay[:, t % 2, h, :], xdt[:, t % 2, s], start=True, stop=True)
                for g in range(2):
                    s = slice(g * 256, (g + 1) * 256)
                    nc.tensor.matmul(y_off[:, s], cT[:, g, tile], state[:, s], start=True, stop=True)
                for g in range(2):
                    s = slice(g * 256, (g + 1) * 256)
                    last = nc.tensor.matmul(s_bank[:, s], Bt[:, t, g * P:(g + 1) * P], xend[:, t % 2, s], start=True, stop=True)
                last.then_inc(*stepped.up())
            scores(0)
            for t in range(NT):
                if t + 1 < NT:
                    scores(t + 1)
                outputs(t)

        @block.vector
        def _(dve):
            link = linker(dve, core.vchain)
            dve.wait_ge(*core.dma.at(16))
            nc.vector.memset(state[:], 0.0).then_inc(*moved.up())

            def exponents(t):
                dve.wait_ge(*core.ready.at(t + 1))
                for half in range(2):
                    link(nc.vector.tensor_tensor(decay[:, t % 2, 4 * half:4 * half + 4, :],
                                                 rows[half][:].rearrange("p (h c) -> p h c", h=4),
                                                 causal[:].unsqueeze(1).to_broadcast([P, 4, P]), ALU.add))
                nc.vector.tensor_tensor(decay[:, t % 2], decay[:, t % 2], hb(cum, t, P), ALU.subtract).then_inc(*spread.up())
                link(nc.vector.tensor_tensor(per(xdt[:, t % 2, :]), per(x[:, t, :]), hb(dt, t, HD), ALU.mult))
                nc.vector.tensor_tensor(per(xend[:, t % 2, :]), per(xdt[:, t % 2, :]), hb(e_rest, t, HD), ALU.mult).then_inc(*used.up())
                dve.wait_ge(*exped.at(t + 1))
                for g in range(2):
                    d = decay[:, t % 2, 4 * g:4 * g + 4, :]
                    ins = nc.vector.tensor_tensor(d, d, cb[:, g * P:(g + 1) * P].unsqueeze(1).to_broadcast([P, 4, P]), ALU.mult)
                ins.then_inc(*scaled.up())

            def collect(t):
                dve.wait_ge(*stepped.at(t + 1))
                link(nc.vector.tensor_tensor(per(y[:, t, :]), per(y_off[:]), hb(e_cum, t, HD), ALU.mult))
                link(nc.vector.tensor_tensor(y[:, t, :], y[:, t, :], y_in[:], ALU.add))
                link(nc.vector.tensor_tensor(per(part[:]), per(x[:, t, :]),
                                             skip[:].unsqueeze(2).to_broadcast([P, H, HD]), ALU.mult))
                link(nc.vector.tensor_tensor(y[:, t, :], y[:, t, :], part[:], ALU.add))
                if t == 0:
                    dve.wait_ge(*moved.at(1))
                link(nc.vector.tensor_tensor(per(state[:]), per(state[:]), hb(e_total, t, HD), ALU.mult))
                nc.vector.tensor_tensor(state[:], state[:], s_bank[:], ALU.add).then_inc(*moved.up())
                dve.wait_ge(*moved.at(t + 2))
            exponents(0)
            for t in range(NT):
                if t + 1 < NT:
                    exponents(t + 1)
                collect(t)

        @block.scalar
        def _(act):
            for t in range(NT):
                act.wait_ge(*spread.at(t + 1))
                nc.scalar.activation(decay[:, t % 2], decay[:, t % 2], ACT.Exp).then_inc(*exped.up())
    inner.close()
    st.close()


def attention(core, jobs, tables=()):
    nc = core.nc
    st = ExitStack()
    s_bank = [core.ps(st, f"scores{b}") for b in range(2)]
    t_bank = [core.ps(st, f"turned{b}") for b in range(2)]
    o_bank = [core.ps(st, f"mixed{b}") for b in range(2)]
    sc = core.sb(st, "biased", [P, 2, SEQ])
    pr = core.sb(st, "probs", [P, 2, SEQ])
    prT = core.sb(st, "probsT", [P, 2, SEQ])
    top = core.sb(st, "row_max", [P, 4])
    neg = core.sb(st, "neg_max", [P, 4])
    den = core.sb(st, "row_sum", [P, 4])
    inv = core.sb(st, "inverse", [P, 4])
    names = ("att_scored", "att_maxed", "att_exped", "att_transposed", "att_turned", "att_mixed", "att_written", "att_table")
    scored, maxed, exped, transposed, turned, mixed, written, tabled = (core.sig(x) for x in names)
    n = len(jobs)
    with core.block() as block:
        @block.gpsimd
        def _(pool):
            link = linker(pool, core.gchain)
            for after, build in tables:
                if after > 0:
                    pool.wait_ge(*maxed.at(after))
                build(link).then_inc(*tabled.up())

        @block.tensor
        def _(pe):
            def scores(j):
                if j >= 2:
                    pe.wait_ge(*maxed.at(j - 1))
                job = jobs[j]
                sum_of(nc, s_bank[j % 2][:, 0:job["n"]], list(zip(job["q"], job["k"]))).then_inc(*scored.up())

            def turn(j):
                pe.wait_ge(*exped.at(j + 1))
                if j >= 2:
                    pe.wait_ge(*turned.at(j - 1))
                job = jobs[j]
                for c in range(-(-job["n"] // P)):
                    w = min(P, job["n"] - c * P)
                    last = nc.tensor.transpose(t_bank[j % 2][0:w, c * P:(c + 1) * P],
                                               pr[:, j % 2, c * P:c * P + w], core.ident)
                last.then_inc(*transposed.up())

            def mix(j):
                pe.wait_ge(*turned.at(j + 1))
                if j >= 2:
                    pe.wait_ge(*written.at(j - 1))
                job = jobs[j]
                sum_of(nc, o_bank[j % 2][:, 0:job["dv"]],
                       [(prT[0:rows, j % 2, c * P:(c + 1) * P], v) for c, (rows, v) in enumerate(job["v"])]
                       ).then_inc(*mixed.up())
            for j in range(n + 2):
                if j < n:
                    scores(j)
                if 1 <= j <= n:
                    turn(j - 1)
                if j >= 2:
                    mix(j - 2)

        @block.vector
        def _(dve):
            link = linker(dve, core.vchain)

            def maximum(j):
                job = jobs[j]
                w = job["n"]
                dve.wait_ge(*scored.at(j + 1))
                if job.get("table") is not None:
                    dve.wait_ge(*tabled.at(job["table"] + 1))
                if j >= 2:
                    dve.wait_ge(*exped.at(j - 1))
                i = j % 4
                link(nc.vector.tensor_tensor_reduce(sc[:, j % 2, 0:w], s_bank[j % 2][:, 0:w], job["bias"], 1.0, -1e20,
                                                    ALU.add, ALU.max, top[:, i:i + 1]))
                nc.vector.tensor_scalar(neg[:, i:i + 1], top[:, i:i + 1], -1.0, None, ALU.mult).then_inc(*maxed.up())

            def output(j):
                job = jobs[j]
                i = j % 4
                dve.wait_ge(*mixed.at(j + 1))
                link(nc.vector.tensor_scalar(inv[:, i:i + 1], den[:, i:i + 1], 1e-30, None, ALU.max))
                link(nc.vector.reciprocal(inv[:, i:i + 1], inv[:, i:i + 1]))
                if job["gate"] is not None:
                    link(nc.vector.tensor_scalar(inv[:, i:i + 1], inv[:, i:i + 1], job["gate"], None, ALU.mult))
                o = o_bank[j % 2][:, 0:job["dv"]]
                if job["add"]:
                    dve.wait_ge(*written.at(j))
                    ins = nc.vector.scalar_tensor_tensor(out=job["out"], in0=o, scalar=inv[:, i:i + 1], in1=job["out"],
                                                         op0=ALU.mult, op1=ALU.add)
                else:
                    ins = nc.vector.tensor_scalar(job["out"], o, inv[:, i:i + 1], None, ALU.mult)
                ins.then_inc(*written.up())
            for j in range(n + 2):
                if j < n:
                    maximum(j)
                if j >= 2:
                    output(j - 2)

        @block.scalar
        def _(act):
            def exponentials(j):
                w = jobs[j]["n"]
                i = j % 4
                act.wait_ge(*maxed.at(j + 1))
                if j >= 2:
                    act.wait_ge(*transposed.at(j - 1))
                nc.scalar.activation(pr[:, j % 2, 0:w], sc[:, j % 2, 0:w], ACT.Exp, bias=neg[:, i:i + 1],
                                     accum_out=den[:, i:i + 1]).then_inc(*exped.up())

            def keep(j):
                job = jobs[j]
                act.wait_ge(*transposed.at(j + 1))
                if j >= 2:
                    act.wait_ge(*mixed.at(j - 1))
                c = -(-job["n"] // P)
                rows = min(P, job["n"])
                nc.scalar.copy(prT[0:rows, j % 2, 0:c * P], t_bank[j % 2][0:rows, 0:c * P]).then_inc(*turned.up())
            for j in range(n + 1):
                if j < n:
                    exponentials(j)
                if j >= 1:
                    keep(j - 1)
    st.close()


def band_of(table, tile, n):
    at = (NT - 1 - tile) * P
    return table[:, at:at + n]


def nsa(core, stream, hT, gates, y):
    nc, ins = core.nc, core.ins
    st = ExitStack()
    HD = 64
    qT = core.sb(st, "qT", [P, 4, SEQ])
    ksT = core.sb(st, "ksT", [P, SEQ])
    kwT = core.sb(st, "kwT", [P, SEQ])
    vs = core.sb(st, "vs", [P, NT, P])
    vw = core.sb(st, "vw", [P, NT, P])
    kcmpT = core.sb(st, "kcmpT", [P, 32])
    vcmp = core.sb(st, "vcmp", [32, P])
    inner = ExitStack()
    cT = {c: core.sb(inner, f"{c}T", [HD, 2, SEQ]) for c in ("kc", "vc")}
    jobs = []
    for h in range(4):
        jobs.append(("nsa_q", channel_major(core, stream, hT, "nsa_q", h * P, P), "v", lambda link, bank, h=h: nc.vector.tensor_scalar(
            qT[:, h, :], bank[:], HD ** -0.5, None, ALU.mult)))
    for i, c in enumerate(("kc", "vc")):
        for g in range(2):
            jobs.append(("nsa_kv", channel_major(core, stream, hT, "nsa_kv", i * P + g * HD, HD), "a",
                         lambda link, bank, c=c, g=g: nc.scalar.copy(cT[c][:, g, :], bank[0:HD, :])))
    jobs.append(("nsa_kv", channel_major(core, stream, hT, "nsa_kv", 2 * P, P), "v",
                 lambda link, bank: nc.vector.tensor_copy(ksT[:], bank[:])))
    for t in range(NT):
        jobs.append(("nsa_kv", token_major(core, stream, hT, "nsa_kv", t, 3 * P, P), "a",
                     lambda link, bank, t=t: nc.scalar.copy(vs[:, t, :], bank[:, 0:P])))
    jobs.append(("nsa_w", channel_major(core, stream, hT, "nsa_w", 0, P), "v",
                 lambda link, bank: nc.vector.tensor_copy(kwT[:], bank[:])))
    for t in range(NT):
        jobs.append(("nsa_w", token_major(core, stream, hT, "nsa_w", t, P, P), "a",
                     lambda link, bank, t=t: nc.scalar.copy(vw[:, t, :], bank[:, 0:P])))
    product_block(core, jobs, stream)

    w1 = {c: core.sb(inner, f"w_{c}1", [HD, 32, HD]) for c in ("k", "v")}
    w2 = {c: core.sb(inner, f"w_{c}2", [HD, HD]) for c in ("k", "v")}
    pos = {c: core.sb(inner, f"pos_{c}", [HD, 32]) for c in ("k", "v")}
    hid = {c: core.sb(inner, f"hidden_{c}", [HD, 2, N_CMP]) for c in ("k", "v")}
    pb = core.sb(inner, "pos_bias", [HD, 2])
    loads = []
    for c in ("k", "v"):
        loads += [(w1[c][:], ins[f"w_c{c}1"]), (w2[c][:], ins[f"w_c{c}2"][0]), (pos[c][:], ins[f"cmp_pos_{c}"])]
    jobs = []
    for i, c in enumerate(("k", "v")):
        jobs.append((None, lambda bank, c=c: sum_of(nc, bank[0:HD, 0:1], [(w1[c][:, l, :], pos[c][:, l:l + 1]) for l in range(32)]),
                     "a", lambda link, bank, i=i: nc.scalar.copy(pb[:, i:i + 1], bank[0:HD, 0:1])))
    for i, c in enumerate(("k", "v")):
        def fill(bank, c=c):
            src = cT["kc" if c == "k" else "vc"]
            return sum_of(nc, bank[0:HD, 0:2 * N_CMP].rearrange("p (g b) -> p g b", g=2),
                          [(w1[c][:, l, :], src[:, :, l:l + 16 * (N_CMP - 1) + 1:16]) for l in range(32)])

        def read(link, bank, i=i, c=c):
            act_wait()
            return nc.scalar.activation(hid[c][:].rearrange("p g b -> p (g b)"), bank[0:HD, 0:2 * N_CMP], ACT.Silu,
                                        bias=pb[:, i:i + 1])

        def act_wait():
            nc.scalar.wait_ge(*core.afree.at(2))
        jobs.append((None, fill, "a", read))
    product_block(core, jobs, loads=loads)
    jobs = [(None, lambda bank, g=g: nc.tensor.matmul(bank[g * HD:(g + 1) * HD, 0:N_CMP], w2["k"][:], hid["k"][:, g, :],
                                                      start=True, stop=True), "v",
             lambda link, bank, g=g: nc.vector.tensor_copy(kcmpT[g * HD:(g + 1) * HD, 0:N_CMP], bank[g * HD:(g + 1) * HD, 0:N_CMP]))
            for g in range(2)]
    jobs += [(None, lambda bank, g=g: nc.tensor.matmul(bank[0:N_CMP, 0:HD], hid["v"][:, g, :], w2["v"][:], start=True, stop=True),
              "v", lambda link, bank, g=g: nc.vector.tensor_copy(vcmp[0:N_CMP, g * HD:(g + 1) * HD], bank[0:N_CMP, 0:HD]))
             for g in range(2)]
    product_block(core, jobs)
    inner.close()

    inner = ExitStack()
    dist = core.sb(inner, "causal_dist", [P, BAND])
    cdist = core.sb(inner, "cmp_dist", [P, NT * 32])
    table = core.sb(inner, "bias_tables", [P, 2, BAND])
    ctable = core.sb(inner, "cmp_tables", [P, 2, NT * 32])
    with core.block() as block:
        @block.sync
        def _(sp):
            sp.dma_start(dist[:], core.const("causal_dist")).then_inc(*core.dma.up(16))
            sp.dma_start(cdist[:], core.const("cmp_dist")).then_inc(*core.dma.up(16))
            sp.wait_ge(*core.dma.at(32))
    jobs, tables = [], []
    for h in range(8):
        g, lo = h // 4, (h // 4) * HD
        rows = slice(lo, lo + HD)

        def build(link, h=h):
            link(nc.gpsimd.tensor_scalar(table[:, h % 2, :], dist[:], SLOPES[h], None, ALU.mult))
            return nc.gpsimd.tensor_scalar(ctable[:, h % 2, :], cdist[:], SLOPES[h], None, ALU.mult)
        tables.append((12 * (h - 1) if h >= 2 else 0, build))
        for t in range(NT):
            q = [qT[rows, h % 4, t * P:(t + 1) * P]]
            out = y[:, t, h * HD:(h + 1) * HD]
            jobs.append(dict(q=q, k=[kcmpT[rows, 0:N_CMP]], n=N_CMP, bias=ctable[:, h % 2, t * 32:t * 32 + N_CMP],
                             v=[(N_CMP, vcmp[0:N_CMP, rows])], dv=HD, out=out, gate=gates[:, t, 3 * h:3 * h + 1], add=False, table=h))
            for b, (kT, vv) in enumerate(((ksT, vs), (kwT, vw))):
                n = (t + 1) * P
                jobs.append(dict(q=q, k=[kT[rows, 0:n]], n=n, bias=band_of(table[:, h % 2, :], t, n),
                                 v=[(P, vv[:, c, rows]) for c in range(t + 1)], dv=HD, out=out,
                                 gate=gates[:, t, 3 * h + 1 + b:3 * h + 2 + b], add=True, table=h))
    attention(core, jobs, tables)
    inner.close()
    st.close()


def project_out(core, stream, srcT, items, dst, add):
    nc = core.nc
    jobs = []
    for half, item in enumerate(items):
        for t in range(NT):
            d = dst[:, t, half * SEQ:(half + 1) * SEQ]
            if add:
                read = lambda link, bank, d=d: nc.vector.tensor_tensor(d, d, bank[:], ALU.add)
                e = "v"
            else:
                e = "va"[t % 2]
                read = lambda link, bank, d=d, e=e: copy_on(nc, e, d, bank[:])
            jobs.append((item, token_major(core, stream, srcT, item, t, 0, SEQ), e, read))
    product_block(core, jobs, stream)


def post_norm_residual(core, x, out, gain):
    nc = core.nc
    rms_rows(core, out, NT, out)
    with core.block() as block:
        @block.vector
        def _(dve):
            link = linker(dve, core.vchain)
            for t in range(NT):
                link(nc.vector.tensor_tensor(out[:, t, :], out[:, t, :], gain, ALU.mult))
                nc.vector.tensor_tensor(x[:, t, :], x[:, t, :], out[:, t, :], ALU.add)


def mixer(core, stream, hT, y):
    nc, ins = core.nc, core.ins
    st = ExitStack()
    HD = 64
    qT = core.sb(st, "qT", [P, 4, SEQ])
    kT = core.sb(st, "kT", [P, 4, SEQ])
    v = core.sb(st, "v", [P, NT, SEQ])
    half_ones = core.sb(st, "half_ones", [P, P])
    gq = core.sb(st, "gain_q", [P, 2])
    jobs = []
    for item, dst in (("mix_q", qT), ("mix_k", kT)):
        for c in range(4):
            jobs.append((item, channel_major(core, stream, hT, item, c * P, P), "va"[c % 2],
                         lambda link, bank, dst=dst, c=c: copy_on(nc, "va"[c % 2], dst[:, c, :], bank[:])))
    for t in range(NT):
        jobs.append(("mix_v", token_major(core, stream, hT, "mix_v", t, 0, SEQ), "va"[t % 2],
                     lambda link, bank, t=t: copy_on(nc, "va"[t % 2], v[:, t, :], bank[:])))
    product_block(core, jobs, stream, loads=[(half_ones[:], core.const("half_ones")), (gq[:], ins["mix_qk_gain"])])
    with core.block() as block:
        @block.vector
        def _(dve):
            nc.vector.tensor_scalar(gq[:, 0:1], gq[:, 0:1], HD ** -0.5, None, ALU.mult)
    norm_channels(core, [[qT[:, c, :]] for c in range(4)] + [[kT[:, c, :]] for c in range(4)], half_ones[:],
                  core.eps[:, 0:1], [gq[:, 0:1]] * 4 + [gq[:, 1:2]] * 4, HD)
    inner = ExitStack()
    dist = core.sb(inner, "mix_dist", [P, BAND])
    logs = core.sb(inner, "mix_log", [P, BAND])
    table = core.sb(inner, "bias_tables", [P, 2, BAND])
    with core.block() as block:
        @block.sync
        def _(sp):
            sp.dma_start(dist[:], core.const("mix_dist")).then_inc(*core.dma.up(16))
            sp.dma_start(logs[:], core.const("mix_log")).then_inc(*core.dma.up(16))
            sp.wait_ge(*core.dma.at(32))
    jobs, tables = [], []
    for h in range(8):
        lo = (h % 2) * HD
        rows = slice(lo, lo + HD)

        def build(link, h=h):
            link(nc.gpsimd.tensor_scalar(table[:, h % 2, :], dist[:], SLOPES[h], None, ALU.mult))
            return nc.gpsimd.tensor_tensor(table[:, h % 2, :], table[:, h % 2, :], logs[:], ALU.add)
        tables.append((4 * (h - 1) if h >= 2 else 0, build))
        for t in range(NT):
            jobs.append(dict(q=[qT[rows, h // 2, t * P:(t + 1) * P]], k=[kT[rows, h // 2, :]], n=SEQ,
                             bias=band_of(table[:, h % 2, :], t, SEQ), v=[(P, v[:, c, h * HD:(h + 1) * HD]) for c in range(NT)],
                             dv=HD, out=y[:, t, h * HD:(h + 1) * HD], gate=None, add=False, table=h))
    attention(core, jobs, tables)
    inner.close()
    st.close()

    st = ExitStack()
    H = 4
    q = core.sb(st, "rqT", [HD, H, SEQ])
    k = core.sb(st, "rkT", [HD, H, SEQ])
    v = core.sb(st, "rv", [P, NT, SEQ])
    ahead = core.sb(st, "ahead", [P, BAND])
    behind = core.sb(st, "behind", [P, BAND])
    lg = core.sb(st, "log_gamma", [P, 8])
    mag = core.sb(st, "mag", [P, 8])
    gn = core.sb(st, "gn_gain", [P, SEQ])
    table = core.sb(st, "decays", [P, H, BAND])
    jobs = []
    for i, (dst, s) in enumerate(((q, 1.0), (k, HD ** -0.5))):
        for h in range(H):
            jobs.append(("mix_rqk", channel_major(core, stream, hT, "mix_rqk", i * 256 + h * HD, HD), "v",
                         lambda link, bank, dst=dst, h=h, s=s: nc.vector.tensor_scalar(dst[:, h, :], bank[0:HD, :], s, None, ALU.mult)))
    for t in range(NT):
        jobs.append(("mix_rv", token_major(core, stream, hT, "mix_rv", t, 0, SEQ), "a",
                     lambda link, bank, t=t: nc.scalar.copy(v[:, t, :], bank[:])))
    product_block(core, jobs, stream, loads=[
        (lg[:, 0:4], ins["ret_decay_f_2"].to_broadcast([P, 4])), (lg[:, 4:8], ins["ret_decay_b_2"].to_broadcast([P, 4])),
        (ahead[:], core.const("ahead")), (behind[:], core.const("behind")), (gn[:], ins["ret_gn_w_2"].to_broadcast([P, SEQ]))])
    logged, summed = core.sig("lg_logged"), core.sig("lg_tables")
    with core.block() as block:
        @block.vector
        def _(dve):
            link = linker(dve, core.vchain)
            dve.wait_ge(*logged.at(1))
            link(nc.vector.scalar_tensor_tensor(out=lg[:], in0=lg[:], scalar=0.0, in1=mag[:], op0=ALU.min, op1=ALU.subtract))
            for h in range(H):
                link(nc.vector.tensor_scalar(table[:, h, :], ahead[:], lg[:, h:h + 1], None, ALU.mult))
                nc.vector.scalar_tensor_tensor(out=table[:, h, :], in0=behind[:], scalar=lg[:, 4 + h:5 + h], in1=table[:, h, :],
                                               op0=ALU.mult, op1=ALU.add).then_inc(*summed.up())

        @block.scalar
        def _(act):
            link = linker(act, core.achain)
            link(nc.scalar.activation(mag[:], lg[:], ACT.Abs))
            link(nc.scalar.activation(mag[:], mag[:], ACT.Exp, scale=-1.0))
            nc.scalar.activation(mag[:], mag[:], ACT.Ln, bias=core.one[:, 0:1]).then_inc(*logged.up())
            for h in range(H):
                act.wait_ge(*summed.at(h + 1))
                nc.scalar.activation(table[:, h, :], table[:, h, :], ACT.Exp)
    inner = ExitStack()
    s_bank = [core.ps(inner, f"scores{b}") for b in range(4)]
    y_bank = [core.ps(inner, f"y{b}") for b in range(NT)]
    sT = core.sb(inner, "scoresT", [P, 2, NT, SEQ])
    scored, decayed, mixed, written = core.sig("ret_scored"), core.sig("ret_decayed"), core.sig("ret_mixed"), core.sig("ret_written")
    with core.block() as block:
        @block.tensor
        def _(pe):
            def scores(h):
                for t in range(NT):
                    j = h * NT + t
                    if j >= 4:
                        pe.wait_ge(*decayed.at(j - 3))
                    nc.tensor.matmul(s_bank[j % 4][:], k[:, h, t * P:(t + 1) * P], q[:, h, :], start=True, stop=True
                                     ).then_inc(*scored.up())

            def mix(h):
                pe.wait_ge(*decayed.at((h + 1) * NT))
                for i in range(NT):
                    j = h * NT + i
                    if h > 0:
                        pe.wait_ge(*written.at(j - NT + 1))
                    sum_of(nc, y_bank[i][:, 0:P], [(sT[:, h % 2, t, i * P:(i + 1) * P], v[:, t, h * P:(h + 1) * P]) for t in range(NT)]
                           ).then_inc(*mixed.up())
            scores(0)
            for h in range(H):
                if h + 1 < H:
                    scores(h + 1)
                mix(h)

        @block.vector
        def _(dve):
            for j in range(H * NT):
                h, t = j // NT, j % NT
                dve.wait_ge(*scored.at(j + 1))
                if h >= 2:
                    dve.wait_ge(*mixed.at((h - 1) * NT))
                nc.vector.tensor_tensor(sT[:, h % 2, t, :], s_bank[j % 4][:], band_of(table[:, h, :], t, SEQ), ALU.mult
                                        ).then_inc(*decayed.up())

        @block.scalar
        def _(act):
            for j in range(H * NT):
                h, i = j // NT, j % NT
                act.wait_ge(*mixed.at(j + 1))
                nc.scalar.copy(y[:, i, SEQ + h * P:SEQ + (h + 1) * P], y_bank[i][:, 0:P]).then_inc(*written.up())
    inner.close()
    ret = y[:, :, SEQ:2 * SEQ]
    mean = core.sb(st, "mean", [P, NT, H])
    with core.block() as block:
        @block.vector
        def _(dve):
            link = linker(dve, core.vchain)
            for t in range(NT):
                r = ret[:, t, :].rearrange("p (h w) -> p h w", h=H)
                link(nc.vector.tensor_reduce(mean[:, t, :], r, AX.X, ALU.add))
                link(nc.vector.tensor_scalar(mean[:, t, :], mean[:, t, :], 1.0 / P, None, ALU.mult))
                nc.vector.tensor_tensor(r, r, mean[:, t, :].unsqueeze(2).to_broadcast([P, H, P]), ALU.subtract)
    saved, core.eps = core.eps, core.gn_eps
    head_rms(core, ret, H, P, gn[:].rearrange("p (h w) -> p h w", h=H))
    core.eps = saved
    gate_with_z(core, stream, hT, "mix_rg", ret)
    st.close()


def cross_attention(core, stream, hT, memT, yT_or_y):
    nc, ins = core.nc, core.ins
    y = yT_or_y
    st = ExitStack()
    H, HD = 4, 256
    qT = core.sb(st, "qT", [P, 8, SEQ])
    kT = core.sb(st, "kT", [P, 8, N_MEM])
    v = core.sb(st, "v", [P, 2, D])
    g = core.sb(st, "gains", [P, 4])
    zero = core.sb(st, "zero", [P, N_MEM])
    jobs = []
    for half in range(2):
        for c in range(4):
            jobs.append((f"mem_q{half}", channel_major(core, stream, hT, f"mem_q{half}", c * P, P), "va"[c % 2],
                         lambda link, bank, i=half * 4 + c: copy_on(nc, "va"[i % 2], qT[:, i, :], bank[:])))
    for half in range(2):
        for c in range(4):
            jobs.append((f"mem_k{half}", channel_major(core, stream, memT, f"mem_k{half}", c * P, P, N_MEM), "va"[c % 2],
                         lambda link, bank, i=half * 4 + c: copy_on(nc, "va"[i % 2], kT[:, i, :], bank[:, 0:N_MEM])))
    for half in range(2):
        for t in range(2):
            jobs.append((f"mem_v{half}", token_major(core, stream, memT, f"mem_v{half}", t, 0, SEQ), "va"[t % 2],
                         lambda link, bank, half=half, t=t: copy_on(nc, "va"[t % 2], v[:, t, half * SEQ:(half + 1) * SEQ], bank[:])))
    product_block(core, jobs, stream, loads=[(g[:], ins["mem_qk_gain"])])
    with core.block() as block:
        @block.vector
        def _(dve):
            nc.vector.memset(zero[:], 0.0)
            nc.vector.tensor_scalar(g[:, 0:2], g[:, 0:2], HD ** -0.5, None, ALU.mult)
    norm_channels(core, [[qT[:, 2 * h, :], qT[:, 2 * h + 1, :]] for h in range(H)], core.ones, core.eps[:, 0:1],
                  [g[:, 0:1], g[:, 1:2]] * H, HD)
    norm_channels(core, [[kT[:, 2 * h, :], kT[:, 2 * h + 1, :]] for h in range(H)], core.ones, core.eps[:, 0:1],
                  [g[:, 2:3], g[:, 3:4]] * H, HD, ntok=N_MEM)
    jobs = []
    for h in range(H):
        for t in range(NT):
            jobs.append(dict(q=[qT[:, 2 * h + i, t * P:(t + 1) * P] for i in range(2)], k=[kT[:, 2 * h + i, :] for i in range(2)],
                             n=N_MEM, bias=zero[:], v=[(P, v[:, c, h * HD:(h + 1) * HD]) for c in range(2)], dv=HD,
                             out=y[:, t, h * HD:(h + 1) * HD], gate=None, add=False))
    attention(core, jobs)
    st.close()


def route(core, hT, w_route, slots, gates, over_expert, n_over):
    nc = core.nc
    st = ExitStack()
    sb = lambda n, s, dt=F32: core.sb(st, n, s, dt)
    iota = sb("iota", [P, P])
    below = sb("below", [P, P])
    glog, elog = sb("group_logits", [P, NT, 8]), sb("expert_logits", [P, NT, N_EXPERTS])
    g8, gi, e8, ei = sb("g8", [P, NT, 8]), sb("gi", [P, NT, 8], U32), sb("e8", [P, NT, 8]), sb("ei", [P, NT, 8], U32)
    gf, hot, own, part = sb("gf", [P, NT]), sb("hot", [P, NT, 4]), sb("own", [P, NT, 8]), sb("part", [P, NT, 8])
    ef = sb("ef", [P, NT, 2])
    pick = [sb(f"pick{c}", [P, NT, N_EXPERTS]) for c in range(2)]
    both = sb("both", [P, NT, N_EXPERTS])
    jobs = []
    for t in range(NT):
        def fill(bank, t=t):
            return sum_of(nc, bank[:, 0:36], [(hT[:, k, t * P:(t + 1) * P], w_route[:, k, :]) for k in range(KD)])

        def read(link, bank, t=t):
            link(nc.vector.tensor_copy(glog[:, t, 0:4], bank[:, 0:4]))
            link(nc.vector.memset(glog[:, t, 4:8], MASKED))
            return nc.vector.tensor_copy(elog[:, t, :], bank[:, 4:36])
        jobs.append((None, fill, "v", read))
    product_block(core, jobs, loads=[(iota[:], core.const("iota")), (below[:], core.const("below"))])

    bc = lambda ap, n: ap.unsqueeze(2).to_broadcast([P, NT, n])
    row = lambda a, n: iota[:, a:a + n].unsqueeze(1).to_broadcast([P, NT, n])
    diff, gsum = sb("diff", [P, NT]), sb("gsum", [P, NT])
    gexp = sb("gexp", [P, NT, 4])
    chosen, exped = core.sig("route_chosen"), core.sig("route_exped")
    with core.block() as block:
        @block.vector
        def _(dve):
            link = linker(dve, core.vchain)
            for t in range(NT):
                link(nc.vector.max(g8[:, t, :], glog[:, t, :]))
                link(nc.vector.max_index(gi[:, t, :], g8[:, t, :], glog[:, t, :]))
            link(nc.vector.tensor_copy(gf[:], gi[:, :, 0]))
            link(nc.vector.tensor_tensor(hot[:], row(0, 4), bc(gf[:], 4), ALU.is_equal))
            for g in range(N_GROUPS):
                dst = own if g == 0 else part
                link(nc.vector.tensor_tensor(dst[:], elog[:, :, 8 * g:8 * g + 8], hot[:, :, g:g + 1].to_broadcast([P, NT, 8]), ALU.mult))
                if g:
                    link(nc.vector.tensor_tensor(own[:], own[:], part[:], ALU.add))
            for t in range(NT):
                link(nc.vector.max(e8[:, t, :], own[:, t, :]))
                link(nc.vector.max_index(ei[:, t, :], e8[:, t, :], own[:, t, :]))
            link(nc.vector.tensor_tensor(diff[:], e8[:, :, 1], e8[:, :, 0], ALU.subtract))
            link(nc.vector.tensor_tensor(gexp[:], glog[:, :, 0:4], g8[:, :, 0:1].to_broadcast([P, NT, 4]), ALU.subtract))
            link(nc.vector.tensor_copy(ef[:], ei[:, :, 0:2]))
            nc.vector.tensor_scalar(gf[:], gf[:], 8.0, None, ALU.mult).then_inc(*chosen.up())
            dve.wait_ge(*chosen.at(1))
            link(nc.vector.tensor_tensor(ef[:], ef[:], bc(gf[:], 2), ALU.add))
            for c in range(2):
                link(nc.vector.tensor_tensor(pick[c][:], row(0, N_EXPERTS), ef[:, :, c:c + 1].to_broadcast([P, NT, N_EXPERTS]), ALU.is_equal))
            link(nc.vector.tensor_tensor(both[:], pick[0][:], pick[1][:], ALU.add))
            dve.wait_ge(*exped.at(1))
            link(nc.vector.tensor_reduce(gsum[:], gexp[:], AX.X, ALU.add))
            link(nc.vector.scalar_tensor_tensor(out=gsum[:], in0=diff[:], scalar=1.0, in1=gsum[:], op0=ALU.add, op1=ALU.mult))
            link(nc.vector.reciprocal(gates[:, :, 0], gsum[:]))
            nc.vector.tensor_tensor(gates[:, :, 1], gates[:, :, 0], diff[:], ALU.mult)

        @block.scalar
        def _(act):
            act.wait_ge(*chosen.at(1))
            nc.scalar.activation(diff[:], diff[:], ACT.Exp)
            nc.scalar.activation(gexp[:], gexp[:], ACT.Exp).then_inc(*exped.up())

    rank_bank, cnt_bank, base_bank = (core.ps(st, n) for n in ("ranks", "counts", "bases"))
    rank, cnt = sb("rank", [P, NT, N_EXPERTS]), sb("cnt", [N_EXPERTS, 1])
    more, over, incl = sb("more", [N_EXPERTS, 8]), sb("over", [N_EXPERTS, 1]), sb("incl", [N_EXPERTS, 1])
    past = sb("past", [N_EXPERTS, N_OVER])
    first, later = sb("first", [P, N_EXPERTS]), sb("later", [P, N_EXPERTS])
    slot = sb("slot", [P, NT, N_EXPERTS])
    fblock = sb("fblock", [1, N_OVER + 1])
    ranked, counted, based, compared, listed = (core.sig(n) for n in (
        "ranks_ready", "overflow_counted", "bases_ready", "blocks_compared", "blocks_ready"))
    E = N_EXPERTS
    with core.block() as block:
        @block.tensor
        def _(pe):
            for t in range(NT):
                sum_of(nc, rank_bank[:, t * E:(t + 1) * E],
                       [(core.ones, both[:, u, :]) for u in range(t)] + [(below[:], both[:, t, :])])
            sum_of(nc, cnt_bank[0:E, 0:1], [(both[:, t, :], core.ones[:, 0:1]) for t in range(NT)]).then_inc(*ranked.up())
            pe.wait_ge(*counted.at(1))
            nc.tensor.matmul(base_bank[:, 0:E], over[:, 0:1].to_broadcast([E, P]), below[0:E, 0:E], start=True, stop=True)
            nc.tensor.matmul(base_bank[0:E, E:E + 1], core.upto[0:E, 0:E], over[:], start=True, stop=True).then_inc(*based.up())
            pe.wait_ge(*compared.at(1))
            nc.tensor.matmul(cnt_bank[0:1, 8:8 + N_OVER], core.ones[0:E, 0:1], past[:], start=True, stop=True)
            nc.tensor.matmul(cnt_bank[0:1, 8 + N_OVER:9 + N_OVER], core.ones[0:E, 0:1], over[:], start=True, stop=True
                             ).then_inc(*listed.up())

        @block.vector
        def _(dve):
            link = linker(dve, core.vchain)
            dve.wait_ge(*ranked.at(1))
            link(nc.vector.tensor_copy(cnt[:], cnt_bank[0:E, 0:1]))
            link(nc.vector.tensor_scalar(more[:], iota[0:E, 1:9], float(SLOTS), cnt[:, 0:1], ALU.mult, ALU.is_lt))
            nc.vector.tensor_reduce(over[:], more[:], AX.X, ALU.add).then_inc(*counted.up())
            link(nc.vector.tensor_copy(rank[:].rearrange("p t e -> p (t e)"), rank_bank[:, 0:NT * E]))
            link(nc.vector.tensor_scalar(first[:], iota[:, 0:E], float(SLOTS), None, ALU.mult))
            dve.wait_ge(*based.at(1))
            link(nc.vector.tensor_copy(incl[:], base_bank[0:E, E:E + 1]))
            nc.vector.tensor_scalar(past[:], iota[0:E, 0:N_OVER], incl[:, 0:1], None, ALU.is_ge).then_inc(*compared.up())
            link(nc.vector.tensor_scalar(later[:], base_bank[:, 0:E], float(SLOTS), float(SLOTS * (E - 1)), ALU.mult, ALU.add))
            link(nc.vector.tensor_tensor(first[:], first[:], later[:], ALU.subtract))
            link(nc.vector.tensor_scalar(slot[:], rank[:], float(SLOTS), None, ALU.is_lt))
            link(nc.vector.tensor_tensor(slot[:], slot[:], first[:].unsqueeze(1).to_broadcast([P, NT, E]), ALU.mult))
            link(nc.vector.tensor_tensor(slot[:], slot[:], later[:].unsqueeze(1).to_broadcast([P, NT, E]), ALU.add))
            link(nc.vector.tensor_tensor(slot[:], slot[:], rank[:], ALU.add))
            for c in range(2):
                link(nc.vector.tensor_tensor(pick[c][:], pick[c][:], slot[:], ALU.mult))
                link(nc.vector.tensor_reduce(slots[:, :, c], pick[c][:], AX.X, ALU.add))
            dve.wait_ge(*listed.at(1))
            link(nc.vector.tensor_scalar(fblock[:], cnt_bank[0:1, 8:9 + N_OVER], float(E - 1), None, ALU.min))
            nc.vector.tensor_copy(over_expert[:], fblock[:])
    st.close()


def moe(core, x, gain):
    nc, ins = core.nc, core.ins
    st = ExitStack()
    xn = core.sb(st, "xn", [P, NT, D])
    slots = core.sb(st, "slots", [P, NT, 2])
    slot_rows = core.sb(st, "slot_rows", [P, NT, 2], U32)
    gates = core.sb(st, "gates", [P, NT, 2])
    over = core.sb(st, "over_expert", [1, N_OVER + 1], I32)
    expert_rows = nc.dram_tensor("expert_rows", (N_BLOCKS * SLOTS, D), F32).ap()
    w = {"gate": ins["w_exp_gate_2"][0].rearrange("e (k p) n -> e p k n", p=P),
         "up": ins["w_exp_up_2"][0].rearrange("e (k p) n -> e p k n", p=P),
         "down": ins["w_exp_down_2"][0].rearrange("e (k p) n -> e p k n", p=P)}
    kinds = ("gate", "up", "down")
    ring = {(kind, b): core.sb(st, f"{kind}{b}", [P, 4096]) for b in range(2) for kind in kinds}
    view = {(kind, b): ring[kind, b][:].rearrange("p (k n) -> p k n", k=(KD if kind != "down" else 4))
            for b in range(2) for kind in kinds}
    landed = {(kind, b): core.sig(f"expert_{kind}{b}_landed") for b in range(2) for kind in kinds}
    zero = core.sb(st, "zero_rows", [P, D])
    cleared, cleared_dma = core.sig("zero_rows_cleared"), core.sig("overflow_rows_zeroed")
    with core.block() as block:
        @block.vector
        def _(dve):
            nc.vector.memset(zero[:], 0.0).then_inc(*cleared.up())

        @block.sync
        def _(sp):
            sp.wait_ge(*cleared.at(1))
            for r in range(N_EXPERTS * SLOTS, N_BLOCKS * SLOTS, P):
                sp.dma_start(expert_rows[r:r + P, :], zero[:]).then_inc(*cleared_dma.up(16))
            for e in range(2):
                for kind in kinds:
                    sp.dma_start(view[kind, e], w[kind][e]).then_inc(landed[kind, e].sem, 16)
    inner = ExitStack()
    hT = core.sb(inner, "hT", [P, KD, SEQ])
    w_route = core.sb(inner, "w_route", [P, KD, 36])
    norm_to_channels(core, x, NT, gain, hT, keep=xn)
    with core.block() as block:
        @block.sync
        def _(sp):
            sp.dma_start(w_route[:, :, 0:4], ins["w_group_2"][0].rearrange("(k p) n -> p k n", p=P)).then_inc(*core.dma.up(16))
            sp.dma_start(w_route[:, :, 4:36], ins["w_router_2"].rearrange("(k p) n -> p k n", p=P)).then_inc(*core.dma.up(16))
            sp.wait_ge(*core.dma.at(32))
    route(core, hT, w_route, slots, gates, over, None)
    inner.close()

    inner = ExitStack()
    sb = lambda n, s, dt=F32: core.sb(inner, n, s, dt)
    HB = SLOTS
    top_half, low_half = slice(0, HB), slice(HB, P)
    halves = (top_half, low_half)
    iota = sb("iota", [P, P])
    landed_mark = sb("landed_mark", [1, 1])
    rel = sb("slot_in_block", [P, NT, 2])
    pick = [[sb(f"pick{b}_{c}", [P, NT, SLOTS]) for c in range(2)] for b in range(2)]
    picked_rows = [sb(f"picked_rows{b}", [P, SEQ]) for b in range(2)]
    xT = [sb(f"xT{b}", [P, KD, SLOTS]) for b in range(2)]
    silu_up = [sb(f"silu{b}", [P, FF]) for b in range(2)]
    inner_act = [sb(f"gated{b}", [P, FF]) for b in range(2)]
    actT = [sb(f"actT{b}", [P, 4, SLOTS]) for b in range(2)]
    rows = [sb(f"rows{b}", [P, SEQ]) for b in range(2)]
    pick_bank = [core.ps(inner, f"picked{b}") for b in range(2)]
    h_bank = [core.ps(inner, f"h{b}") for b in range(2)]
    y_bank = [core.ps(inner, f"y{b}") for b in range(2)]
    xT_bank = core.ps(inner, "xT_turned")
    actT_bank = core.ps(inner, "act_turned")
    names = ("moe_picked", "moe_gathered", "moe_rows_kept", "moe_rows_turned", "moe_tokens", "moe_hidden", "moe_silu",
             "moe_gated", "moe_act_turned", "moe_act_kept", "moe_rows", "moe_rows_read")
    pick_step = core.sig("moe_pick_step")
    all_signals = [core.sig(n) for n in names]
    picked, gathered, kept, turned, tokens, hidden, silu, gated, act_turned, act_kept, rows_s, read_s = all_signals
    stored = [core.sig(f"moe_rows_stored{b}") for b in range(2)]
    with core.block() as block:
        @block.sync
        def _(sp):
            sp.dma_start(iota[:], core.const("iota")).then_inc(*core.dma.up(16))
            sp.wait_ge(*core.dma.at(16))

        @block.vector
        def _(dve):
            nc.vector.tensor_scalar(rel[:], slots[:], float(SLOTS), None, ALU.add)
            for s in all_signals:
                dve.sem_inc(s.sem, 1)
            for s in stored:
                dve.sem_inc(s.sem, 32)
            nc.vector.tensor_copy(slot_rows[:], slots[:])
            for act_rows in inner_act:
                nc.vector.memset(act_rows[:], 0.0)

    def count(j, per, more):
        i, c = j
        return i * (2 * per) + (c * per + more)

    def passed(eng, signal, j, back=0):
        eng.wait_ge(signal.sem, count(j, 1, 2 - back))

    def load(sp, j, b, expert):
        for kind in kinds:
            passed(sp, rows_s if kind == "down" else hidden, j, 2)
            sp.dma_start(view[kind, b], w[kind][expert].rearrange("e p k n -> (e p) k n")).then_inc(landed[kind, b].sem, 16)

    def gather(pe, j, b, first=False):
        passed(pe, picked, j)
        if not first:
            passed(pe, kept, j, 2)
        for t in range(NT):
            for h, half in enumerate(halves):
                last = nc.tensor.matmul(pick_bank[b][half, :], pick[b][0][:, t, :], xn[:, t, h * SEQ:(h + 1) * SEQ],
                                        start=(t == 0), stop=(t == NT - 1))
        last.then_inc(gathered.sem, 1)

    def turn_rows(pe, j, b, first=False):
        passed(pe, kept, j)
        if not first:
            passed(pe, tokens, j, 1)
        for c in range(KD // 2):
            last = nc.tensor.transpose(xT_bank[:, c * P:(c + 1) * P], picked_rows[b][:, c * P:(c + 1) * P], core.ident)
        last.then_inc(turned.sem, 1)

    def expand(pe, j, b, uses, first=False):
        passed(pe, tokens, j)
        if not first:
            passed(pe, gated, j, 2)
        for kind in ("gate", "up"):
            pe.wait_ge(landed[kind, b].sem, uses * 16)
        for k in range(KD):
            for kind, half in (("gate", top_half), ("up", low_half)):
                last = nc.tensor.matmul(h_bank[b][half, :], xT[b][:, k, :], view[kind, b][:, k, :],
                                        start=(k == 0), stop=(k == KD - 1))
        last.then_inc(hidden.sem, 1)

    def turn_act(pe, j, b, first=False):
        passed(pe, gated, j)
        if not first:
            passed(pe, act_kept, j, 1)
        for f in range(4):
            last = nc.tensor.transpose(actT_bank[:, f * P:(f + 1) * P], inner_act[b][:, f * P:(f + 1) * P], core.ident)
        last.then_inc(act_turned.sem, 1)

    def contract(pe, j, b, uses, first=False):
        passed(pe, act_kept, j)
        if not first:
            passed(pe, read_s, j, 2)
        pe.wait_ge(landed["down", b].sem, uses * 16)
        for f in range(4):
            for h, half in enumerate(halves):
                last = nc.tensor.matmul(y_bank[b][half, :], actT[b][:, f, :], view["down", b][:, f, h * SEQ:(h + 1) * SEQ],
                                        start=(f == 0), stop=(f == 3))
        last.then_inc(rows_s.sem, 1)

    def pick_tokens(dve, j, b, first=False):
        nc.vector.tensor_scalar(rel[:], rel[:], -float(SLOTS), None, ALU.add).then_inc(pick_step.sem, 1)
        dve.wait_ge(pick_step.sem, count(j, 3, 1))
        if not first:
            passed(dve, gathered, j, 2)
        for c in range(2):
            nc.vector.tensor_tensor(pick[b][c][:], iota[:, 0:SLOTS].unsqueeze(1).to_broadcast([P, NT, SLOTS]),
                                    rel[:, :, c:c + 1].to_broadcast([P, NT, SLOTS]), ALU.is_equal).then_inc(pick_step.sem, 1)
        dve.wait_ge(pick_step.sem, count(j, 3, 3))
        nc.vector.tensor_tensor(pick[b][0][:], pick[b][0][:], pick[b][1][:], ALU.add).then_inc(picked.sem, 1)

    def take_tokens(dve, j, b, first=False):
        passed(dve, turned, j)
        if not first:
            passed(dve, hidden, j, 2)
        nc.vector.tensor_tensor(xT[b][:].rearrange("p (h c) s -> p h c s", h=2),
                                xT_bank[:].rearrange("p (c h s) -> p h c s", c=4, h=2),
                                gain.rearrange("p (h c) -> p h c", h=2).unsqueeze(3).to_broadcast([P, 2, 4, SLOTS]),
                                ALU.mult).then_inc(tokens.sem, 1)

    def gate_hidden(dve, j, b, first=False):
        passed(dve, silu, j)
        if not first:
            passed(dve, act_turned, j, 2)
        nc.vector.tensor_tensor(inner_act[b][low_half, :], silu_up[b][low_half, :], h_bank[b][low_half, :], ALU.mult
                                ).then_inc(gated.sem, 1)

    def keep_rows(act, j, b, first=False):
        passed(act, gathered, j)
        if not first:
            passed(act, turned, j, 2)
        nc.scalar.copy(picked_rows[b][:], pick_bank[b][:]).then_inc(kept.sem, 1)

    def take_silu(act, j, b, first=False):
        passed(act, hidden, j)
        if not first:
            passed(act, gated, j, 2)
        nc.scalar.activation(silu_up[b][low_half, :], h_bank[b][top_half, :], ACT.Silu).then_inc(silu.sem, 1)

    def keep_act(act, j, b, first=False):
        passed(act, act_turned, j)
        if not first:
            passed(act, rows_s, j, 2)
        nc.scalar.copy(actT[b][:], actT_bank[:].rearrange("p (f h s) -> p f h s", f=4, h=2)[:, :, 1, :]).then_inc(act_kept.sem, 1)

    def store_rows(act, j, b, uses):
        passed(act, rows_s, j)
        act.wait_ge(stored[b].sem, uses * 32)
        nc.scalar.copy(rows[b][:], y_bank[b][:]).then_inc(read_s.sem, 1)
        passed(act, read_s, j)
        for h, half in enumerate(halves):
            act.dma_start(expert_rows[bass.ds(count(j, SLOTS, 0), SLOTS), h * SEQ:(h + 1) * SEQ], rows[b][half, :]
                          ).then_inc(stored[b].sem, 16)

    PAIRS = N_EXPERTS // 2
    END = (0, N_EXPERTS - 1)
    with core.block() as block:
        @block.sync
        def _(sp):
            with sp.Fori(0, PAIRS - 1) as i:
                for b in range(2):
                    load(sp, (i, 2 + b), b, bass.ds(i * 2 + 2 + b, 1))

        @block.tensor
        def _(pe):
            gather(pe, (0, 0), 0, True)
            turn_rows(pe, (0, 0), 0, True)
            gather(pe, (0, 1), 1, True)
            expand(pe, (0, 0), 0, 1, True)
            turn_rows(pe, (0, 1), 1)
            turn_act(pe, (0, 0), 0, True)
            with pe.Fori(0, PAIRS - 1) as i:
                for b, ahead in ((1, 0), (0, 1)):
                    j, before, after = (i, 1 + ahead), (i, ahead), (i, 2 + ahead)
                    gather(pe, after, 1 - b)
                    contract(pe, before, 1 - b, i + 1)
                    expand(pe, j, b, i + 1 + ahead)
                    turn_rows(pe, after, 1 - b)
                    turn_act(pe, j, b)
            contract(pe, (0, N_EXPERTS - 2), 0, PAIRS)
            expand(pe, END, 1, PAIRS)
            turn_act(pe, END, 1)
            contract(pe, END, 1, PAIRS)

        @block.vector
        def _(dve):
            pick_tokens(dve, (0, 0), 0, True)
            pick_tokens(dve, (0, 1), 1, True)
            take_tokens(dve, (0, 0), 0, True)
            pick_tokens(dve, (0, 2), 0)
            gate_hidden(dve, (0, 0), 0, True)
            take_tokens(dve, (0, 1), 1, True)
            with dve.Fori(0, PAIRS - 1) as i:
                for b, ahead in ((1, 0), (0, 1)):
                    j, after, later = (i, 1 + ahead), (i, 2 + ahead), (i, 3 + ahead)
                    pick_tokens(dve, later, b)
                    gate_hidden(dve, j, b)
                    take_tokens(dve, after, 1 - b)
            gate_hidden(dve, END, 1)

        @block.scalar
        def _(act):
            keep_rows(act, (0, 0), 0, True)
            keep_rows(act, (0, 1), 1, True)
            take_silu(act, (0, 0), 0, True)
            keep_act(act, (0, 0), 0, True)
            with act.Fori(0, PAIRS - 1) as i:
                for b, ahead in ((1, 0), (0, 1)):
                    j, before, after = (i, 1 + ahead), (i, ahead), (i, 2 + ahead)
                    keep_rows(act, after, 1 - b)
                    store_rows(act, before, 1 - b, i + 1)
                    take_silu(act, j, b)
                    keep_act(act, j, b)
            store_rows(act, (0, N_EXPERTS - 2), 0, PAIRS)
            take_silu(act, END, 1)
            keep_act(act, END, 1)
            store_rows(act, END, 1, PAIRS)
            for b in range(2):
                act.wait_ge(stored[b].sem, 32 * (PAIRS + 1))

    def overflow(eng, body):
        n_over = eng.value_load(over[0:1, N_OVER:N_OVER + 1], min_val=0, max_val=N_OVER)
        with eng.Fori(0, N_OVER // 2) as i:
            with eng.If(i * 2 < n_over):
                for b in range(2):
                    body(i, (i, N_EXPERTS + b), b)

    with core.block() as block:
        @block.sync
        def _(sp):
            def body(i, j, b):
                expert = sp.value_load(over[0:1, bass.ds(i * 2 + b, 1)], min_val=0, max_val=N_EXPERTS - 1)
                load(sp, j, b, bass.ds(expert, 1))
            overflow(sp, body)

        @block.tensor
        def _(pe):
            def body(i, j, b):
                gather(pe, j, b)
                turn_rows(pe, j, b)
                expand(pe, j, b, i + PAIRS + 1)
                turn_act(pe, j, b)
                contract(pe, j, b, i + PAIRS + 1)
            overflow(pe, body)

        @block.vector
        def _(dve):
            def body(i, j, b):
                pick_tokens(dve, (i, N_EXPERTS + b + 1), 1 - b)
                take_tokens(dve, j, b)
                gate_hidden(dve, j, b)
            overflow(dve, body)

        @block.scalar
        def _(act):
            act.wait_ge(*cleared_dma.now())

            def body(i, j, b):
                keep_rows(act, j, b)
                take_silu(act, j, b)
                keep_act(act, j, b)
                store_rows(act, j, b, i + PAIRS + 1)
                act.wait_ge(stored[b].sem, (i + PAIRS + 2) * 32)
                if b == 1:
                    nc.scalar.copy(landed_mark[:], iota[0:1, 0:1])
            overflow(act, body)
    inner.close()

    inner = ExitStack()
    got = [core.sb(inner, f"got{b}", [P, D]) for b in range(2 * NT)]
    fetched, added = core.sig("expert_rows_fetched"), core.sig("expert_rows_added")
    with core.block() as block:
        @block.gpsimd
        def _(pool):
            for t in range(NT):
                for c in range(2):
                    pool.indirect_dma_start(got[2 * t + c][:], None, expert_rows,
                                            bass.IndirectOffsetOnAxis(ap=slot_rows[:, t, c:c + 1], axis=0)
                                            ).then_inc(*fetched.up(16))

        @block.vector
        def _(dve):
            dve.wait_ge(*fetched.at(16 * 2 * NT))
            for t in range(NT):
                for c in range(2):
                    nc.vector.scalar_tensor_tensor(out=x[:, t, :], in0=got[2 * t + c][:], scalar=gates[:, t, c:c + 1],
                                                   in1=x[:, t, :], op0=ALU.mult, op1=ALU.add).then_inc(*added.up())
                    dve.wait_ge(*added.at(2 * t + c + 1))
    inner.close()
    st.close()


def build_program(nc, ins, out, dbg=None, upto=99):
    core = Core(nc, ins, out, dbg)
    core.const_at = CONST_AT
    top = ExitStack()
    ident = core.sb(top, "ident", [P, P])
    ones = core.sb(top, "ones", [P, P])
    upto_m = core.sb(top, "upto", [P, P])
    eps = core.sb(top, "eps", [P, 1])
    gn_eps = core.sb(top, "gn_eps", [P, 1])
    one = core.sb(top, "one", [P, 1])
    core.ident, core.ones, core.upto, core.eps, core.gn_eps, core.one = ident[:], ones[:], upto_m[:], eps, gn_eps, one
    gains = core.sb(top, "norm_gains", [P, 5, KD])
    x = core.sb(top, "x", [P, NT, D])

    w_in = ins["w_in"][0].rearrange("(k p) n -> p k n", p=P)
    w_in_2 = ins["w_in_2"][0].rearrange("(k p) n -> p k n", p=P)

    def cols(name, at, n, src=w_in):
        return (name, src[:, :, at:at + n], KD, n)

    def merge_items(n):
        return [cols(f"merge{n}_{h}", AT["merge_gate"] + n * D + h * SEQ, SEQ) for h in range(2)] + \
            [(f"w_br{n}", ins["w_br"][0, n].rearrange("(k p) n -> p k n", p=P), 4, D)]

    def halves(name, src, base=0):
        w = src.rearrange("(k p) n -> p k n", p=P)
        return [cols(f"{name}{h}", base + h * SEQ, SEQ, w) for h in range(2)]

    items = [cols(f"gdn_{c}", AT[f"gdn_{c}"], 512) for c in "qkvz"] + merge_items(0)
    items += [cols("gla_qk", AT["gla_q"], 512), cols("gla_v", AT["gla_v"], 512), cols("gla_z", AT["gla_z"], 512)] + merge_items(1)
    items += [cols("ssd_x", AT["ssd_x"], 512), cols("ssd_bc", AT["ssd_b"], 512), cols("ssd_z", AT["ssd_z"], 512)] + merge_items(2)
    items += [cols("nsa_q", AT["nsa_q"], 512), cols("nsa_kv", AT["nsa_kc"], 512), cols("nsa_w", AT["nsa_kw"], 256),
              cols("nsa_z", AT["nsa_z"], 512)] + merge_items(3)
    items += halves("w_out", ins["w_out"][0])
    for n, name in enumerate(("mix_q", "mix_k", "mix_v", "mix_rqk", "mix_rv", "mix_rg")):
        items.append(cols(name, 512 * n, 512, w_in_2))
    items += halves("w_out_2", ins["w_out_2"][0])
    items += halves("mem_q", ins["w_mq_2"][0]) + halves("mem_k", ins["w_mkv_2"][0]) + halves("mem_v", ins["w_mkv_2"][0], D)
    items += halves("mem_o", ins["w_mo_2"][0])

    def dump(name, ap):
        if name in core.dbg:
            with core.block() as block:
                @block.sync
                def _(sp):
                    sp.dma_start(core.dbg[name], ap).then_inc(*core.dma.up(16))
                    sp.wait_ge(*core.dma.at(16))

    xin = ins["x"][0].rearrange("(t p) d -> p t d", p=P)
    body = ExitStack()
    stream = Stream(core, body, 4, items)
    with core.block() as block:
        @block.sync
        def _(sp):
            loads = [(x[:], xin), (ident[:], core.const("ident")), (ones[:], core.const("ones")),
                     (upto_m[:], core.const("upto")), (gains[:], ins["norm_gains"])]
            for dst, src in loads:
                sp.dma_start(dst, src).then_inc(*core.dma.up(16))
            for _ in range(stream.slots):
                stream.load(sp)
            sp.wait_ge(*core.dma.at(16 * len(loads)))

        @block.vector
        def _(dve):
            nc.vector.memset(eps[:], EPS)
            nc.vector.memset(gn_eps[:], GN_EPS)
            nc.vector.memset(one[:], 1.0)

    b1 = ExitStack()
    hT = core.sb(b1, "hT", [P, KD, SEQ])
    norm_to_channels(core, x, NT, gains[:, 0, :], hT)
    dump("hT", hT[:])
    merged = core.sb(b1, "merged", [P, NT, D])
    dec = {n: core.sb(b1, n, [P, NT, w]) for n, w in (("rate", 12), ("dt", 12), ("cum", 12), ("e_cum", 12),
                                                      ("e_rest", 12), ("e_total", 12), ("beta", 4), ("gates", 24))}
    gkT = core.sb(b1, "gkT", [16, SEQ])
    inner = ExitStack()
    small = core.sb(inner, "small", [P, NT, 40])
    w_small = core.sb(inner, "w_small", [P, KD, 56])
    head_par = core.sb(inner, "head_par", [P, 24])
    with core.block() as block:
        @block.sync
        def _(sp):
            loads = [(w_small[:, :, a:a + n], w_in[:, :, AT[c]:AT[c] + n]) for a, n, c in (
                (0, 8, "gdn_beta"), (8, 8, "ssd_dt"), (16, 24, "nsa_gate"), (40, 16, "gla_gk"))]
            loads += [(head_par[:, a:a + n], ins[c].to_broadcast([P, n])) for a, n, c in (
                (0, 4, "a_log_a"), (4, 8, "a_log_c"), (12, 4, "dt_bias_a"), (16, 8, "dt_bias_c"))]
            for dst, src in loads:
                sp.dma_start(dst, src).then_inc(*core.dma.up(16))
            sp.wait_ge(*core.dma.at(16 * len(loads)))
    small_products(core, stream, hT, w_small, small, gkT)
    decay_rates(core, small, head_par, dec["rate"], dec["dt"], dec["gates"], dec["beta"])
    decay_sums(core, dec["rate"], core.upto, dec["cum"], dec["e_cum"], dec["e_rest"], dec["e_total"])
    inner.close()
    dump("rate", dec["rate"][:])

    def finish_branch(n, y, head_norm, z, order):
        st = ExitStack()
        gain = core.sb(st, "gain", [P, SEQ])
        heads, width, src = head_norm
        if heads:
            with core.block() as block:
                @block.sync
                def _(sp):
                    sp.dma_start(gain[:, 0:width], src.to_broadcast([P, width])).then_inc(*core.dma.up(16))
                    sp.wait_ge(*core.dma.at(16))
        for step in order:
            if step == "norm":
                head_rms(core, y, heads, width, gain[:, 0:width])
            else:
                gate_with_z(core, stream, hT, z, y)
        dump(f"y{n}", y[:])
        st.close()
        st = ExitStack()
        yT = core.sb(st, "yT", [P, 4, SEQ])
        to_channels(core, y, yT, 4)
        merge_branch(core, stream, hT, yT, n, merged)
        st.close()

    branches = (
        (lambda y: gdn(core, stream, hT, dec, y), (4, P, ins["onorm_a"]), "gdn_z", ("norm", "gate")),
        (lambda y: gla(core, stream, hT, gkT, y), (4, P, ins["onorm_b"]), "gla_z", ("norm", "gate")),
        (lambda y: ssd(core, stream, hT, dec, y), (1, SEQ, ins["onorm_c"]), "ssd_z", ("gate", "norm")),
        (lambda y: nsa(core, stream, hT, dec["gates"], y), (0, 0, None), "nsa_z", ("gate",)),
    )
    for n, (run, norm, z, order) in enumerate(branches):
        if n >= upto:
            break
        st = ExitStack()
        y = core.sb(st, "y", [P, NT, SEQ])
        run(y)
        dump(f"raw{n}", y[:])
        finish_branch(n, y, norm, z, order)
        st.close()
    dump("merged", merged[:])
    if upto < 5:
        return finish_program(core, top, body, b1, x)
    inner = ExitStack()
    gain = core.sb(inner, "gain", [P, D])
    to_channels(core, merged, hT, KD)
    project_out(core, stream, hT, ("w_out0", "w_out1"), merged, False)
    with core.block() as block:
        @block.sync
        def _(sp):
            sp.dma_start(gain[:], ins["norm_post"].to_broadcast([P, D])).then_inc(*core.dma.up(16))
            sp.wait_ge(*core.dma.at(16))
    post_norm_residual(core, x, merged, gain[:])
    inner.close()
    dump("x1", x[:])
    b1.close()
    if upto < 6:
        return finish_program(core, top, body, b1, x)

    b2 = ExitStack()
    hT = core.sb(b2, "hT", [P, KD, SEQ])
    y = core.sb(b2, "y", [P, NT, D])
    norm_to_channels(core, x, NT, gains[:, 1, :], hT)
    mixer(core, stream, hT, y)
    dump("mix", y[:])
    to_channels(core, y, hT, KD)
    project_out(core, stream, hT, ("w_out_20", "w_out_21"), x, True)
    dump("x2", x[:])
    norm_to_channels(core, x, NT, gains[:, 2, :], hT)
    inner = ExitStack()
    memT = core.sb(inner, "memT", [P, KD, N_MEM])
    mem = core.sb(inner, "mem", [P, 2, D])
    with core.block() as block:
        @block.sync
        def _(sp):
            sp.dma_start(mem[:], ins["mem_2"][0].rearrange("(t p) d -> p t d", p=P)).then_inc(*core.dma.up(16))
            sp.wait_ge(*core.dma.at(16))
    norm_to_channels(core, mem, 2, gains[:, 3, :], memT)
    cross_attention(core, stream, hT, memT, y)
    inner.close()
    to_channels(core, y, hT, KD)
    project_out(core, stream, hT, ("mem_o0", "mem_o1"), x, True)
    dump("x3", x[:])
    b2.close()
    body.close()
    if upto < 7:
        return finish_program(core, top, body, b2, x)
    moe(core, x, gains[:, 4, :])
    return finish_program(core, top, body, b2, x)


def finish_program(core, top, body, b, x):
    with core.block() as block:
        @block.sync
        def _(sp):
            sp.dma_start(core.out[0].rearrange("(t p) d -> p t d", p=P), x[:]).then_inc(*core.stored.up(16))
            sp.wait_ge(*core.stored.at(16))


CONST_AT, CONSTANTS = shape_constants()


def lay_out(inputs):
    a = {k: np.ascontiguousarray(v) for k, v in inputs.items()}
    by_channel = lambda v: np.ascontiguousarray(v.reshape(-1, P).T)
    for name in ("conv_a", "conv_c"):
        w = a[name][0]
        a[name] = np.ascontiguousarray(w.T.reshape(-1, P, w.shape[0]).transpose(1, 0, 2))
    a["conv_bias_c"] = by_channel(a["conv_bias_c"])
    a["norm_gains"] = np.ascontiguousarray(np.stack([by_channel(a.pop(n)) for n in (
        "norm_pre", "norm_mix_w_2", "norm_mem_w_2", "norm_memkv_w_2", "norm_moe_w_2")], axis=1))
    q, k = a.pop("attn_q_norm_w_2")[0], a.pop("attn_k_norm_w_2")[0]
    a["mix_qk_gain"] = np.ascontiguousarray(np.stack([np.concatenate([q, q]), np.concatenate([k, k])], axis=1))
    q, k = a.pop("mem_q_norm_w_2")[0], a.pop("mem_k_norm_w_2")[0]
    a["mem_qk_gain"] = np.ascontiguousarray(np.stack([q[:P], q[P:], k[:P], k[P:]], axis=1))
    for c in "kv":
        a[f"w_c{c}1"] = np.ascontiguousarray(a[f"w_c{c}1"][0].reshape(32, 64, 64).transpose(1, 0, 2))
        a[f"cmp_pos_{c}"] = np.ascontiguousarray(a[f"cmp_pos_{c}"][0].T)
    a["w_router_2"] = np.ascontiguousarray(a["w_router_2"][0].transpose(1, 0, 2).reshape(D, N_EXPERTS))
    q = slice(AT["nsa_q"], AT["nsa_q"] + 512)
    w = a["w_in"].copy()
    w[..., q] = w[..., q].reshape(1, D, 2, 4, 64).transpose(0, 1, 3, 2, 4).reshape(1, D, 512)
    a["w_in"] = w
    a["shape_constants"] = CONSTANTS
    return a


def kernel(**inputs):
    import concourse.bacc as bacc
    from concourse.bass_utils import run_bass_kernel_spmd as run

    nc = bacc.Bacc("TRN2", target_bir_lowering=False, num_devices=1)
    arrays = lay_out(inputs)
    ins = {n: nc.dram_tensor(n, a.shape, mybir.dt.from_np(a.dtype), kind="ExternalInput").ap() for n, a in arrays.items()}
    out = nc.dram_tensor("out", (1, SEQ, D), F32, kind="ExternalOutput").ap()
    build_program(nc, ins, out)
    return run(nc, [arrays], core_ids=[0]).results[0]["out"]
```

```python
from contextlib import ExitStack

import numpy as np

import concourse.bass as bass
from concourse import mybir

F32 = mybir.dt.float32
F32R = mybir.dt.float32r
I32 = mybir.dt.int32
U32 = mybir.dt.uint32
ALU = mybir.AluOpType
ACT = mybir.ActivationFunctionType
AX = mybir.AxisListType

P = 128
D = 1024
KD = D // P
SEQ = 512
NT = SEQ // P
PIECES = 8
EPS = 1e-6
GN_EPS = 1e-5
MASKED = -1e30
ALIBI_HEADS = 8

W_IN_COLS = (
    ("gdn_q", 512), ("gdn_k", 512), ("gdn_v", 512), ("gdn_beta", 4), ("gdn_a", 4), ("gdn_z", 512),
    ("gla_q", 256), ("gla_k", 256), ("gla_v", 512), ("gla_gk", 16), ("gla_z", 512),
    ("ssd_x", 512), ("ssd_b", 256), ("ssd_c", 256), ("ssd_dt", 8), ("ssd_z", 512),
    ("nsa_q", 512), ("nsa_kc", 128), ("nsa_vc", 128), ("nsa_ks", 128), ("nsa_vs", 128),
    ("nsa_kw", 128), ("nsa_vw", 128), ("nsa_gate", 24), ("nsa_z", 512), ("merge_gate", 4096),
)
AT = {}
_at = 0
for _name, _width in W_IN_COLS:
    AT[_name] = _at
    _at += _width
D_IN = _at

N_MEM = 256
N_EXPERTS = 32
N_GROUPS = 4
FF = 512
SLOTS = 64
N_OVER = -(-((2 * SEQ - N_EXPERTS) // SLOTS) // 2) * 2
N_BLOCKS = N_EXPERTS + N_OVER
N_CMP = 31

SLOPES = [2.0 ** (-8.0 * (h + 1) / ALIBI_HEADS) for h in range(ALIBI_HEADS)]
BAND = SEQ + (NT - 1) * P


def shape_constants():
    p = np.arange(P)[:, None].astype(np.float64)
    c = np.arange(P)[None, :].astype(np.float64)
    band = np.arange(BAND)[None, :]
    t = {}
    t["ident"] = p == c
    t["ones"] = np.ones((P, P))
    t["upto"] = p <= c
    t["below"] = p < c
    t["half_ones"] = (p // 64) == (c // 64)
    t["strict_bias"] = np.where(c < p, 0.0, MASKED)
    t["causal_biasT"] = np.where(p <= c, 0.0, MASKED)
    for lvl in range(7):
        b = 2**lvl
        t[f"level{lvl}"] = ((p // (2 * b)) == (c // (2 * b))) & ((p // b) % 2 == 1) & ((c // b) % 2 == 0)
    same = (p // 64) == (c // 64)
    within = same & (p <= c)
    mid = same & ((p % 64) <= 32)
    t["gla_from_mid"] = within.astype(float) - mid
    t["gla_within"] = within
    t["gla_to_half_end"] = same.astype(float) - within
    t["gla_to_end"] = 1.0 - (p <= c)
    t["gla_near"] = within
    t["gla_far"] = (p < 64) & (c >= 64)
    dist = p + (NT - 1) * P - band
    t["causal_dist"] = np.where(dist >= 0, dist, -MASKED)
    a = np.abs(dist)
    count = (a <= 64) * 1.0 + ((a % 4 == 0) & (a <= 256)) + (a % 16 == 0)
    t["mix_dist"] = a
    t["mix_log"] = np.where(count > 0, -np.log(np.maximum(count, 1)), -MASKED)
    t["ahead"] = np.maximum((band - (NT - 1) * P) - p, 0)
    t["behind"] = np.maximum(p - (band - (NT - 1) * P), 0)
    cmp_pos = np.arange(32)[None, None, :] * 16 + 31
    tok = np.arange(P)[:, None, None] + P * np.arange(NT)[None, :, None]
    cmp = np.where((cmp_pos <= tok) & (np.arange(32) < N_CMP), tok - cmp_pos, -MASKED)
    t["cmp_dist"] = cmp.reshape(P, NT * 32)
    t["iota"] = c + 0 * p
    names = {}
    at = 0
    cols = []
    for k, v in t.items():
        v = np.broadcast_to(np.asarray(v, np.float64), (P, v.shape[1])).astype(np.float32)
        names[k] = (at, v.shape[1])
        at += v.shape[1]
        cols.append(v)
    return names, np.ascontiguousarray(np.concatenate(cols, axis=1))


class Signal:

    def __init__(self, sem):
        self.sem, self.n, self.base = sem, 0, 0

    def up(self, by=1):
        self.n += by
        return self.sem, by

    def at(self, k):
        return self.sem, self.base + k

    def now(self):
        return self.sem, self.n


class Core:

    def __init__(self, nc, ins, out):
        self.nc, self.ins, self.out = nc, ins, out
        self.stack = ExitStack()
        self.counters = []
        self.names = {}
        n = self.new_counter
        self.dma = n("loads_landed")
        self.stored = n("stores_landed")
        self.vchain = n("vector_step")
        self.achain = n("scalar_step")
        self.gchain = n("gpsimd_step")
        self.ready = n("product_ready")
        self.vfree = n("bank_read_by_vector")
        self.afree = n("bank_read_by_scalar")
        self.rounded = n("weights_rounded")
        self.split = n("weights_split")
        self.uid = 0

    def new_counter(self, name):
        s = Signal(self.stack.enter_context(self.nc.semaphore(name)))
        self.counters.append(s)
        self.names[name] = s
        return s

    def sig(self, name):
        return self.names[name] if name in self.names else self.new_counter(name)

    def sb(self, stack, name, shape, dt=F32):
        self.uid += 1
        return stack.enter_context(self.nc.sbuf_tensor(f"{name}_{self.uid}", shape, dt))

    def ps(self, stack, name, shape=(P, SEQ), dt=F32):
        self.uid += 1
        return stack.enter_context(self.nc.psum_tensor(f"{name}_{self.uid}", list(shape), dt))

    def block(self):
        for s in self.counters:
            s.base = s.n
        return self.nc.Block()

    def const(self, name):
        at, n = self.const_at[name]
        return self.ins["shape_constants"][:, at:at + n]


def linker(eng, sig):
    def link(ins):
        ins.then_inc(*sig.up())
        eng.wait_ge(*sig.now())
        return ins
    return link


class Stream:
    def __init__(self, core, stack, slots, items):
        self.core, self.slots, self.items = core, slots, items
        self.ring = core.sb(stack, "weight_ring", [P, slots, 4096])
        self.low = core.nc.alloc_sbuf_tensor_at("low_parts", [P, slots, 4096], F32R,
                                                offset=core.nc.sbuf_base - slots * 4096 * 4)
        self.at = {key: n for n, (key, _, _, _) in enumerate(items)}
        self.landed = [core.new_counter(f"weights_in_slot{s}") for s in range(slots)]
        self.issued = 0
        self.high = {}

    def parts(self, key):
        n = self.at[key]
        _, _, a, b = self.items[n]
        low = self.low[:, n % self.slots, 0:a * b]
        return tuple(v.rearrange("p (a b) -> p a b", a=a) for v in (self.high[key][:, 0:a * b], low))

    def piece(self, key, q):
        n = self.at[key]
        _, _, a, b = self.items[n]
        s = slice(q * a * b // PIECES, (q + 1) * a * b // PIECES)
        return self.ring[:, n % self.slots, s], self.high[key][:, s], self.low[:, n % self.slots, s]

    def view(self, key):
        n = self.at[key]
        _, _, a, b = self.items[n]
        return self.ring[:, n % self.slots, 0:a * b].rearrange("p (a b) -> p a b", a=a)

    def load(self, sp):
        n = self.issued
        key, src, _, _ = self.items[n]
        sp.dma_start(self.view(key), src).then_inc(*self.landed[n % self.slots].up(16))
        self.issued += 1

    def arrived(self, eng, key):
        n = self.at[key]
        eng.wait_ge(self.landed[n % self.slots].sem, 16 * (n // self.slots + 1))

    def refill(self, sp, key, wait=None):
        assert self.at[key] + self.slots == self.issued or self.issued >= len(self.items), key
        if self.issued < len(self.items):
            if wait:
                sp.wait_ge(*wait)
            self.load(sp)


def split_plan(items, buffers=2):
    order = []
    for item in items:
        if item is not None and item not in order:
            order.append(item)
    last = {item: j for j, item in enumerate(items)}

    def pieces(i, qs):
        free = last[order[i - buffers]] if i >= buffers else None
        return [("split", (i * PIECES + q, order[i], q, free)) for q in qs]
    plan = pieces(0, range(PIECES)) if order else []
    for i, item in enumerate(order):
        jobs = [j for j, it in enumerate(items) if it == item]
        for at, j in enumerate(jobs):
            if i + 1 < len(order):
                plan += pieces(i + 1, range(PIECES * at // len(jobs), PIECES * (at + 1) // len(jobs)))
            plan.append(("read", j))
    plan += [("read", j) for j, item in enumerate(items) if item is None]
    return plan


def round_piece(core, stream, act, item, q, free):
    if q == 0:
        stream.arrived(act, item)
        if free is not None:
            act.wait_ge(*core.ready.at(free + 1))
    src, high, _ = stream.piece(item, q)
    core.nc.scalar.copy(high, src).then_inc(*core.rounded.up())


def rest_of_piece(core, stream, dve, nth, item, q):
    src, high, low = stream.piece(item, q)
    dve.wait_ge(*core.rounded.at(nth + 1))
    core.nc.vector.tensor_tensor(low, src, high, ALU.subtract).then_inc(*core.split.up())


def high_buffers(core, stack, stream, items):
    order = []
    for item in items:
        if item is not None and item not in order:
            order.append(item)
    if order:
        buf = core.sb(stack, "high_parts", [P, min(2, len(order)), 4096], F32R)
        for i, item in enumerate(order):
            stream.high[item] = buf[:, i % 2, :]
    return {item: i for i, item in enumerate(order)}


def wait_for_pieces(core, pe, i):
    def before(k):
        pe.wait_ge(*core.split.at(i * PIECES + k + 1))
    return before


def product_block(core, jobs, stream=None, loads=(), banks=6, early=None):
    nc = core.nc
    st = ExitStack()
    bank = [core.ps(st, f"bank{b}") for b in range(banks)]
    item_of = [job[0] for job in jobs]
    nth_item = high_buffers(core, st, stream, item_of)
    plan = split_plan(item_of)
    first_small = item_of.index(None) if None in item_of else None
    free = {"v": core.vfree, "a": core.afree}
    nth = []
    seen = {"v": 0, "a": 0}
    for job in jobs:
        seen[job[2]] += 1
        nth.append(seen[job[2]])
    last_of = {}
    for j, job in enumerate(jobs):
        if job[0] is not None:
            last_of[job[0]] = j
    with core.block() as block:
        @block.sync
        def _(sp):
            for dst, src in loads:
                sp.dma_start(dst, src).then_inc(*core.dma.up(16))
            for key in sorted(last_of, key=lambda k: last_of[k]):
                stream.refill(sp, key, core.ready.at(last_of[key] + 1))
            if loads:
                sp.wait_ge(*core.dma.at(16 * len(loads)))

        @block.tensor
        def _(pe):
            if early:
                pe.wait_ge(*early.now())
            waited = set()
            for j, (item, fill, _, _) in enumerate(jobs):
                if loads and j == first_small:
                    pe.wait_ge(*core.dma.at(16 * len(loads)))
                if j >= banks:
                    pe.wait_ge(*free[jobs[j - banks][2]].at(nth[j - banks]))
                if item is None:
                    last = fill(bank[j % banks])
                else:
                    last = fill(bank[j % banks], None if item in waited else wait_for_pieces(core, pe, nth_item[item]))
                    waited.add(item)
                last.then_inc(*core.ready.up())

        def reader(eng, which, chain):
            link = linker(eng, chain)
            meets_loads = [j for j, job in enumerate(jobs) if job[0] is None and job[2] == which] if loads else []
            for step, what in plan:
                if step == "split":
                    nth_piece, item, q, frees = what
                    if which == "a":
                        round_piece(core, stream, eng, item, q, frees)
                    else:
                        rest_of_piece(core, stream, eng, nth_piece, item, q)
                    continue
                j = what
                _, _, e, read = jobs[j]
                if e == which:
                    if j in meets_loads[:1]:
                        eng.wait_ge(*core.dma.at(16 * len(loads)))
                    eng.wait_ge(*core.ready.at(j + 1))
                    read(link, bank[j % banks]).then_inc(*free[which].up())

        @block.vector
        def _(dve):
            reader(dve, "v", core.vchain)

        @block.scalar
        def _(act):
            reader(act, "a", core.achain)
    st.close()


def sum_of(nc, out, pairs):
    for n, (lhsT, rhs) in enumerate(pairs):
        last = nc.tensor.matmul(out, lhsT, rhs, start=(n == 0), stop=(n == len(pairs) - 1))
    return last


def sum_of_split(nc, out, pairs, before=None):
    for n, ((lh, ll), (rh, rl)) in enumerate(pairs):
        if before:
            before(n)
        nc.tensor.matmul(out, lh, rh, start=(n == 0), stop=False)
        nc.tensor.matmul(out, lh, rl, start=False, stop=False)
        last = nc.tensor.matmul(out, ll, rh, start=False, stop=(n == len(pairs) - 1))
    return last


def copy_on(nc, which, out, in_):
    return nc.vector.tensor_copy(out, in_) if which == "v" else nc.scalar.copy(out, in_)


def transpose_job(core, srcs, dst, which, gain=None, item=None):
    nc = core.nc
    n = srcs[0].shape[-1]
    m = srcs[0].shape[0]

    def fill(bank):
        for i, s in enumerate(srcs):
            last = nc.tensor.transpose(bank[0:n, i * m:(i + 1) * m], s, core.ident[0:m, 0:m])
        return last

    def read(link, bank):
        src = bank[0:n, 0:m * len(srcs)]
        if len(dst.shape) == 3:
            src = src.rearrange("p (a b) -> p a b", b=dst.shape[-1])
        if gain is None:
            return copy_on(nc, which, dst, src)
        if which == "v":
            return nc.vector.tensor_scalar(dst, src, gain, None, ALU.mult)
        return nc.scalar.mul(dst, src, gain)
    return (item, fill, which, read)


def channel_major(core, stream, src, item, cols, m, ntok=SEQ, kd=KD):

    def fill(bank, before=None):
        high, low = stream.parts(item)
        return sum_of_split(core.nc, bank[0:m, 0:ntok],
                            [((high[:, k, cols:cols + m], low[:, k, cols:cols + m]),
                              (src[:, 0, k, 0:ntok], src[:, 1, k, 0:ntok])) for k in range(kd)], before)
    return fill


def token_major(core, stream, src, item, tile, cols, n, kd=KD):

    def fill(bank, before=None):
        high, low = stream.parts(item)
        s, c = slice(tile * P, (tile + 1) * P), slice(cols, cols + n)
        return sum_of_split(core.nc, bank[:, 0:n],
                            [((src[:, 0, k, s], src[:, 1, k, s]), (high[:, k, c], low[:, k, c])) for k in range(kd)], before)
    return fill


def split_transposes(core, groups):
    nc = core.nc
    st = ExitStack()
    bank = [core.ps(st, f"turned{b}") for b in range(4)]
    high_done, low_done = core.sig("turned_high"), core.sig("turned_low")
    width = [P * len(g[0]) for g in groups]
    with core.block() as block:
        @block.tensor
        def _(pe):
            for j, (srcs, _, _, _) in enumerate(groups):
                if j >= 4:
                    pe.wait_ge(*low_done.at(j - 3))
                for i, s in enumerate(srcs):
                    last = nc.tensor.transpose(bank[j % 4][:, i * P:(i + 1) * P], s, core.ident)
                last.then_inc(*core.ready.up())

        @block.scalar
        def _(act):
            for j, (_, high, _, gain) in enumerate(groups):
                act.wait_ge(*core.ready.at(j + 1))
                nc.scalar.mul(high, bank[j % 4][:, 0:width[j]], gain).then_inc(*high_done.up())

        @block.vector
        def _(dve):
            for j, (_, high, low, gain) in enumerate(groups):
                dve.wait_ge(*high_done.at(j + 1))
                nc.vector.scalar_tensor_tensor(out=low, in0=bank[j % 4][:, 0:width[j]], scalar=gain, in1=high,
                                               op0=ALU.mult, op1=ALU.subtract).then_inc(*low_done.up())
    st.close()


def rms_rows(core, src, tiles, dst):
    nc = core.nc
    st = ExitStack()
    sq = core.sb(st, "squares", [P, tiles, D])
    ss = core.sb(st, "sum_squares", [P, tiles])
    rs = core.sb(st, "rms", [P, tiles])
    summed = core.sig("squares_summed")
    rooted = core.sig("rms_rooted")
    with core.block() as block:
        @block.scalar
        def _(act):
            for t in range(0, tiles, 2):
                nc.scalar.activation(sq[:, t, :], src[:, t, :], ACT.Square, accum_out=ss[:, t:t + 1]).then_inc(*core.achain.up())
            act.wait_ge(*core.achain.now())
            act.wait_ge(*summed.at(tiles // 2))
            nc.scalar.activation(rs[:], ss[:], ACT.Sqrt, scale=1.0 / D, bias=core.eps[:, 0:1]).then_inc(*rooted.up())

        @block.vector
        def _(dve):
            link = linker(dve, core.vchain)
            for t in range(1, tiles, 2):
                nc.vector.tensor_tensor_reduce(sq[:, t, :], src[:, t, :], src[:, t, :], 1.0, 0.0, ALU.mult, ALU.add,
                                               ss[:, t:t + 1]).then_inc(*summed.up())
            dve.wait_ge(*rooted.at(1))
            link(nc.vector.reciprocal(rs[:], rs[:]))
            for t in range(tiles):
                nc.vector.tensor_scalar(dst[:, t, :], src[:, t, :], rs[:, t:t + 1], None, ALU.mult)
    st.close()


def norm_to_channels(core, src, tiles, gain, hT, keep=None):
    st = ExitStack()
    xn = keep if keep is not None else core.sb(st, "normed", [P, tiles, D])
    rms_rows(core, src, tiles, xn)
    srcs = [[xn[:, t, k * P:(k + 1) * P] for t in range(tiles)] for k in range(KD)]
    if hT.dtype == F32R:
        split_transposes(core, [(srcs[k], hT[:, 0, k, :], hT[:, 1, k, :], gain[:, k:k + 1]) for k in range(KD)])
    else:
        product_block(core, [transpose_job(core, srcs[k], hT[:, k, 0:tiles * P], "va"[k % 2], gain=gain[:, k:k + 1])
                             for k in range(KD)])
    st.close()


def norm_channels(core, chunks, group, eps, gains, per_head, ntok=SEQ, mean=True):
    nc = core.nc
    st = ExitStack()
    flat = [(g, c) for g, cs in enumerate(chunks) for c in cs]
    most = max(len(cs) for cs in chunks)
    sq = core.sb(st, "squares", [P, 2, most, ntok])
    inv = core.sb(st, "inverses", [P, len(chunks), ntok])
    bank = [core.ps(st, f"sums{b}") for b in range(2)]
    squared, summed, logged, rooted, scaled = (core.sig(x) for x in (
        "ch_squared", "ch_summed", "ch_logged", "ch_rooted", "ch_scaled"))
    n = len(chunks)
    done = [sum(len(cs) for cs in chunks[:g + 1]) for g in range(n)]
    with core.block() as block:
        @block.scalar
        def _(act):
            for g in range(n):
                act.wait_ge(*summed.at(g + 1))
                nc.scalar.activation(inv[:, g, :], bank[g % 2][:, 0:ntok], ACT.Ln,
                                     scale=1.0 / per_head if mean else 1.0, bias=eps).then_inc(*logged.up())
            for g in range(n):
                act.wait_ge(*logged.at(g + 1))
                nc.scalar.activation(inv[:, g, :], inv[:, g, :], ACT.Exp, scale=-0.5).then_inc(*rooted.up())

        @block.tensor
        def _(pe):
            for g in range(n):
                pe.wait_ge(*squared.at(done[g]))
                if g >= 2:
                    pe.wait_ge(*logged.at(g - 1))
                sum_of(nc, bank[g % 2][:, 0:ntok], [(group, sq[:, g % 2, i, :]) for i in range(len(chunks[g]))]
                       ).then_inc(*summed.up())

        @block.vector
        def _(dve):
            def square(g):
                if g >= 2:
                    dve.wait_ge(*summed.at(g - 1))
                for i, c in enumerate(chunks[g]):
                    nc.vector.tensor_tensor(sq[:, g % 2, i, :], c, c, ALU.mult).then_inc(*squared.up())

            k = 0
            for g in range(n):
                square(g)
            for g in range(n):
                dve.wait_ge(*rooted.at(g + 1))
                for c in chunks[g]:
                    nc.vector.scalar_tensor_tensor(out=c, in0=c, scalar=gains[k], in1=inv[:, g, :],
                                                   op0=ALU.mult, op1=ALU.mult).then_inc(*scaled.up())
                    k += 1
    st.close()


def conv_block(core, stream, src, chunks, taps, bias):
    nc = core.nc
    st = ExitStack()
    bank = [core.ps(st, f"raw{b}") for b in range(4)]
    acc = core.sb(st, "convolved", [P, 3, SEQ])
    convolved, activated = core.sig("chunk_convolved"), core.sig("chunk_activated")
    n = len(chunks)
    last_of = {c[0]: j for j, c in enumerate(chunks)}
    item_of = [c[0] for c in chunks]
    nth_item = high_buffers(core, st, stream, item_of)
    plan = split_plan(item_of)
    with core.block() as block:
        @block.sync
        def _(sp):
            for key in sorted(last_of, key=lambda k: last_of[k]):
                stream.refill(sp, key, core.ready.at(last_of[key] + 1))

        @block.tensor
        def _(pe):
            for j, (item, col, _, _) in enumerate(chunks):
                if j >= 4:
                    pe.wait_ge(*convolved.at(j - 3))
                first = item_of.index(item) == j
                channel_major(core, stream, src, item, col, P)(
                    bank[j % 4], wait_for_pieces(core, pe, nth_item[item]) if first else None).then_inc(*core.ready.up())

        @block.vector
        def _(dve):
            link = linker(dve, core.vchain)
            for step, what in plan:
                if step == "split":
                    nth_piece, item, q, _ = what
                    rest_of_piece(core, stream, dve, nth_piece, item, q)
                    continue
                j, w = what, chunks[what][3]
                dve.wait_ge(*core.ready.at(j + 1))
                if j >= 3:
                    dve.wait_ge(*activated.at(j - 2))
                a, raw = acc[:, j % 3, :], bank[j % 4]
                link(nc.vector.tensor_scalar(a, raw[:], taps[:, w, 3:4], None, ALU.mult))
                for back in (1, 2, 3):
                    ins = nc.vector.scalar_tensor_tensor(
                        out=acc[:, j % 3, back:], in0=raw[:, 0:SEQ - back], scalar=taps[:, w, 3 - back:4 - back],
                        in1=acc[:, j % 3, back:], op0=ALU.mult, op1=ALU.add)
                    if back < 3:
                        link(ins)
                ins.then_inc(*convolved.up())

        @block.scalar
        def _(act):
            for step, what in plan:
                if step == "split":
                    _, item, q, frees = what
                    round_piece(core, stream, act, item, q, frees)
                    continue
                j, (_, _, dst, w) = what, chunks[what]
                act.wait_ge(*convolved.at(j + 1))
                nc.scalar.activation(dst, acc[:, j % 3, :], ACT.Silu,
                                     bias=bias[:, w:w + 1] if bias is not None else 0.0).then_inc(*activated.up())
    st.close()


def merge_branch(core, stream, hT, yT, n, merged):
    nc = core.nc
    st = ExitStack()
    gate_bank = [core.ps(st, f"gate{b}") for b in range(NT)]
    proj_bank = [core.ps(st, f"proj{b}") for b in range(NT)]
    gate = core.sb(st, "gate", [P, 3, SEQ])
    part = core.sb(st, "part", [P, 3, SEQ])
    projected = core.sig("branch_products")
    gated, multiplied, added = core.sig("gate_ready"), core.sig("branch_gated"), core.sig("branch_added")
    jobs = [(half, t) for half in range(2) for t in range(NT)]
    first_gate, second_gate, w_br = f"merge{n}_0", f"merge{n}_1", f"w_br{n}"
    high = core.sb(st, "high_parts", [P, 3, 4096], F32R)
    for i, item in enumerate((first_gate, w_br, second_gate)):
        stream.high[item] = high[:, i, :]
    pieces = [(w_br, q) for q in range(0, PIECES, 2)] + [(first_gate, q) for q in range(PIECES)] \
        + [(w_br, q) for q in range(1, PIECES, 2)] + [(second_gate, q) for q in range(PIECES)]
    place = {p: i for i, p in enumerate(pieces)}
    ahead = PIECES * 3 // 2
    plan = [("split", i) for i in range(ahead)]
    for j in range(len(jobs)):
        if j < NT - 1:
            plan += [("split", ahead + 4 * j + i) for i in range(4)]
        plan.append(("read", j))
    with core.block() as block:
        @block.sync
        def _(sp):
            stream.refill(sp, first_gate, core.ready.at(NT))
            stream.refill(sp, w_br, projected.at(2))
            stream.refill(sp, second_gate, core.ready.at(2 * NT))

        @block.tensor
        def _(pe):
            for half, item in enumerate((first_gate, second_gate)):
                def branch_piece(k):
                    pe.wait_ge(*core.split.at(place[w_br, 2 * k + half] + 1))

                def gate_piece(k):
                    pe.wait_ge(*core.split.at(place[item, k] + 1))
                for t in range(NT):
                    if half == 1:
                        pe.wait_ge(*multiplied.at(t + 1))
                    last = token_major(core, stream, yT, w_br, t, half * SEQ, SEQ, kd=4)(
                        proj_bank[t], branch_piece if t == 0 else None)
                last.then_inc(*projected.up())
                for t in range(NT):
                    if half == 1:
                        pe.wait_ge(*gated.at(t + 1))
                    token_major(core, stream, hT, item, t, 0, SEQ)(
                        gate_bank[t], gate_piece if t == 0 else None).then_inc(*core.ready.up())

        @block.scalar
        def _(act):
            for step, j in plan:
                if step == "split":
                    item, q = pieces[j]
                    round_piece(core, stream, act, item, q, None)
                    continue
                act.wait_ge(*core.ready.at(j + 1))
                if j >= 3:
                    act.wait_ge(*multiplied.at(j - 2))
                nc.scalar.activation(gate[:, j % 3, :], gate_bank[j % NT][:], ACT.Sigmoid).then_inc(*gated.up())

        @block.vector
        def _(dve):
            for step, j in plan:
                if step == "split":
                    rest_of_piece(core, stream, dve, j, *pieces[j])
                    continue
                half, t = jobs[j]
                dve.wait_ge(*gated.at(j + 1))
                m = merged[:, t, half * SEQ:(half + 1) * SEQ]
                if n == 0:
                    nc.vector.tensor_tensor(m, proj_bank[j % NT][:], gate[:, j % 3, :], ALU.mult
                                            ).then_inc(*multiplied.up())
                    continue
                if j >= 3:
                    dve.wait_ge(*added.at(j - 2))
                nc.vector.tensor_tensor(part[:, j % 3, :], proj_bank[j % NT][:], gate[:, j % 3, :], ALU.mult
                                        ).then_inc(*multiplied.up())
                dve.wait_ge(*multiplied.at(j + 1))
                nc.vector.tensor_tensor(m, m, part[:, j % 3, :], ALU.add).then_inc(*added.up())
    st.close()


def gate_with_z(core, stream, hT, item, y, norm=None):
    nc = core.nc
    st = ExitStack()
    bank = [core.ps(st, f"z{b}") for b in range(4)]
    z = core.sb(st, "z", [P, 2, SEQ])
    gated, used = core.sig("z_ready"), core.sig("z_used")
    high_buffers(core, st, stream, [item])
    if norm:
        on_scalar, on_vector = head_rms_steps(core, st, y, *norm)
    with core.block() as block:
        @block.sync
        def _(sp):
            stream.refill(sp, item, core.ready.at(NT))

        @block.tensor
        def _(pe):
            for t in range(NT):
                token_major(core, stream, hT, item, t, 0, SEQ)(
                    bank[t], wait_for_pieces(core, pe, 0) if t == 0 else None).then_inc(*core.ready.up())

        @block.scalar
        def _(act):
            for q in range(PIECES):
                round_piece(core, stream, act, item, q, None)
            if norm:
                on_scalar(act)
            for t in range(NT):
                act.wait_ge(*core.ready.at(t + 1))
                if t >= 2:
                    act.wait_ge(*used.at(t - 1))
                nc.scalar.activation(z[:, t % 2, :], bank[t][:], ACT.Silu).then_inc(*gated.up())

        @block.vector
        def _(dve):
            for q in range(PIECES):
                rest_of_piece(core, stream, dve, q, item, q)
            if norm:
                on_vector(dve)
            for t in range(NT):
                dve.wait_ge(*gated.at(t + 1))
                nc.vector.tensor_tensor(y[:, t, :], y[:, t, :], z[:, t % 2, :], ALU.mult).then_inc(*used.up())
    st.close()


def to_channels(core, y, yT, chunks):
    split_transposes(core, [([y[:, t, c * P:(c + 1) * P] for t in range(NT)], yT[:, 0, c, :], yT[:, 1, c, :], core.one[:, 0:1])
                            for c in range(chunks)])


def head_rms_steps(core, stack, y, heads, width, gain):
    nc = core.nc
    sq = core.sb(stack, "squares", [P, NT, heads, width])
    ss = core.sb(stack, "sum_squares", [P, NT, heads])
    each = gain if len(gain.shape) == 3 else gain.unsqueeze(1).to_broadcast([P, heads, width])
    squared, summed, rooted = core.sig("heads_squared"), core.sig("heads_summed"), core.sig("heads_rooted")
    eps = core.eps

    def on_scalar(act):
        for t in range(NT):
            nc.scalar.activation(sq[:, t], y[:, t, :].rearrange("p (h w) -> p h w", h=heads), ACT.Square
                                 ).then_inc(*squared.up())
        act.wait_ge(*summed.at(1))
        nc.scalar.activation(ss[:], ss[:], ACT.Sqrt, scale=1.0 / width, bias=eps[:, 0:1]).then_inc(*rooted.up())

    def on_vector(dve):
        link = linker(dve, core.vchain)
        dve.wait_ge(*squared.at(NT))
        nc.vector.tensor_reduce(ss[:], sq[:], AX.X, ALU.add).then_inc(*summed.up())
        dve.wait_ge(*rooted.at(1))
        link(nc.vector.reciprocal(ss[:], ss[:]))
        for t in range(NT):
            yt = y[:, t, :].rearrange("p (h w) -> p h w", h=heads)
            link(nc.vector.tensor_tensor(yt, yt, ss[:, t, :].unsqueeze(2).to_broadcast([P, heads, width]), ALU.mult))
            link(nc.vector.tensor_tensor(yt, yt, each, ALU.mult))
    return on_scalar, on_vector


def head_rms(core, y, heads, width, gain):
    st = ExitStack()
    on_scalar, on_vector = head_rms_steps(core, st, y, heads, width, gain)
    with core.block() as block:
        @block.scalar
        def _(act):
            on_scalar(act)

        @block.vector
        def _(dve):
            on_vector(dve)
    st.close()


def small_products(core, stream, hT, w_small, small, gkT):
    nc = core.nc
    st = ExitStack()
    smallT = core.sb(st, "smallT", [P, SEQ])

    def fill(bank):
        return sum_of_split(nc, bank[0:56, :], [((w_small[:, 0, k, :], w_small[:, 1, k, :]), (hT[:, 0, k, :], hT[:, 1, k, :]))
                                                for k in range(KD)])

    def read(link, bank):
        link(nc.vector.tensor_copy(gkT[:], bank[0:16, :]))
        link(nc.vector.memset(smallT[:], 0.0))
        return nc.vector.tensor_copy(smallT[0:56, :], bank[0:56, :])
    product_block(core, [(None, fill, "v", read)])
    product_block(core, [(None, lambda bank, t=t: nc.tensor.transpose(bank[:, 0:P], smallT[:, t * P:(t + 1) * P], core.ident),
                          "v", lambda link, bank, t=t: nc.vector.tensor_copy(small[:, t, :], bank[:, 16:56])) for t in range(NT)])
    st.close()


def decay_rates(core, small, head_par, rate, dt, gates, beta):
    nc = core.nc
    st = ExitStack()
    x = core.sb(st, "x", [P, NT, 12])
    e = core.sb(st, "e", [P, NT, 12])
    a = core.sb(st, "a", [P, 12])
    shifted, logged, ready = core.sig("dt_shifted"), core.sig("dt_logged"), core.sig("a_exped")
    with core.block() as block:
        @block.vector
        def _(dve):
            link = linker(dve, core.vchain)
            nc.vector.tensor_tensor(x[:], small[:, :, 4:16], head_par[:, 12:24].unsqueeze(1).to_broadcast([P, NT, 12]), ALU.add
                                    ).then_inc(*shifted.up())
            dve.wait_ge(*logged.at(1))
            link(nc.vector.scalar_tensor_tensor(out=dt[:], in0=x[:], scalar=0.0, in1=e[:], op0=ALU.max, op1=ALU.add))
            dve.wait_ge(*ready.at(1))
            link(nc.vector.tensor_tensor(rate[:], dt[:], a[:].unsqueeze(1).to_broadcast([P, NT, 12]), ALU.mult))
            nc.vector.tensor_scalar(rate[:], rate[:], -1.0, None, ALU.mult)

        @block.scalar
        def _(act):
            link = linker(act, core.achain)
            act.wait_ge(*shifted.at(1))
            link(nc.scalar.activation(e[:], x[:], ACT.Abs))
            link(nc.scalar.activation(e[:], e[:], ACT.Exp, scale=-1.0))
            nc.scalar.activation(a[:], head_par[:, 0:12], ACT.Exp).then_inc(*ready.up())
            nc.scalar.activation(e[:], e[:], ACT.Ln, bias=core.one[:, 0:1]).then_inc(*logged.up())
            nc.scalar.activation(beta[:], small[:, :, 0:4], ACT.Sigmoid)
            nc.scalar.activation(gates[:], small[:, :, 16:40], ACT.Sigmoid)
    st.close()


def decay_sums(core, rate, upto, cum, e_cum, e_rest, e_total):
    nc = core.nc
    st = ExitStack()
    bank = core.ps(st, "sums")
    tot = core.sb(st, "total", [P, NT, 12])
    summed, split = core.sig("rates_summed"), core.sig("rates_split")
    n = NT * 12
    with core.block() as block:
        @block.tensor
        def _(pe):
            nc.tensor.matmul(bank[:, 0:n], upto, rate[:].rearrange("p t h -> p (t h)"), start=True, stop=True)
            nc.tensor.matmul(bank[:, n:2 * n], core.ones, rate[:].rearrange("p t h -> p (t h)"), start=True, stop=True
                             ).then_inc(*summed.up())

        @block.vector
        def _(dve):
            link = linker(dve, core.vchain)
            dve.wait_ge(*summed.at(1))
            link(nc.vector.tensor_copy(cum[:].rearrange("p t h -> p (t h)"), bank[:, 0:n]))
            nc.vector.tensor_tensor(tot[:].rearrange("p t h -> p (t h)"), bank[:, n:2 * n],
                                    cum[:].rearrange("p t h -> p (t h)"), ALU.subtract).then_inc(*split.up())

        @block.scalar
        def _(act):
            act.wait_ge(*split.at(1))
            nc.scalar.activation(e_rest[:], tot[:], ACT.Exp)
            nc.scalar.activation(e_cum[:], cum[:], ACT.Exp)
            nc.scalar.activation(e_total[:].rearrange("p t h -> p (t h)"), bank[:, n:2 * n], ACT.Exp)
    st.close()


def gdn(core, stream, hT, dec, y, small_of):
    nc, ins = core.nc, core.ins
    st = ExitStack()
    H = 4
    qT = core.sb(st, "qT", [P, H, SEQ])
    kT = core.sb(st, "kT", [P, H, SEQ])
    vT = core.sb(st, "vT", [P, H, SEQ])
    conv_block(core, stream, hT, [(f"gdn{w}", c * P, dst[:, c, :], 4 * i + c)
                                  for i, (w, dst) in enumerate((("_q", qT), ("_k", kT), ("_v", vT))) for c in range(4)],
               small_of["conv_a"], None)
    norm_channels(core, [[qT[:, h, :]] for h in range(H)] + [[kT[:, h, :]] for h in range(H)], core.ones,
                  core.eps[:, 0:1], [P ** -0.5] * H + [1.0] * H, P, mean=False)
    k = core.sb(st, "k", [P, NT, SEQ])
    v = core.sb(st, "v", [P, NT, SEQ])
    attnT = core.sb(st, "attnT", [P, NT, SEQ])
    product_block(core, [transpose_job(core, [s[:, h, t * P:(t + 1) * P] for t in range(NT)],
                                       d[:, :, h * P:(h + 1) * P], "va"[h % 2])
                         for s, d in ((kT, k), (vT, v)) for h in range(H)])
    lower = vT
    cum, e_cum, e_rest, e_total = (dec[x] for x in ("cum", "e_cum", "e_rest", "e_total"))
    rate, beta = dec["rate"], dec["beta"]

    inner = ExitStack()
    rows = [core.ps(inner, f"rows{b}") for b in range(2)]
    kk = [core.ps(inner, f"kk{b}") for b in range(2)]
    qk = [core.ps(inner, f"qk{b}") for b in range(2)]
    strict = core.sb(inner, "strict", [P, P])
    causal = core.sb(inner, "causal", [P, P])
    dl = core.sb(inner, "decay_lower", [P, 2, SEQ])
    da = core.sb(inner, "decay_attn", [P, 2, SEQ])
    dq = core.sb(inner, "decay_q", [P, 2, SEQ])
    spread, exped, used = core.sig("tile_exponents"), core.sig("tile_exped"), core.sig("tile_decays_used")
    lowered, decayed = core.sig("tile_lower_ready"), core.sig("tile_queries_decayed")
    hb = lambda ap, t: ap[:, t, 0:H].unsqueeze(2).to_broadcast([P, H, P])
    four = lambda ap: ap.rearrange("p (h c) -> p h c", h=H)
    with core.block() as block:
        @block.sync
        def _(sp):
            sp.dma_start(strict[:], core.const("strict_bias")).then_inc(*core.dma.up(16))
            sp.dma_start(causal[:], core.const("causal_biasT")).then_inc(*core.dma.up(16))

        @block.tensor
        def _(pe):
            for t in range(NT):
                if t >= 2:
                    pe.wait_ge(*used.at(t - 1))
                    pe.wait_ge(*exped.at(t - 1))
                tile = slice(t * P, (t + 1) * P)
                for h in range(H):
                    nc.tensor.matmul(rows[t % 2][:, h * P:(h + 1) * P], rate[:, t, h:h + 1].to_broadcast([P, P]),
                                     core.upto, start=True, stop=True)
                for h in range(H):
                    nc.tensor.matmul(kk[t % 2][:, h * P:(h + 1) * P], kT[:, h, tile], kT[:, h, tile], start=True, stop=True)
                for h in range(H):
                    last = nc.tensor.matmul(qk[t % 2][:, h * P:(h + 1) * P], kT[:, h, tile], qT[:, h, tile],
                                            start=True, stop=True)
                last.then_inc(*core.ready.up())

        @block.vector
        def _(dve):
            link = linker(dve, core.vchain)
            dve.wait_ge(*core.dma.at(32))

            def exponents(t):
                dve.wait_ge(*core.ready.at(t + 1))
                r = four(rows[t % 2][:])
                l, a = four(dl[:, t % 2, :]), four(da[:, t % 2, :])
                link(nc.vector.tensor_tensor(l, strict[:].unsqueeze(1).to_broadcast([P, H, P]), r, ALU.subtract))
                link(nc.vector.tensor_tensor(a, causal[:].unsqueeze(1).to_broadcast([P, H, P]), r, ALU.add))
                link(nc.vector.tensor_tensor(l, l, hb(cum, t), ALU.add))
                nc.vector.tensor_tensor(a, a, hb(cum, t), ALU.subtract).then_inc(*spread.up())

            def scores(t):
                dve.wait_ge(*exped.at(t + 1))
                lo = lower[:, t, :]
                nc.vector.tensor_tensor(lo, kk[t % 2][:], dl[:, t % 2, :], ALU.mult).then_inc(*lowered.up())
                nc.vector.tensor_tensor(attnT[:, t, :], qk[t % 2][:], da[:, t % 2, :], ALU.mult).then_inc(*used.up())
            exponents(0)
            for t in range(NT):
                if t + 1 < NT:
                    exponents(t + 1)
                scores(t)

        @block.scalar
        def _(act):
            for t in range(NT):
                act.wait_ge(*spread.at(t + 1))
                if t >= 2:
                    act.wait_ge(*used.at(t - 1))
                    act.wait_ge(*decayed.at(t - 1))
                nc.scalar.activation(dl[:, t % 2, :], dl[:, t % 2, :], ACT.Exp)
                nc.scalar.activation(da[:, t % 2, :], da[:, t % 2, :], ACT.Exp)
                nc.scalar.activation(dq[:, t % 2, :], rows[t % 2][:], ACT.Exp).then_inc(*exped.up())

        @block.gpsimd
        def _(pool):
            for t in range(NT):
                q, lo = qT[:, :, t * P:(t + 1) * P], four(lower[:, t, :])
                pool.wait_ge(*exped.at(t + 1))
                nc.gpsimd.tensor_tensor(q, q, four(dq[:, t % 2, :]), ALU.mult).then_inc(*decayed.up())
                pool.wait_ge(*lowered.at(t + 1))
                nc.gpsimd.tensor_tensor(lo, lo, hb(beta, t), ALU.mult)
    inner.close()

    inner = ExitStack()
    inv = core.sb(inner, "inv", [P, NT, SEQ])
    invT = core.sb(inner, "invT", [P, NT, SEQ])
    level = core.sb(inner, "levels", [P, 7, P])
    pair = core.sb(inner, "pair_blocks", [P, 3, SEQ])
    mid = core.sb(inner, "pair_times_inv", [P, 2, SEQ])
    psum_in = ExitStack()
    first = [core.ps(psum_in, f"first{b}") for b in range(2)]
    second = [core.ps(psum_in, f"second{b}") for b in range(2)]
    third = [core.ps(psum_in, f"third{b}") for b in range(2)]
    masked, halfway, copied, twice, updated = (core.sig(x) for x in (
        "pair_masked", "pair_inv_product", "pair_inv_copied", "inverse_products", "inverse_updated"))
    jobs = [(lvl, t) for lvl in range(7) for t in range(NT)]
    n = len(jobs)
    with core.block() as block:
        @block.sync
        def _(sp):
            at, _ = core.const_at["level0"]
            sp.dma_start(level[:].rearrange("p l n -> p (l n)"), ins["shape_constants"][:, at:at + 7 * P]).then_inc(*core.dma.up(16))
            sp.wait_ge(*core.dma.at(16))

        @block.vector
        def _(dve):
            for t in range(NT):
                nc.vector.tensor_copy(four(inv[:, t, :]), core.ident.unsqueeze(1).to_broadcast([P, H, P]))

        @block.scalar
        def _(act):
            for t in range(NT):
                nc.scalar.copy(four(invT[:, t, :]), core.ident.unsqueeze(1).to_broadcast([P, H, P]))
    with core.block() as block:
        @block.tensor
        def _(pe):
            def one(j):
                lvl, t = jobs[j]
                pe.wait_ge(*masked.at(j + 1))
                if j >= NT:
                    pe.wait_ge(*updated.at(j - NT + 1))
                if j >= 2:
                    pe.wait_ge(*copied.at(j - 1))
                for h in range(H):
                    s = slice(h * P, (h + 1) * P)
                    last = nc.tensor.matmul(first[j % 2][:, s], pair[:, j % 3, s], invT[:, t, s], start=True, stop=True)
                last.then_inc(*halfway.up())

            def two(j):
                lvl, t = jobs[j]
                pe.wait_ge(*copied.at(j + 1))
                if j >= 2:
                    pe.wait_ge(*updated.at(j - 1))
                for h in range(H):
                    s = slice(h * P, (h + 1) * P)
                    nc.tensor.matmul(second[j % 2][:, s], inv[:, t, s], mid[:, j % 2, s], start=True, stop=True)
                    last = nc.tensor.matmul(third[j % 2][:, s], mid[:, j % 2, s], inv[:, t, s], start=True, stop=True)
                last.then_inc(*twice.up())
            one(0)
            for j in range(n):
                if j + 1 < n:
                    one(j + 1)
                two(j)

        @block.scalar
        def _(act):
            for j in range(n):
                act.wait_ge(*halfway.at(j + 1))
                if j >= 2:
                    act.wait_ge(*twice.at(j - 1))
                nc.scalar.copy(mid[:, j % 2, :], first[j % 2][:]).then_inc(*copied.up())

        @block.vector
        def _(dve):
            def mask(j):
                lvl, t = jobs[j]
                if j >= 3:
                    dve.wait_ge(*halfway.at(j - 2))
                nc.vector.tensor_tensor(four(pair[:, j % 3, :]), four(lower[:, t, :]),
                                        level[:, lvl, :].unsqueeze(1).to_broadcast([P, H, P]), ALU.mult).then_inc(*masked.up())

            def update(j):
                lvl, t = jobs[j]
                dve.wait_ge(*twice.at(j + 1))
                if j >= NT:
                    dve.wait_ge(*updated.at(j - NT + 1))
                nc.vector.tensor_tensor(invT[:, t, :], invT[:, t, :], second[j % 2][:], ALU.subtract)
                nc.vector.tensor_tensor(inv[:, t, :], inv[:, t, :], third[j % 2][:], ALU.subtract).then_inc(*updated.up())
            mask(0)
            mask(1)
            for j in range(n):
                if j + 2 < n:
                    mask(j + 2)
                update(j)
    psum_in.close()

    u, wT = lower, inv
    kb = pair
    psum_in = ExitStack()
    u_bank = [core.ps(psum_in, f"u{b}") for b in range(2)]
    w_bank = [core.ps(psum_in, f"w{b}") for b in range(2)]
    scaled, solved, kept = core.sig("kv_scaled"), core.sig("kv_solved"), core.sig("kv_kept")
    with core.block() as block:
        @block.vector
        def _(dve):
            link = linker(dve, core.vchain)
            for t in range(NT):
                if t >= 2:
                    dve.wait_ge(*solved.at(t - 1))
                k4, v4, b4 = four(k[:, t, :]), four(v[:, t, :]), four(kb[:, t % 2, :])
                link(nc.vector.tensor_tensor(b4, k4, hb(beta, t), ALU.mult))
                nc.vector.tensor_tensor(v4, v4, hb(beta, t), ALU.mult)
                nc.vector.tensor_tensor(k4, k4, hb(e_rest, t), ALU.mult)
                nc.vector.tensor_tensor(b4, b4, hb(e_cum, t), ALU.mult).then_inc(*scaled.up())

        @block.tensor
        def _(pe):
            for t in range(NT):
                pe.wait_ge(*scaled.at(t + 1))
                if t >= 2:
                    pe.wait_ge(*kept.at(t - 1))
                for h in range(H):
                    s = slice(h * P, (h + 1) * P)
                    nc.tensor.matmul(u_bank[t % 2][:, s], invT[:, t, s], v[:, t, s], start=True, stop=True)
                    last = nc.tensor.matmul(w_bank[t % 2][:, s], kb[:, t % 2, s], invT[:, t, s], start=True, stop=True)
                last.then_inc(*solved.up())

        @block.scalar
        def _(act):
            for t in range(NT):
                act.wait_ge(*solved.at(t + 1))
                nc.scalar.copy(u[:, t, :], u_bank[t % 2][:])
                nc.scalar.copy(wT[:, t, :], w_bank[t % 2][:]).then_inc(*kept.up())
    psum_in.close()

    state = core.sb(inner, "state", [P, SEQ])
    new = mid
    psum_in = ExitStack()
    ws_bank = core.ps(psum_in, "ws")
    y_bank = [core.ps(psum_in, f"y{b}") for b in range(2)]
    s_bank = core.ps(psum_in, "ds")
    from_state, renewed, stepped, moved, written = (core.sig(x) for x in (
        "state_read", "values_renewed", "state_step_ready", "state_updated", "scan_written"))
    with core.block() as block:
        @block.vector
        def _(dve):
            link = linker(dve, core.vchain)
            nc.vector.memset(state[:], 0.0).then_inc(*moved.up())
            for t in range(NT):
                dve.wait_ge(*from_state.at(t + 1))
                nc.vector.tensor_tensor(new[:, t % 2, :], u[:, t, :], ws_bank[:], ALU.subtract).then_inc(*renewed.up())
                dve.wait_ge(*stepped.at(t + 1))
                if t == 0:
                    dve.wait_ge(*moved.at(1))
                link(nc.vector.tensor_tensor(four(state[:]), four(state[:]), hb(e_total, t), ALU.mult))
                nc.vector.tensor_tensor(state[:], state[:], s_bank[:], ALU.add).then_inc(*moved.up())
                if t < NT - 1:
                    dve.wait_ge(*moved.at(t + 2))

        @block.tensor
        def _(pe):
            for t in range(NT):
                tile = slice(t * P, (t + 1) * P)
                pe.wait_ge(*moved.at(t + 1))
                for h in range(H):
                    s = slice(h * P, (h + 1) * P)
                    last = nc.tensor.matmul(ws_bank[:, s], wT[:, t, s], state[:, s], start=True, stop=True)
                last.then_inc(*from_state.up())
                pe.wait_ge(*renewed.at(t + 1))
                if t >= 2:
                    pe.wait_ge(*written.at(t - 1))
                for h in range(H):
                    s = slice(h * P, (h + 1) * P)
                    sum_of(nc, y_bank[t % 2][:, s], [(qT[:, h, tile], state[:, s]), (attnT[:, t, s], new[:, t % 2, s])])
                for h in range(H):
                    s = slice(h * P, (h + 1) * P)
                    last = nc.tensor.matmul(s_bank[:, s], k[:, t, s], new[:, t % 2, s], start=True, stop=True)
                last.then_inc(*stepped.up())

        @block.scalar
        def _(act):
            for t in range(NT):
                act.wait_ge(*stepped.at(t + 1))
                nc.scalar.copy(y[:, t, :], y_bank[t % 2][:]).then_inc(*written.up())
    psum_in.close()
    inner.close()
    st.close()


def gla(core, stream, hT, gkT, y):
    nc, ins = core.nc, core.ins
    st = ExitStack()
    H, DK, DV = 4, 64, 128
    qk = core.sb(st, "qk", [P, NT, SEQ])
    v = core.sb(st, "v", [P, NT, SEQ])
    gk = core.sb(st, "gk", [P, NT, 256])
    w_gk = core.sb(st, "w_gk", [16, 256])
    b_gk = core.sb(st, "b_gk", [P, 256])
    mats = core.sb(st, "sum_matrices", [P, 7, P])
    names = ("gla_from_mid", "gla_within", "gla_to_half_end", "upto", "gla_to_end", "gla_near", "gla_far")
    jobs = []
    for t in range(NT):
        fill = token_major(core, stream, hT, "gla_qk", t, 0, SEQ)

        def read(link, bank, t=t):
            link(nc.vector.tensor_scalar(qk[:, t, 0:256], bank[:, 0:256], DK ** -0.5, None, ALU.mult))
            return nc.vector.tensor_copy(qk[:, t, 256:512], bank[:, 256:512])
        jobs.append(("gla_qk", fill, "v", read))
    for t in range(NT):
        jobs.append(("gla_v", token_major(core, stream, hT, "gla_v", t, 0, SEQ), "a",
                     lambda link, bank, t=t: nc.scalar.copy(v[:, t, :], bank[:])))
    for t in range(NT):
        jobs.append((None, lambda bank, t=t: nc.tensor.matmul(bank[:, 0:256], gkT[:, t * P:(t + 1) * P], w_gk[:],
                                                              start=True, stop=True), "v",
                     lambda link, bank, t=t: nc.vector.tensor_tensor(gk[:, t, :], bank[:, 0:256], b_gk[:], ALU.add)))
    product_block(core, jobs, stream, loads=[(w_gk[:], ins["w_gk"][0]), (b_gk[:], ins["b_gk"].to_broadcast([P, 256]))]
                  + [(mats[:, i, :], core.const(x)) for i, x in enumerate(names)])

    inner = ExitStack()
    mag = core.sb(inner, "mag", [P, NT, 256])
    logged = core.sig("gk_logged")
    with core.block() as block:
        @block.vector
        def _(dve):
            link = linker(dve, core.vchain)
            dve.wait_ge(*logged.at(1))
            link(nc.vector.scalar_tensor_tensor(out=gk[:], in0=gk[:], scalar=0.0, in1=mag[:], op0=ALU.min, op1=ALU.subtract))
            nc.vector.tensor_scalar(gk[:], gk[:], 1.0 / 16.0, None, ALU.mult)

        @block.scalar
        def _(act):
            link = linker(act, core.achain)
            link(nc.scalar.activation(mag[:], gk[:], ACT.Abs))
            link(nc.scalar.activation(mag[:], mag[:], ACT.Exp, scale=-1.0))
            nc.scalar.activation(mag[:], mag[:], ACT.Ln, bias=core.one[:, 0:1]).then_inc(*logged.up())
    inner.close()

    inner = ExitStack()
    state = core.sb(inner, "state", [P, H * DV])
    dec = core.sb(inner, "state_decay", [DK, NT * H])
    fac = core.sb(inner, "factors", [P, NT, 6, 256])
    facT = core.sb(inner, "factorsT", [P, 2, 5, H * P])
    aT = core.sb(inner, "aT", [P, 2, H * P])
    far_part = core.sb(inner, "far_part", [P, H * P])
    summed, exped, moved = core.sig("gk_summed"), core.sig("gk_exped"), core.sig("gla_state")
    psum_in = ExitStack()
    tot = core.ps(psum_in, "totals")
    with core.block() as block:
        @block.tensor
        def _(pe):
            for t in range(NT):
                for h in range(H):
                    i = t * H + h
                    last = nc.tensor.matmul(tot[0:DK, i:i + 1], gk[:, t, h * DK:(h + 1) * DK], core.ones[:, 0:1],
                                            start=True, stop=True)
            last.then_inc(*summed.up())

        @block.scalar
        def _(act):
            act.wait_ge(*summed.at(1))
            nc.scalar.activation(dec[:], tot[0:DK, 0:NT * H], ACT.Exp)

        @block.vector
        def _(dve):
            nc.vector.memset(state[:], 0.0)

        @block.gpsimd
        def _(pool):
            nc.gpsimd.memset(facT[DK:P, :, :, :], 0.0)
    psum_in.close()

    psum_in = ExitStack()
    sums = [core.ps(psum_in, f"sums{b}") for b in range(6)]
    pair_of = lambda t, i: sums[t % 2 * 3 + i // 2][:, (i % 2) * 256:(i % 2) * 256 + 256]
    with core.block() as block:
        @block.tensor
        def _(pe):
            for t in range(NT):
                if t >= 2:
                    pe.wait_ge(*exped.at(6 * (t - 1)))
                for i in range(5):
                    last = nc.tensor.matmul(pair_of(t, i), mats[:, i, :], gk[:, t, :], start=True, stop=True)
                last.then_inc(*summed.up())

        @block.scalar
        def _(act):
            for t in range(NT):
                act.wait_ge(*summed.at(t + 1))
                for i in range(6):
                    nc.scalar.activation(fac[:, t, i, :], pair_of(t, 0 if i == 5 else i), ACT.Exp,
                                         scale=-1.0 if i == 5 else 1.0).then_inc(*exped.up())

        @block.vector
        def _(dve):
            for t in range(NT):
                for i in range(6):
                    dve.wait_ge(*exped.at(6 * t + i + 1))
                    src = qk[:, t, 0:256] if i in (0, 1, 3) else qk[:, t, 256:512]
                    nc.vector.tensor_tensor(fac[:, t, i, :], fac[:, t, i, :], src, ALU.mult)
    psum_in.close()
    order = (0, 1, 3, 5, 2)
    scored, masked, stepped = core.sig("gla_scored"), core.sig("gla_masked"), core.sig("gla_stepped")
    head = [slice(h * P, (h + 1) * P) for h in range(H)]
    for pair in range(NT // 2):
        product_block(core, [transpose_job(core, [fac[:, 2 * pair + b, i, h * DK:(h + 1) * DK] for h in range(H)],
                                           facT[0:DK, b, n, :], "va"[n % 2]) for b in range(2) for n, i in enumerate(order)])
        psum_in = ExitStack()
        near, far, y_bank = ([core.ps(psum_in, f"{x}{b}") for b in range(2)] for x in ("near", "far", "y"))
        s_bank = core.ps(psum_in, "ds")

        with core.block() as block:
            @block.tensor
            def _(pe):
                for b in range(2):
                    q_near, q_far, _, k_near, k_far = (facT[:, b, n, :] for n in range(5))
                    for s in head:
                        nc.tensor.matmul(near[b][:, s], k_near[:, s], q_near[:, s], start=True, stop=True)
                    for s in head:
                        last = nc.tensor.matmul(far[b][:, s], k_far[:, s], q_far[:, s], start=True, stop=True)
                    last.then_inc(*scored.up())
                for b in range(2):
                    t = 2 * pair + b
                    q_state, k_end = facT[:, b, 2, :], fac[:, t, 4, :]
                    pe.wait_ge(*masked.at(b + 1))
                    if b == 1:
                        pe.wait_ge(*moved.at(1))
                    for s in head:
                        sum_of(nc, y_bank[b][:, s], [(q_state[:, s], state[:, s]), (aT[:, b, s], v[:, t, s])])
                    for h, s in enumerate(head):
                        last = nc.tensor.matmul(s_bank[0:DK, s], k_end[:, h * DK:(h + 1) * DK], v[:, t, s], start=True, stop=True)
                    last.then_inc(*stepped.up())

            @block.vector
            def _(dve):
                four = lambda ap: ap.rearrange("p (h c) -> p h c", h=H)
                m = lambda i: mats[:, i, :].unsqueeze(1).to_broadcast([P, H, P])
                link = linker(dve, core.vchain)
                for b in range(2):
                    dve.wait_ge(*scored.at(b + 1))
                    if b == 1:
                        dve.wait_ge(*masked.at(1))
                    link(nc.vector.tensor_tensor(four(far_part[:]), four(far[b][:]), m(6), ALU.mult))
                    link(nc.vector.scalar_tensor_tensor(out=four(aT[:, b, :]), in0=four(near[b][:]), scalar=3e38, in1=m(5),
                                                        op0=ALU.min, op1=ALU.mult))
                    nc.vector.tensor_tensor(aT[:, b, :], aT[:, b, :], far_part[:], ALU.add).then_inc(*masked.up())
                for b in range(2):
                    dve.wait_ge(*stepped.at(b + 1))
                    if b == 1:
                        dve.wait_ge(*moved.at(1))
                    for h, s in enumerate(head):
                        i = (2 * pair + b) * H + h
                        last = nc.vector.scalar_tensor_tensor(out=state[0:DK, s], in0=state[0:DK, s], scalar=dec[:, i:i + 1],
                                                              in1=s_bank[0:DK, s], op0=ALU.mult, op1=ALU.add)
                    last.then_inc(*moved.up())

            @block.scalar
            def _(act):
                for b in range(2):
                    act.wait_ge(*stepped.at(b + 1))
                    nc.scalar.copy(y[:, 2 * pair + b, :], y_bank[b][:])
        psum_in.close()
    inner.close()
    st.close()


def ssd(core, stream, hT, dec, y, small_of):
    nc, ins = core.nc, core.ins
    st = ExitStack()
    H, HD = 8, 64
    x = core.sb(st, "x", [P, NT, SEQ])
    Bt = core.sb(st, "B", [P, NT, 256])
    bT = core.sb(st, "BT", [P, 2, SEQ])
    cT = core.sb(st, "CT", [P, 2, SEQ])
    skip = small_of["d_skip_c"]
    inner = ExitStack()
    xT = core.sb(inner, "xT", [P, 4, SEQ])
    conv_block(core, stream, hT, [("ssd_x", c * P, xT[:, c, :], c) for c in range(4)]
               + [("ssd_bc", c * P, (bT if c < 2 else cT)[:, c % 2, :], 4 + c) for c in range(4)], small_of["conv_c"], small_of["conv_bias_c"])
    product_block(core, [transpose_job(core, [s[:, c, t * P:(t + 1) * P] for t in range(NT)],
                                       d[:, :, c * P:(c + 1) * P], "va"[c % 2])
                         for s, d, n in ((xT, x, 4), (bT, Bt, 2)) for c in range(n)])
    inner.close()

    inner = ExitStack()
    causal = core.sb(inner, "causal", [P, P])
    decay = core.sb(inner, "decay", [P, 2, H, P])
    xdt = core.sb(inner, "x_dt", [P, 2, SEQ])
    xend = core.sb(inner, "x_end", [P, 2, SEQ])
    state = core.sb(inner, "state", [P, SEQ])
    part = core.sb(inner, "part", [P, SEQ])
    rows = [core.ps(inner, f"rows{b}") for b in range(2)]
    cb, y_in, y_off, s_bank = (core.ps(inner, n) for n in ("cb", "y_in", "y_off", "ds"))
    cum, e_cum, e_rest, e_total, rate, dt = (dec[k] for k in ("cum", "e_cum", "e_rest", "e_total", "rate", "dt"))
    hb = lambda ap, t, w: ap[:, t, 4:12].unsqueeze(2).to_broadcast([P, H, w])
    per = lambda ap: ap.rearrange("p (h c) -> p h c", h=H)
    spread, exped, scaled, stepped, moved, used = (core.sig(n) for n in (
        "ssd_exponents", "ssd_exped", "ssd_scaled", "ssd_stepped", "ssd_state", "ssd_rows_read"))
    with core.block() as block:
        @block.sync
        def _(sp):
            sp.dma_start(causal[:], core.const("causal_biasT")).then_inc(*core.dma.up(16))

        @block.tensor
        def _(pe):
            def scores(t):
                tile = slice(t * P, (t + 1) * P)
                if t >= 1:
                    pe.wait_ge(*used.at(t))
                    pe.wait_ge(*scaled.at(t))
                for h in range(H):
                    nc.tensor.matmul(rows[h // 4][:, (h % 4) * P:(h % 4 + 1) * P],
                                     rate[:, t, 4 + h:5 + h].to_broadcast([P, P]), core.upto, start=True, stop=True)
                for g in range(2):
                    last = nc.tensor.matmul(cb[:, g * P:(g + 1) * P], bT[:, g, tile], cT[:, g, tile], start=True, stop=True)
                last.then_inc(*core.ready.up())

            def outputs(t):
                tile = slice(t * P, (t + 1) * P)
                pe.wait_ge(*scaled.at(t + 1))
                pe.wait_ge(*moved.at(t + 1))
                for h in range(H):
                    s = slice(h * HD, (h + 1) * HD)
                    nc.tensor.matmul(y_in[:, s], decay[:, t % 2, h, :], xdt[:, t % 2, s], start=True, stop=True)
                for g in range(2):
                    s = slice(g * 256, (g + 1) * 256)
                    nc.tensor.matmul(y_off[:, s], cT[:, g, tile], state[:, s], start=True, stop=True)
                for g in range(2):
                    s = slice(g * 256, (g + 1) * 256)
                    last = nc.tensor.matmul(s_bank[:, s], Bt[:, t, g * P:(g + 1) * P], xend[:, t % 2, s], start=True, stop=True)
                last.then_inc(*stepped.up())
            scores(0)
            for t in range(NT):
                if t + 1 < NT:
                    scores(t + 1)
                outputs(t)

        @block.vector
        def _(dve):
            link = linker(dve, core.vchain)
            dve.wait_ge(*core.dma.at(16))
            nc.vector.memset(state[:], 0.0).then_inc(*moved.up())

            def exponents(t):
                dve.wait_ge(*core.ready.at(t + 1))
                for half in range(2):
                    link(nc.vector.tensor_tensor(decay[:, t % 2, 4 * half:4 * half + 4, :],
                                                 rows[half][:].rearrange("p (h c) -> p h c", h=4),
                                                 causal[:].unsqueeze(1).to_broadcast([P, 4, P]), ALU.add))
                nc.vector.tensor_tensor(decay[:, t % 2], decay[:, t % 2], hb(cum, t, P), ALU.subtract).then_inc(*spread.up())
                link(nc.vector.tensor_tensor(per(xdt[:, t % 2, :]), per(x[:, t, :]), hb(dt, t, HD), ALU.mult))
                nc.vector.tensor_tensor(per(xend[:, t % 2, :]), per(xdt[:, t % 2, :]), hb(e_rest, t, HD), ALU.mult).then_inc(*used.up())
                dve.wait_ge(*exped.at(t + 1))
                for g in range(2):
                    d = decay[:, t % 2, 4 * g:4 * g + 4, :]
                    ins = nc.vector.tensor_tensor(d, d, cb[:, g * P:(g + 1) * P].unsqueeze(1).to_broadcast([P, 4, P]), ALU.mult)
                ins.then_inc(*scaled.up())

            def collect(t):
                dve.wait_ge(*stepped.at(t + 1))
                link(nc.vector.tensor_tensor(per(y[:, t, :]), per(y_off[:]), hb(e_cum, t, HD), ALU.mult))
                link(nc.vector.tensor_tensor(y[:, t, :], y[:, t, :], y_in[:], ALU.add))
                link(nc.vector.tensor_tensor(per(part[:]), per(x[:, t, :]),
                                             skip[:].unsqueeze(2).to_broadcast([P, H, HD]), ALU.mult))
                link(nc.vector.tensor_tensor(y[:, t, :], y[:, t, :], part[:], ALU.add))
                if t == 0:
                    dve.wait_ge(*moved.at(1))
                link(nc.vector.tensor_tensor(per(state[:]), per(state[:]), hb(e_total, t, HD), ALU.mult))
                nc.vector.tensor_tensor(state[:], state[:], s_bank[:], ALU.add).then_inc(*moved.up())
                dve.wait_ge(*moved.at(t + 2))
            exponents(0)
            for t in range(NT):
                if t + 1 < NT:
                    exponents(t + 1)
                collect(t)

        @block.scalar
        def _(act):
            for t in range(NT):
                act.wait_ge(*spread.at(t + 1))
                nc.scalar.activation(decay[:, t % 2], decay[:, t % 2], ACT.Exp).then_inc(*exped.up())
    inner.close()
    st.close()


def attention(core, jobs, tables=()):
    nc = core.nc
    st = ExitStack()
    s_bank = [core.ps(st, f"scores{b}") for b in range(3)]
    t_bank = [core.ps(st, f"turned{b}") for b in range(3)]
    o_bank = [core.ps(st, f"mixed{b}") for b in range(2)]
    sc = core.sb(st, "biased", [P, 3, SEQ])
    pr = core.sb(st, "probs", [P, 3, SEQ])
    prT = core.sb(st, "probsT", [P, 3, SEQ])
    neg = core.sb(st, "neg_max", [P, 8])
    den = core.sb(st, "row_sum", [P, 8])
    inv = core.sb(st, "inverse", [P, 8])
    names = ("att_scored", "att_maxed", "att_exped", "att_transposed", "att_turned", "att_mixed", "att_written", "att_table",
             "att_inverted", "att_factor")
    scored, maxed, exped, transposed, turned, mixed, written, tabled, inverted, factored = (core.sig(x) for x in names)
    n = len(jobs)
    with core.block() as block:
        @block.gpsimd
        def _(pool):
            link = linker(pool, core.gchain)
            for after, build in tables:
                if after > 0:
                    pool.wait_ge(*maxed.at(after))
                build(link).then_inc(*tabled.up())

        @block.tensor
        def _(pe):
            def scores(j):
                if j >= 3:
                    pe.wait_ge(*maxed.at(j - 2))
                job = jobs[j]
                sum_of(nc, s_bank[j % 3][:, 0:job["n"]], list(zip(job["q"], job["k"]))).then_inc(*scored.up())

            def turn(j):
                pe.wait_ge(*exped.at(j + 1))
                if j >= 3:
                    pe.wait_ge(*turned.at(j - 2))
                job = jobs[j]
                for c in range(-(-job["n"] // P)):
                    w = min(P, job["n"] - c * P)
                    last = nc.tensor.transpose(t_bank[j % 3][0:w, c * P:(c + 1) * P],
                                               pr[:, j % 3, c * P:c * P + w], core.ident)
                last.then_inc(*transposed.up())

            def mix(j):
                pe.wait_ge(*turned.at(j + 1))
                if j >= 2:
                    pe.wait_ge(*written.at(j - 1))
                job = jobs[j]
                sum_of(nc, o_bank[j % 2][:, 0:job["dv"]],
                       [(prT[0:rows, j % 3, c * P:(c + 1) * P], v) for c, (rows, v) in enumerate(job["v"])]
                       ).then_inc(*mixed.up())
            for j in range(n + 4):
                if j < n:
                    scores(j)
                if 2 <= j < n + 2:
                    turn(j - 2)
                if j >= 4:
                    mix(j - 4)

        @block.vector
        def _(dve):
            link = linker(dve, core.vchain)

            def maximum(j):
                job = jobs[j]
                w = job["n"]
                dve.wait_ge(*scored.at(j + 1))
                if job.get("table") is not None:
                    dve.wait_ge(*tabled.at(job["table"] + 1))
                if j >= 3:
                    dve.wait_ge(*exped.at(j - 2))
                i = j % 8
                nc.vector.tensor_tensor_reduce(sc[:, j % 3, 0:w], s_bank[j % 3][:, 0:w], job["bias"], 1.0, 1e20,
                                               ALU.add, ALU.min, neg[:, i:i + 1]).then_inc(*maxed.up())

            def inverse(j):
                i = j % 8
                dve.wait_ge(*exped.at(j + 1))
                if jobs[j].get("may_lack_keys"):
                    link(nc.vector.tensor_scalar(den[:, i:i + 1], den[:, i:i + 1], 1e-30, None, ALU.max))
                nc.vector.reciprocal(inv[:, i:i + 1], den[:, i:i + 1]).then_inc(*inverted.up())

            def factor(j):
                i = j % 8
                if jobs[j]["gate"] is not None:
                    dve.wait_ge(*inverted.at(j + 1))
                    nc.vector.tensor_scalar(inv[:, i:i + 1], inv[:, i:i + 1], jobs[j]["gate"], None, ALU.mult
                                            ).then_inc(*factored.up())

            gated_jobs = [sum(job["gate"] is not None for job in jobs[:j + 1]) for j in range(n)]

            def output(j):
                job = jobs[j]
                i = j % 8
                dve.wait_ge(*mixed.at(j + 1))
                dve.wait_ge(*inverted.at(j + 1))
                if job["gate"] is not None:
                    dve.wait_ge(*factored.at(gated_jobs[j]))
                o = o_bank[j % 2][:, 0:job["dv"]]
                if job["add"]:
                    dve.wait_ge(*written.at(j))
                    ins = nc.vector.scalar_tensor_tensor(out=job["out"], in0=o, scalar=inv[:, i:i + 1], in1=job["out"],
                                                         op0=ALU.mult, op1=ALU.add)
                else:
                    ins = nc.vector.tensor_scalar(job["out"], o, inv[:, i:i + 1], None, ALU.mult)
                ins.then_inc(*written.up())
            for j in range(n + 4):
                if 3 <= j < n + 3:
                    inverse(j - 3)
                if j < n:
                    maximum(j)
                if 3 <= j < n + 3:
                    factor(j - 3)
                if j >= 4:
                    output(j - 4)

        @block.scalar
        def _(act):
            def exponentials(j):
                w = jobs[j]["n"]
                i = j % 8
                act.wait_ge(*maxed.at(j + 1))
                if j >= 3:
                    act.wait_ge(*transposed.at(j - 2))
                nc.scalar.activation(pr[:, j % 3, 0:w], sc[:, j % 3, 0:w], ACT.Exp, bias=neg[:, i:i + 1], scale=-1.0,
                                     accum_out=den[:, i:i + 1]).then_inc(*exped.up())

            def keep(j):
                job = jobs[j]
                act.wait_ge(*transposed.at(j + 1))
                if j >= 3:
                    act.wait_ge(*mixed.at(j - 2))
                c = -(-job["n"] // P)
                rows = min(P, job["n"])
                nc.scalar.copy(prT[0:rows, j % 3, 0:c * P], t_bank[j % 3][0:rows, 0:c * P]).then_inc(*turned.up())
            for j in range(n + 2):
                if j >= 2:
                    keep(j - 2)
                if j < n:
                    exponentials(j)
    st.close()


def band_of(table, tile, n):
    at = (NT - 1 - tile) * P
    return table[:, at:at + n]


def nsa(core, stream, hT, gates, y):
    nc, ins = core.nc, core.ins
    st = ExitStack()
    HD = 64
    qT = core.sb(st, "qT", [P, 8, SEQ])
    ksT = core.sb(st, "ksT", [P, SEQ])
    kwT = core.sb(st, "kwT", [P, SEQ])
    vs = core.sb(st, "vs", [P, NT, P])
    vw = core.sb(st, "vw", [P, NT, P])
    kcmpT = core.sb(st, "kcmpT", [P, 32])
    vcmp = core.sb(st, "vcmp", [32, P])
    inner = ExitStack()
    cT = {c: core.sb(inner, f"{c}T", [P, 2, SEQ]) for c in ("kc", "vc")}
    w1 = {c: core.sb(inner, f"w_{c}1", [P, 16, HD]) for c in ("k", "v")}
    w2 = {c: core.sb(inner, f"w_{c}2", [HD, HD]) for c in ("k", "v")}
    pos = {c: core.sb(inner, f"pos_{c}", [P, 16]) for c in ("k", "v")}
    fetched = core.sig("compress_weights_landed")
    with core.block() as block:
        @block.sync
        def _(sp):
            for c in ("k", "v"):
                for dst, src in ((w1[c], ins[f"w_c{c}1"]), (w2[c], ins[f"w_c{c}2"][0]), (pos[c], ins[f"cmp_pos_{c}"])):
                    sp.dma_start(dst[:], src).then_inc(*fetched.up(16))
    jobs = []
    for h in range(4):
        def read(link, bank, h=h):
            nc.vector.memset(qT[HD:P, h, :], 0.0)
            nc.vector.memset(qT[0:HD, h + 4, :], 0.0)
            link(nc.vector.tensor_scalar(qT[0:HD, h, :], bank[0:HD, :], -HD ** -0.5, None, ALU.mult))
            return nc.vector.tensor_scalar(qT[HD:P, h + 4, :], bank[HD:P, :], -HD ** -0.5, None, ALU.mult)
        jobs.append(("nsa_q", channel_major(core, stream, hT, "nsa_q", h * P, P), "v", read))
    for i, c in enumerate(("kc", "vc")):
        for g in range(2):
            def read(link, bank, c=c, g=g):
                link(nc.scalar.copy(cT[c][0:HD, g, :], bank[0:HD, :]))
                return nc.scalar.copy(cT[c][HD:P, g, 0:SEQ - 1], bank[0:HD, 1:SEQ])
            jobs.append(("nsa_kv", channel_major(core, stream, hT, "nsa_kv", i * P + g * HD, HD), "a", read))
    jobs.append(("nsa_kv", channel_major(core, stream, hT, "nsa_kv", 2 * P, P), "v",
                 lambda link, bank: nc.vector.tensor_copy(ksT[:], bank[:])))
    for t in range(NT):
        jobs.append(("nsa_kv", token_major(core, stream, hT, "nsa_kv", t, 3 * P, P), "a",
                     lambda link, bank, t=t: nc.scalar.copy(vs[:, t, :], bank[:, 0:P])))
    jobs.append(("nsa_w", channel_major(core, stream, hT, "nsa_w", 0, P), "v",
                 lambda link, bank: nc.vector.tensor_copy(kwT[:], bank[:])))
    for t in range(NT):
        jobs.append(("nsa_w", token_major(core, stream, hT, "nsa_w", t, P, P), "a",
                     lambda link, bank, t=t: nc.scalar.copy(vw[:, t, :], bank[:, 0:P])))
    product_block(core, jobs, stream)

    hid = {c: core.sb(inner, f"hidden_{c}", [HD, 2, N_CMP]) for c in ("k", "v")}
    pb = core.sb(inner, "pos_bias", [HD, 2])
    jobs = []
    for i, c in enumerate(("k", "v")):
        jobs.append((None, lambda bank, c=c: sum_of(nc, bank[0:HD, 0:1], [(w1[c][:, l, :], pos[c][:, l:l + 1]) for l in range(16)]),
                     "a", lambda link, bank, i=i: nc.scalar.copy(pb[:, i:i + 1], bank[0:HD, 0:1])))
    for i, c in enumerate(("k", "v")):
        def fill(bank, c=c):
            src = cT["kc" if c == "k" else "vc"]
            return sum_of(nc, bank[0:HD, 0:2 * N_CMP].rearrange("p (g b) -> p g b", g=2),
                          [(w1[c][:, l, :], src[:, :, 2 * l:2 * l + 16 * (N_CMP - 1) + 1:16]) for l in range(16)])

        def read(link, bank, i=i, c=c):
            act_wait()
            return nc.scalar.activation(hid[c][:].rearrange("p g b -> p (g b)"), bank[0:HD, 0:2 * N_CMP], ACT.Silu,
                                        bias=pb[:, i:i + 1])

        def act_wait():
            nc.scalar.wait_ge(*core.afree.at(2))
        jobs.append((None, fill, "a", read))
    product_block(core, jobs, early=fetched)
    jobs = [(None, lambda bank, g=g: nc.tensor.matmul(bank[g * HD:(g + 1) * HD, 0:N_CMP], w2["k"][:], hid["k"][:, g, :],
                                                      start=True, stop=True), "v",
             lambda link, bank, g=g: nc.vector.tensor_copy(kcmpT[g * HD:(g + 1) * HD, 0:N_CMP], bank[g * HD:(g + 1) * HD, 0:N_CMP]))
            for g in range(2)]
    jobs += [(None, lambda bank, g=g: nc.tensor.matmul(bank[0:N_CMP, 0:HD], hid["v"][:, g, :], w2["v"][:], start=True, stop=True),
              "v", lambda link, bank, g=g: nc.vector.tensor_copy(vcmp[0:N_CMP, g * HD:(g + 1) * HD], bank[0:N_CMP, 0:HD]))
             for g in range(2)]
    product_block(core, jobs)
    inner.close()

    inner = ExitStack()
    dist = core.sb(inner, "causal_dist", [P, BAND])
    cdist = core.sb(inner, "cmp_dist", [P, NT * 32])
    table = core.sb(inner, "bias_tables", [P, 2, BAND])
    ctable = core.sb(inner, "cmp_tables", [P, 2, NT * 32])
    with core.block() as block:
        @block.sync
        def _(sp):
            sp.dma_start(dist[:], core.const("causal_dist")).then_inc(*core.dma.up(16))
            sp.dma_start(cdist[:], core.const("cmp_dist")).then_inc(*core.dma.up(16))
            sp.wait_ge(*core.dma.at(32))
    jobs, tables = [], []
    for h in range(8):
        g, lo = h // 4, (h // 4) * HD
        rows = slice(lo, lo + HD)

        def build(link, h=h):
            link(nc.gpsimd.tensor_scalar(table[:, h % 2, :], dist[:], SLOPES[h], None, ALU.mult))
            return nc.gpsimd.tensor_scalar(ctable[:, h % 2, :], cdist[:], SLOPES[h], None, ALU.mult)
        tables.append((12 * (h - 1) if h >= 2 else 0, build))
        for t in range(NT):
            q = [qT[:, h, t * P:(t + 1) * P]]
            out = y[:, t, h * HD:(h + 1) * HD]
            jobs.append(dict(q=q, k=[kcmpT[:, 0:N_CMP]], n=N_CMP, bias=ctable[:, h % 2, t * 32:t * 32 + N_CMP],
                             v=[(N_CMP, vcmp[0:N_CMP, rows])], dv=HD, out=out, gate=gates[:, t, 3 * h:3 * h + 1], add=False, table=h,
                             may_lack_keys=True))
            for b, (kT, vv) in enumerate(((ksT, vs), (kwT, vw))):
                n = (t + 1) * P
                jobs.append(dict(q=q, k=[kT[:, 0:n]], n=n, bias=band_of(table[:, h % 2, :], t, n),
                                 v=[(P, vv[:, c, rows]) for c in range(t + 1)], dv=HD, out=out,
                                 gate=gates[:, t, 3 * h + 1 + b:3 * h + 2 + b], add=True, table=h))
    attention(core, jobs, tables)
    inner.close()
    st.close()


def project_out(core, stream, srcT, items, dst, add):
    nc = core.nc
    jobs = []
    for half, item in enumerate(items):
        for t in range(NT):
            d = dst[:, t, half * SEQ:(half + 1) * SEQ]
            if add:
                read = lambda link, bank, d=d: nc.vector.tensor_tensor(d, d, bank[:], ALU.add)
                e = "v"
            else:
                e = "va"[t % 2]
                read = lambda link, bank, d=d, e=e: copy_on(nc, e, d, bank[:])
            jobs.append((item, token_major(core, stream, srcT, item, t, 0, SEQ), e, read))
    product_block(core, jobs, stream)


def post_norm_residual(core, x, out, gain):
    nc = core.nc
    rms_rows(core, out, NT, out)
    with core.block() as block:
        @block.vector
        def _(dve):
            link = linker(dve, core.vchain)
            for t in range(NT):
                link(nc.vector.tensor_tensor(out[:, t, :], out[:, t, :], gain, ALU.mult))
                nc.vector.tensor_tensor(x[:, t, :], x[:, t, :], out[:, t, :], ALU.add)


def mixer(core, stream, hT, y):
    nc, ins = core.nc, core.ins
    st = ExitStack()
    HD = 64
    qT = core.sb(st, "qT", [P, 4, SEQ])
    kT = core.sb(st, "kT", [P, 4, SEQ])
    v = core.sb(st, "v", [P, NT, SEQ])
    half_ones = core.sb(st, "half_ones", [P, P])
    gq = core.sb(st, "gain_q", [P, 2])
    jobs = []
    for item, dst in (("mix_q", qT), ("mix_k", kT)):
        for c in range(4):
            jobs.append((item, channel_major(core, stream, hT, item, c * P, P), "va"[c % 2],
                         lambda link, bank, dst=dst, c=c: copy_on(nc, "va"[c % 2], dst[:, c, :], bank[:])))
    for t in range(NT):
        jobs.append(("mix_v", token_major(core, stream, hT, "mix_v", t, 0, SEQ), "va"[t % 2],
                     lambda link, bank, t=t: copy_on(nc, "va"[t % 2], v[:, t, :], bank[:])))
    product_block(core, jobs, stream, loads=[(half_ones[:], core.const("half_ones")), (gq[:], ins["mix_qk_gain"])])
    with core.block() as block:
        @block.vector
        def _(dve):
            nc.vector.tensor_scalar(gq[:, 0:1], gq[:, 0:1], -HD ** -0.5, None, ALU.mult)
    norm_channels(core, [[qT[:, c, :]] for c in range(4)] + [[kT[:, c, :]] for c in range(4)], half_ones[:],
                  core.eps[:, 0:1], [gq[:, 0:1]] * 4 + [gq[:, 1:2]] * 4, HD)
    inner = ExitStack()
    qz = core.sb(inner, "head_qT", [P, 8, SEQ])
    by_pair = qz[:].rearrange("p (c two) s -> p c two s", two=2)
    dist = core.sb(inner, "mix_dist", [P, BAND])
    logs = core.sb(inner, "mix_log", [P, BAND])
    table = core.sb(inner, "bias_tables", [P, 2, BAND])
    with core.block() as block:
        @block.sync
        def _(sp):
            sp.dma_start(dist[:], core.const("mix_dist")).then_inc(*core.dma.up(16))
            sp.dma_start(logs[:], core.const("mix_log")).then_inc(*core.dma.up(16))
            sp.wait_ge(*core.dma.at(32))

        @block.vector
        def _(dve):
            nc.vector.memset(by_pair[HD:P, :, 0, :], 0.0)
            nc.vector.tensor_copy(by_pair[0:HD, :, 0, :], qT[0:HD, :, :])

        @block.scalar
        def _(act):
            nc.scalar.copy(by_pair[HD:P, :, 1, :], qT[HD:P, :, :])

        @block.gpsimd
        def _(pool):
            nc.gpsimd.memset(by_pair[0:HD, :, 1, :], 0.0)
    jobs, tables = [], []
    for h in range(8):

        def build(link, h=h):
            link(nc.gpsimd.tensor_scalar(table[:, h % 2, :], dist[:], SLOPES[h], None, ALU.mult))
            return nc.gpsimd.tensor_tensor(table[:, h % 2, :], table[:, h % 2, :], logs[:], ALU.add)
        tables.append((4 * (h - 1) if h >= 2 else 0, build))
        for t in range(NT):
            jobs.append(dict(q=[qz[:, h, t * P:(t + 1) * P]], k=[kT[:, h // 2, :]], n=SEQ,
                             bias=band_of(table[:, h % 2, :], t, SEQ), v=[(P, v[:, c, h * HD:(h + 1) * HD]) for c in range(NT)],
                             dv=HD, out=y[:, t, h * HD:(h + 1) * HD], gate=None, add=False, table=h))
    attention(core, jobs, tables)
    inner.close()
    st.close()

    st = ExitStack()
    H = 4
    q = core.sb(st, "rqT", [P, H, SEQ])
    k = core.sb(st, "rkT", [P, H, SEQ])
    v = core.sb(st, "rv", [P, NT, SEQ])
    ahead = core.sb(st, "ahead", [P, BAND])
    behind = core.sb(st, "behind", [P, BAND])
    lg = core.sb(st, "log_gamma", [P, 8])
    mag = core.sb(st, "mag", [P, 8])
    gn = core.sb(st, "gn_gain", [P, SEQ])
    table = core.sb(st, "decays", [P, H, BAND])
    jobs = []
    for i, (dst, s) in enumerate(((q, 1.0), (k, HD ** -0.5))):
        for h in range(H):
            jobs.append(("mix_rqk", channel_major(core, stream, hT, "mix_rqk", i * 256 + h * HD, HD), "v",
                         lambda link, bank, dst=dst, h=h, s=s: nc.vector.tensor_scalar(dst[0:HD, h, :], bank[0:HD, :], s, None, ALU.mult)))
    for t in range(NT):
        jobs.append(("mix_rv", token_major(core, stream, hT, "mix_rv", t, 0, SEQ), "a",
                     lambda link, bank, t=t: nc.scalar.copy(v[:, t, :], bank[:])))
    product_block(core, jobs, stream, loads=[
        (lg[:, 0:4], ins["ret_decay_f_2"].to_broadcast([P, 4])), (lg[:, 4:8], ins["ret_decay_b_2"].to_broadcast([P, 4])),
        (ahead[:], core.const("ahead")), (behind[:], core.const("behind")), (gn[:], ins["ret_gn_w_2"].to_broadcast([P, SEQ]))])
    logged, summed = core.sig("lg_logged"), core.sig("lg_tables")
    with core.block() as block:
        @block.vector
        def _(dve):
            link = linker(dve, core.vchain)
            nc.vector.memset(q[HD:P, :, :], 0.0)
            nc.vector.memset(k[HD:P, :, :], 0.0)
            dve.wait_ge(*logged.at(1))
            link(nc.vector.scalar_tensor_tensor(out=lg[:], in0=lg[:], scalar=0.0, in1=mag[:], op0=ALU.min, op1=ALU.subtract))
            for h in range(H):
                link(nc.vector.tensor_scalar(table[:, h, :], ahead[:], lg[:, h:h + 1], None, ALU.mult))
                nc.vector.scalar_tensor_tensor(out=table[:, h, :], in0=behind[:], scalar=lg[:, 4 + h:5 + h], in1=table[:, h, :],
                                               op0=ALU.mult, op1=ALU.add).then_inc(*summed.up())

        @block.scalar
        def _(act):
            link = linker(act, core.achain)
            link(nc.scalar.activation(mag[:], lg[:], ACT.Abs))
            link(nc.scalar.activation(mag[:], mag[:], ACT.Exp, scale=-1.0))
            nc.scalar.activation(mag[:], mag[:], ACT.Ln, bias=core.one[:, 0:1]).then_inc(*logged.up())
            for h in range(H):
                act.wait_ge(*summed.at(h + 1))
                nc.scalar.activation(table[:, h, :], table[:, h, :], ACT.Exp)
    inner = ExitStack()
    s_bank = [core.ps(inner, f"scores{b}") for b in range(4)]
    y_bank = [core.ps(inner, f"y{b}") for b in range(NT)]
    sT = core.sb(inner, "scoresT", [P, 2, NT, SEQ])
    scored, decayed, mixed, written = core.sig("ret_scored"), core.sig("ret_decayed"), core.sig("ret_mixed"), core.sig("ret_written")
    with core.block() as block:
        @block.tensor
        def _(pe):
            def scores(h):
                for t in range(NT):
                    j = h * NT + t
                    if j >= 4:
                        pe.wait_ge(*decayed.at(j - 3))
                    nc.tensor.matmul(s_bank[j % 4][:], k[:, h, t * P:(t + 1) * P], q[:, h, :], start=True, stop=True
                                     ).then_inc(*scored.up())

            def mix(h):
                pe.wait_ge(*decayed.at((h + 1) * NT))
                for i in range(NT):
                    j = h * NT + i
                    if h > 0:
                        pe.wait_ge(*written.at(j - NT + 1))
                    sum_of(nc, y_bank[i][:, 0:P], [(sT[:, h % 2, t, i * P:(i + 1) * P], v[:, t, h * P:(h + 1) * P]) for t in range(NT)]
                           ).then_inc(*mixed.up())
            scores(0)
            for h in range(H):
                if h + 1 < H:
                    scores(h + 1)
                mix(h)

        @block.vector
        def _(dve):
            for j in range(H * NT):
                h, t = j // NT, j % NT
                dve.wait_ge(*scored.at(j + 1))
                if h >= 2:
                    dve.wait_ge(*mixed.at((h - 1) * NT))
                nc.vector.tensor_tensor(sT[:, h % 2, t, :], s_bank[j % 4][:], band_of(table[:, h, :], t, SEQ), ALU.mult
                                        ).then_inc(*decayed.up())

        @block.scalar
        def _(act):
            for j in range(H * NT):
                h, i = j // NT, j % NT
                act.wait_ge(*mixed.at(j + 1))
                nc.scalar.copy(y[:, i, SEQ + h * P:SEQ + (h + 1) * P], y_bank[i][:, 0:P]).then_inc(*written.up())
    inner.close()
    ret = y[:, :, SEQ:2 * SEQ]
    mean = core.sb(st, "mean", [P, NT, H])
    with core.block() as block:
        @block.vector
        def _(dve):
            link = linker(dve, core.vchain)
            for t in range(NT):
                r = ret[:, t, :].rearrange("p (h w) -> p h w", h=H)
                link(nc.vector.tensor_reduce(mean[:, t, :], r, AX.X, ALU.add))
                link(nc.vector.tensor_scalar(mean[:, t, :], mean[:, t, :], 1.0 / P, None, ALU.mult))
                nc.vector.tensor_tensor(r, r, mean[:, t, :].unsqueeze(2).to_broadcast([P, H, P]), ALU.subtract)
    saved, core.eps = core.eps, core.gn_eps
    gate_with_z(core, stream, hT, "mix_rg", ret, (H, P, gn[:].rearrange("p (h w) -> p h w", h=H)))
    core.eps = saved
    st.close()


def cross_attention(core, stream, hT, memT, yT_or_y):
    nc, ins = core.nc, core.ins
    y = yT_or_y
    st = ExitStack()
    H, HD = 4, 256
    qT = core.sb(st, "qT", [P, 8, SEQ])
    kT = core.sb(st, "kT", [P, 8, N_MEM])
    v = core.sb(st, "v", [P, 2, D])
    g = core.sb(st, "gains", [P, 4])
    zero = core.sb(st, "zero", [P, N_MEM])
    jobs = []
    for half in range(2):
        for c in range(4):
            jobs.append((f"mem_q{half}", channel_major(core, stream, hT, f"mem_q{half}", c * P, P), "va"[c % 2],
                         lambda link, bank, i=half * 4 + c: copy_on(nc, "va"[i % 2], qT[:, i, :], bank[:])))
    for half in range(2):
        for c in range(4):
            jobs.append((f"mem_k{half}", channel_major(core, stream, memT, f"mem_k{half}", c * P, P, N_MEM), "va"[c % 2],
                         lambda link, bank, i=half * 4 + c: copy_on(nc, "va"[i % 2], kT[:, i, :], bank[:, 0:N_MEM])))
    for half in range(2):
        for t in range(2):
            jobs.append((f"mem_v{half}", token_major(core, stream, memT, f"mem_v{half}", t, 0, SEQ), "va"[t % 2],
                         lambda link, bank, half=half, t=t: copy_on(nc, "va"[t % 2], v[:, t, half * SEQ:(half + 1) * SEQ], bank[:])))
    product_block(core, jobs, stream, loads=[(g[:], ins["mem_qk_gain"])])
    with core.block() as block:
        @block.vector
        def _(dve):
            nc.vector.memset(zero[:], 0.0)
            nc.vector.tensor_scalar(g[:, 0:2], g[:, 0:2], -HD ** -0.5, None, ALU.mult)
    norm_channels(core, [[qT[:, 2 * h, :], qT[:, 2 * h + 1, :]] for h in range(H)], core.ones, core.eps[:, 0:1],
                  [g[:, 0:1], g[:, 1:2]] * H, HD)
    norm_channels(core, [[kT[:, 2 * h, :], kT[:, 2 * h + 1, :]] for h in range(H)], core.ones, core.eps[:, 0:1],
                  [g[:, 2:3], g[:, 3:4]] * H, HD, ntok=N_MEM)
    jobs = []
    for h in range(H):
        for t in range(NT):
            jobs.append(dict(q=[qT[:, 2 * h + i, t * P:(t + 1) * P] for i in range(2)], k=[kT[:, 2 * h + i, :] for i in range(2)],
                             n=N_MEM, bias=zero[:], v=[(P, v[:, c, h * HD:(h + 1) * HD]) for c in range(2)], dv=HD,
                             out=y[:, t, h * HD:(h + 1) * HD], gate=None, add=False))
    attention(core, jobs)
    st.close()


def route(core, hT, w_route, iota, below, slots, gates, over_expert):
    nc = core.nc
    st = ExitStack()
    sb = lambda n, s, dt=F32: core.sb(st, n, s, dt)
    glog, elog = sb("group_logits", [P, NT, 8]), sb("expert_logits", [P, NT, N_EXPERTS])
    g8, gi, e8, ei = sb("g8", [P, NT, 8]), sb("gi", [P, NT, 8], U32), sb("e8", [P, NT, 8]), sb("ei", [P, NT, 8], U32)
    gf, hot, own, part = sb("gf", [P, NT]), sb("hot", [P, NT, 4]), sb("own", [P, NT, 8]), sb("part", [P, NT, 8])
    ef = sb("ef", [P, NT, 2])
    pick = [sb(f"pick{c}", [P, NT, N_EXPERTS]) for c in range(2)]
    both = sb("both", [P, NT, N_EXPERTS])
    jobs = []
    for t in range(NT):
        def fill(bank, t=t):
            return sum_of(nc, bank[:, 0:36], [(hT[:, k, t * P:(t + 1) * P], w_route[:, k, :]) for k in range(KD)])

        def read(link, bank, t=t):
            link(nc.vector.tensor_copy(glog[:, t, 0:4], bank[:, 0:4]))
            link(nc.vector.memset(glog[:, t, 4:8], MASKED))
            return nc.vector.tensor_copy(elog[:, t, :], bank[:, 4:36])
        jobs.append((None, fill, "v", read))
    product_block(core, jobs, early=core.sig("route_weights_landed"))

    bc = lambda ap, n: ap.unsqueeze(2).to_broadcast([P, NT, n])
    row = lambda a, n: iota[:, a:a + n].unsqueeze(1).to_broadcast([P, NT, n])
    diff, gsum = sb("diff", [P, NT]), sb("gsum", [P, NT])
    gexp = sb("gexp", [P, NT, 4])
    chosen, exped = core.sig("route_chosen"), core.sig("route_exped")
    with core.block() as block:
        @block.vector
        def _(dve):
            link = linker(dve, core.vchain)
            for t in range(NT):
                link(nc.vector.max(g8[:, t, :], glog[:, t, :]))
                link(nc.vector.max_index(gi[:, t, :], g8[:, t, :], glog[:, t, :]))
            link(nc.vector.tensor_copy(gf[:], gi[:, :, 0]))
            link(nc.vector.tensor_tensor(hot[:], row(0, 4), bc(gf[:], 4), ALU.is_equal))
            for g in range(N_GROUPS):
                dst = own if g == 0 else part
                link(nc.vector.tensor_tensor(dst[:], elog[:, :, 8 * g:8 * g + 8], hot[:, :, g:g + 1].to_broadcast([P, NT, 8]), ALU.mult))
                if g:
                    link(nc.vector.tensor_tensor(own[:], own[:], part[:], ALU.add))
            for t in range(NT):
                link(nc.vector.max(e8[:, t, :], own[:, t, :]))
                link(nc.vector.max_index(ei[:, t, :], e8[:, t, :], own[:, t, :]))
            link(nc.vector.tensor_tensor(diff[:], e8[:, :, 1], e8[:, :, 0], ALU.subtract))
            link(nc.vector.tensor_tensor(gexp[:], glog[:, :, 0:4], g8[:, :, 0:1].to_broadcast([P, NT, 4]), ALU.subtract))
            link(nc.vector.tensor_copy(ef[:], ei[:, :, 0:2]))
            nc.vector.tensor_scalar(gf[:], gf[:], 8.0, None, ALU.mult).then_inc(*chosen.up())
            dve.wait_ge(*chosen.at(1))
            link(nc.vector.tensor_tensor(ef[:], ef[:], bc(gf[:], 2), ALU.add))
            for c in range(2):
                link(nc.vector.tensor_tensor(pick[c][:], row(0, N_EXPERTS), ef[:, :, c:c + 1].to_broadcast([P, NT, N_EXPERTS]), ALU.is_equal))
            link(nc.vector.tensor_tensor(both[:], pick[0][:], pick[1][:], ALU.add))
            dve.wait_ge(*exped.at(1))
            link(nc.vector.tensor_reduce(gsum[:], gexp[:], AX.X, ALU.add))
            link(nc.vector.scalar_tensor_tensor(out=gsum[:], in0=diff[:], scalar=1.0, in1=gsum[:], op0=ALU.add, op1=ALU.mult))
            link(nc.vector.reciprocal(gates[:, :, 0], gsum[:]))
            nc.vector.tensor_tensor(gates[:, :, 1], gates[:, :, 0], diff[:], ALU.mult)

        @block.scalar
        def _(act):
            act.wait_ge(*chosen.at(1))
            nc.scalar.activation(diff[:], diff[:], ACT.Exp)
            nc.scalar.activation(gexp[:], gexp[:], ACT.Exp).then_inc(*exped.up())

    rank_bank, cnt_bank, base_bank = (core.ps(st, n) for n in ("ranks", "counts", "bases"))
    rank, cnt = sb("rank", [P, NT, N_EXPERTS]), sb("cnt", [N_EXPERTS, 1])
    more, over, incl = sb("more", [N_EXPERTS, 8]), sb("over", [N_EXPERTS, 1]), sb("incl", [N_EXPERTS, 1])
    past = sb("past", [N_EXPERTS, N_OVER])
    first, later = sb("first", [P, N_EXPERTS]), sb("later", [P, N_EXPERTS])
    slot = sb("slot", [P, NT, N_EXPERTS])
    fblock = sb("fblock", [1, N_OVER + 1])
    ranked, counted, based, compared, listed = (core.sig(n) for n in (
        "ranks_ready", "overflow_counted", "bases_ready", "blocks_compared", "blocks_ready"))
    E = N_EXPERTS
    with core.block() as block:
        @block.tensor
        def _(pe):
            for t in range(NT):
                sum_of(nc, rank_bank[:, t * E:(t + 1) * E],
                       [(core.ones, both[:, u, :]) for u in range(t)] + [(below[:], both[:, t, :])])
            sum_of(nc, cnt_bank[0:E, 0:1], [(both[:, t, :], core.ones[:, 0:1]) for t in range(NT)]).then_inc(*ranked.up())
            pe.wait_ge(*counted.at(1))
            nc.tensor.matmul(base_bank[:, 0:E], over[:, 0:1].to_broadcast([E, P]), below[0:E, 0:E], start=True, stop=True)
            nc.tensor.matmul(base_bank[0:E, E:E + 1], core.upto[0:E, 0:E], over[:], start=True, stop=True).then_inc(*based.up())
            pe.wait_ge(*compared.at(1))
            nc.tensor.matmul(cnt_bank[0:1, 8:8 + N_OVER], core.ones[0:E, 0:1], past[:], start=True, stop=True)
            nc.tensor.matmul(cnt_bank[0:1, 8 + N_OVER:9 + N_OVER], core.ones[0:E, 0:1], over[:], start=True, stop=True
                             ).then_inc(*listed.up())

        @block.vector
        def _(dve):
            link = linker(dve, core.vchain)
            dve.wait_ge(*ranked.at(1))
            link(nc.vector.tensor_copy(cnt[:], cnt_bank[0:E, 0:1]))
            link(nc.vector.tensor_scalar(more[:], iota[0:E, 1:9], float(SLOTS), cnt[:, 0:1], ALU.mult, ALU.is_lt))
            nc.vector.tensor_reduce(over[:], more[:], AX.X, ALU.add).then_inc(*counted.up())
            link(nc.vector.tensor_copy(rank[:].rearrange("p t e -> p (t e)"), rank_bank[:, 0:NT * E]))
            link(nc.vector.tensor_scalar(first[:], iota[:, 0:E], float(SLOTS), None, ALU.mult))
            dve.wait_ge(*based.at(1))
            link(nc.vector.tensor_copy(incl[:], base_bank[0:E, E:E + 1]))
            nc.vector.tensor_scalar(past[:], iota[0:E, 0:N_OVER], incl[:, 0:1], None, ALU.is_ge).then_inc(*compared.up())
            link(nc.vector.tensor_scalar(later[:], base_bank[:, 0:E], float(SLOTS), float(SLOTS * (E - 1)), ALU.mult, ALU.add))
            link(nc.vector.tensor_tensor(first[:], first[:], later[:], ALU.subtract))
            link(nc.vector.tensor_scalar(slot[:], rank[:], float(SLOTS), None, ALU.is_lt))
            link(nc.vector.tensor_tensor(slot[:], slot[:], first[:].unsqueeze(1).to_broadcast([P, NT, E]), ALU.mult))
            link(nc.vector.tensor_tensor(slot[:], slot[:], later[:].unsqueeze(1).to_broadcast([P, NT, E]), ALU.add))
            link(nc.vector.tensor_tensor(slot[:], slot[:], rank[:], ALU.add))
            for c in range(2):
                link(nc.vector.tensor_tensor(pick[c][:], pick[c][:], slot[:], ALU.mult))
                link(nc.vector.tensor_reduce(slots[:, :, c], pick[c][:], AX.X, ALU.add))
            dve.wait_ge(*listed.at(1))
            link(nc.vector.tensor_scalar(fblock[:], cnt_bank[0:1, 8:9 + N_OVER], float(E - 1), None, ALU.min))
            nc.vector.tensor_copy(over_expert[:], fblock[:])
    st.close()


def moe(core, x, gain):
    nc, ins = core.nc, core.ins
    st = ExitStack()
    xn = core.sb(st, "xn", [P, NT, D])
    slots = core.sb(st, "slots", [P, NT, 2])
    slot_rows = core.sb(st, "slot_rows", [P, NT, 2], U32)
    gates = core.sb(st, "gates", [P, NT, 2])
    over = core.sb(st, "over_expert", [1, N_OVER + 1], I32)
    expert_rows = nc.dram_tensor("expert_rows", (N_BLOCKS * SLOTS, D), F32).ap()
    w = {"gate": ins["w_exp_gate_2"][0].rearrange("e (k p) n -> e p k n", p=P),
         "up": ins["w_exp_up_2"][0].rearrange("e (k p) n -> e p k n", p=P),
         "down": ins["w_exp_down_2"][0].rearrange("e (k p) n -> e p k n", p=P)}
    kinds = ("gate", "up", "down")
    ring = {(kind, b): core.sb(st, f"{kind}{b}", [P, 4096]) for b in range(2) for kind in kinds}
    view = {(kind, b): ring[kind, b][:].rearrange("p (k n) -> p k n", k=(KD if kind != "down" else 4))
            for b in range(2) for kind in kinds}
    landed = {(kind, b): core.sig(f"expert_{kind}{b}_landed") for b in range(2) for kind in kinds}
    zero = core.sb(st, "zero_rows", [P, D])
    w_route = core.sb(st, "w_route", [P, KD, 36])
    iota = core.sb(st, "iota", [P, P])
    below = core.sb(st, "below", [P, P])
    route_landed = core.sig("route_weights_landed")
    cleared, cleared_dma = core.sig("zero_rows_cleared"), core.sig("overflow_rows_zeroed")
    with core.block() as block:
        @block.vector
        def _(dve):
            nc.vector.memset(zero[:], 0.0).then_inc(*cleared.up())

        @block.sync
        def _(sp):
            for dst, src in ((w_route[:, :, 0:4], ins["w_group_2"][0].rearrange("(k p) n -> p k n", p=P)),
                             (w_route[:, :, 4:36], ins["w_router_2"].rearrange("(k p) n -> p k n", p=P)),
                             (iota[:], core.const("iota")), (below[:], core.const("below"))):
                sp.dma_start(dst, src).then_inc(*route_landed.up(16))
            sp.wait_ge(*cleared.at(1))
            spare = expert_rows[N_EXPERTS * SLOTS:N_BLOCKS * SLOTS, :].rearrange("(r p) d -> p r d", p=P)
            sp.dma_start(spare, zero[:].unsqueeze(1).to_broadcast(spare.shape)).then_inc(*cleared_dma.up(16))
            for e in range(2):
                for kind in kinds:
                    sp.dma_start(view[kind, e], w[kind][e]).then_inc(landed[kind, e].sem, 16)
    inner = ExitStack()
    hT = core.sb(inner, "hT", [P, KD, SEQ])
    norm_to_channels(core, x, NT, gain, hT, keep=xn)
    route(core, hT, w_route, iota, below, slots, gates, over)
    inner.close()

    inner = ExitStack()
    sb = lambda n, s, dt=F32: core.sb(inner, n, s, dt)
    HB = SLOTS
    top_half, low_half = slice(0, HB), slice(HB, P)
    halves = (top_half, low_half)
    landed_mark = sb("landed_mark", [1, 1])
    rel = sb("slot_in_block", [P, NT, 2])
    pick = [[sb(f"pick{b}_{c}", [P, NT, SLOTS]) for c in range(2)] for b in range(2)]
    picked_rows = [sb(f"picked_rows{b}", [P, SEQ]) for b in range(2)]
    xT = [sb(f"xT{b}", [P, KD, SLOTS]) for b in range(2)]
    silu_up = [sb(f"silu{b}", [P, FF]) for b in range(2)]
    inner_act = [sb(f"gated{b}", [P, FF]) for b in range(2)]
    actT = [sb(f"actT{b}", [P, 4, SLOTS]) for b in range(2)]
    rows = [sb(f"rows{b}", [P, SEQ]) for b in range(2)]
    pick_bank = [core.ps(inner, f"picked{b}") for b in range(2)]
    h_bank = [core.ps(inner, f"h{b}") for b in range(2)]
    y_bank = [core.ps(inner, f"y{b}") for b in range(2)]
    xT_bank = core.ps(inner, "xT_turned")
    actT_bank = core.ps(inner, "act_turned")
    names = ("moe_picked", "moe_gathered", "moe_rows_kept", "moe_rows_turned", "moe_tokens", "moe_hidden", "moe_silu",
             "moe_gated", "moe_act_turned", "moe_act_kept", "moe_rows", "moe_rows_read")
    pick_step = core.sig("moe_pick_step")
    all_signals = [core.sig(n) for n in names]
    picked, gathered, kept, turned, tokens, hidden, silu, gated, act_turned, act_kept, rows_s, read_s = all_signals
    stored = [core.sig(f"moe_rows_stored{b}") for b in range(2)]
    with core.block() as block:
        @block.vector
        def _(dve):
            nc.vector.tensor_scalar(rel[:], slots[:], float(SLOTS), None, ALU.add)
            for s in all_signals:
                dve.sem_inc(s.sem, 1)
            for s in stored:
                dve.sem_inc(s.sem, 32)
            nc.vector.tensor_copy(slot_rows[:], slots[:])
            for act_rows in inner_act:
                nc.vector.memset(act_rows[:], 0.0)

    def count(j, per, more):
        i, c = j
        return i * (2 * per) + (c * per + more)

    def passed(eng, signal, j, back=0):
        eng.wait_ge(signal.sem, count(j, 1, 2 - back))

    def load(sp, j, b, expert):
        for kind in kinds:
            passed(sp, rows_s if kind == "down" else hidden, j, 2)
            sp.dma_start(view[kind, b], w[kind][expert].rearrange("e p k n -> (e p) k n")).then_inc(landed[kind, b].sem, 16)

    def gather(pe, j, b, first=False):
        passed(pe, picked, j)
        if not first:
            passed(pe, kept, j, 2)
        for t in range(NT):
            for h, half in enumerate(halves):
                last = nc.tensor.matmul(pick_bank[b][half, :], pick[b][0][:, t, :], xn[:, t, h * SEQ:(h + 1) * SEQ],
                                        start=(t == 0), stop=(t == NT - 1))
        last.then_inc(gathered.sem, 1)

    def turn_rows(pe, j, b, first=False):
        passed(pe, kept, j)
        if not first:
            passed(pe, tokens, j, 1)
        for c in range(KD // 2):
            last = nc.tensor.transpose(xT_bank[:, c * P:(c + 1) * P], picked_rows[b][:, c * P:(c + 1) * P], core.ident)
        last.then_inc(turned.sem, 1)

    def expand(pe, j, b, uses, first=False):
        passed(pe, tokens, j)
        if not first:
            passed(pe, gated, j, 2)
        for kind in ("gate", "up"):
            pe.wait_ge(landed[kind, b].sem, uses * 16)
        for k in range(KD):
            for kind, half in (("gate", top_half), ("up", low_half)):
                last = nc.tensor.matmul(h_bank[b][half, :], xT[b][:, k, :], view[kind, b][:, k, :],
                                        start=(k == 0), stop=(k == KD - 1))
        last.then_inc(hidden.sem, 1)

    def turn_act(pe, j, b, first=False):
        passed(pe, gated, j)
        if not first:
            passed(pe, act_kept, j, 1)
        for f in range(4):
            last = nc.tensor.transpose(actT_bank[:, f * P:(f + 1) * P], inner_act[b][:, f * P:(f + 1) * P], core.ident)
        last.then_inc(act_turned.sem, 1)

    def contract(pe, j, b, uses, first=False):
        passed(pe, act_kept, j)
        if not first:
            passed(pe, read_s, j, 2)
        pe.wait_ge(landed["down", b].sem, uses * 16)
        for f in range(4):
            for h, half in enumerate(halves):
                last = nc.tensor.matmul(y_bank[b][half, :], actT[b][:, f, :], view["down", b][:, f, h * SEQ:(h + 1) * SEQ],
                                        start=(f == 0), stop=(f == 3))
        last.then_inc(rows_s.sem, 1)

    def pick_tokens(dve, j, b, first=False):
        nc.vector.tensor_scalar(rel[:], rel[:], -float(SLOTS), None, ALU.add).then_inc(pick_step.sem, 1)
        dve.wait_ge(pick_step.sem, count(j, 3, 1))
        if not first:
            passed(dve, gathered, j, 2)
        for c in range(2):
            nc.vector.tensor_tensor(pick[b][c][:], iota[:, 0:SLOTS].unsqueeze(1).to_broadcast([P, NT, SLOTS]),
                                    rel[:, :, c:c + 1].to_broadcast([P, NT, SLOTS]), ALU.is_equal).then_inc(pick_step.sem, 1)
        dve.wait_ge(pick_step.sem, count(j, 3, 3))
        nc.vector.tensor_tensor(pick[b][0][:], pick[b][0][:], pick[b][1][:], ALU.add).then_inc(picked.sem, 1)

    def take_tokens(dve, j, b, first=False):
        passed(dve, turned, j)
        if not first:
            passed(dve, hidden, j, 2)
        nc.vector.tensor_tensor(xT[b][:].rearrange("p (h c) s -> p h c s", h=2),
                                xT_bank[:].rearrange("p (c h s) -> p h c s", c=4, h=2),
                                gain.rearrange("p (h c) -> p h c", h=2).unsqueeze(3).to_broadcast([P, 2, 4, SLOTS]),
                                ALU.mult).then_inc(tokens.sem, 1)

    def gate_hidden(dve, j, b, first=False):
        passed(dve, silu, j)
        if not first:
            passed(dve, act_turned, j, 2)
        nc.vector.tensor_tensor(inner_act[b][low_half, :], silu_up[b][low_half, :], h_bank[b][low_half, :], ALU.mult
                                ).then_inc(gated.sem, 1)

    def keep_rows(act, j, b, first=False):
        passed(act, gathered, j)
        if not first:
            passed(act, turned, j, 2)
        nc.scalar.copy(picked_rows[b][:], pick_bank[b][:]).then_inc(kept.sem, 1)

    def take_silu(act, j, b, first=False):
        passed(act, hidden, j)
        if not first:
            passed(act, gated, j, 2)
        nc.scalar.activation(silu_up[b][low_half, :], h_bank[b][top_half, :], ACT.Silu).then_inc(silu.sem, 1)

    def keep_act(act, j, b, first=False):
        passed(act, act_turned, j)
        if not first:
            passed(act, rows_s, j, 2)
        nc.scalar.copy(actT[b][:], actT_bank[:].rearrange("p (f h s) -> p f h s", f=4, h=2)[:, :, 1, :]).then_inc(act_kept.sem, 1)

    def store_rows(act, j, b, uses):
        passed(act, rows_s, j)
        act.wait_ge(stored[b].sem, uses * 32)
        nc.scalar.copy(rows[b][:], y_bank[b][:]).then_inc(read_s.sem, 1)
        passed(act, read_s, j)
        for h, half in enumerate(halves):
            act.dma_start(expert_rows[bass.ds(count(j, SLOTS, 0), SLOTS), h * SEQ:(h + 1) * SEQ], rows[b][half, :]
                          ).then_inc(stored[b].sem, 16)

    PAIRS = N_EXPERTS // 2
    END = (0, N_EXPERTS - 1)
    with core.block() as block:
        @block.sync
        def _(sp):
            with sp.Fori(0, PAIRS - 1) as i:
                for b in range(2):
                    load(sp, (i, 2 + b), b, bass.ds(i * 2 + 2 + b, 1))

        @block.tensor
        def _(pe):
            gather(pe, (0, 0), 0, True)
            turn_rows(pe, (0, 0), 0, True)
            gather(pe, (0, 1), 1, True)
            expand(pe, (0, 0), 0, 1, True)
            turn_rows(pe, (0, 1), 1)
            turn_act(pe, (0, 0), 0, True)
            with pe.Fori(0, PAIRS - 1) as i:
                for b, ahead in ((1, 0), (0, 1)):
                    j, before, after = (i, 1 + ahead), (i, ahead), (i, 2 + ahead)
                    gather(pe, after, 1 - b)
                    contract(pe, before, 1 - b, i + 1)
                    expand(pe, j, b, i + 1 + ahead)
                    turn_rows(pe, after, 1 - b)
                    turn_act(pe, j, b)
            contract(pe, (0, N_EXPERTS - 2), 0, PAIRS)
            expand(pe, END, 1, PAIRS)
            turn_act(pe, END, 1)
            contract(pe, END, 1, PAIRS)

        @block.vector
        def _(dve):
            pick_tokens(dve, (0, 0), 0, True)
            pick_tokens(dve, (0, 1), 1, True)
            take_tokens(dve, (0, 0), 0, True)
            pick_tokens(dve, (0, 2), 0)
            gate_hidden(dve, (0, 0), 0, True)
            take_tokens(dve, (0, 1), 1, True)
            with dve.Fori(0, PAIRS - 1) as i:
                for b, ahead in ((1, 0), (0, 1)):
                    j, after, later = (i, 1 + ahead), (i, 2 + ahead), (i, 3 + ahead)
                    pick_tokens(dve, later, b)
                    gate_hidden(dve, j, b)
                    take_tokens(dve, after, 1 - b)
            gate_hidden(dve, END, 1)

        @block.scalar
        def _(act):
            keep_rows(act, (0, 0), 0, True)
            keep_rows(act, (0, 1), 1, True)
            take_silu(act, (0, 0), 0, True)
            keep_act(act, (0, 0), 0, True)
            with act.Fori(0, PAIRS - 1) as i:
                for b, ahead in ((1, 0), (0, 1)):
                    j, before, after = (i, 1 + ahead), (i, ahead), (i, 2 + ahead)
                    keep_rows(act, after, 1 - b)
                    store_rows(act, before, 1 - b, i + 1)
                    take_silu(act, j, b)
                    keep_act(act, j, b)
            store_rows(act, (0, N_EXPERTS - 2), 0, PAIRS)
            take_silu(act, END, 1)
            keep_act(act, END, 1)
            store_rows(act, END, 1, PAIRS)
            for b in range(2):
                act.wait_ge(stored[b].sem, 32 * (PAIRS + 1))

    def overflow(eng, body):
        n_over = eng.value_load(over[0:1, N_OVER:N_OVER + 1], min_val=0, max_val=N_OVER)
        with eng.Fori(0, N_OVER // 2) as i:
            with eng.If(i * 2 < n_over):
                for b in range(2):
                    body(i, (i, N_EXPERTS + b), b)

    with core.block() as block:
        @block.sync
        def _(sp):
            def body(i, j, b):
                expert = sp.value_load(over[0:1, bass.ds(i * 2 + b, 1)], min_val=0, max_val=N_EXPERTS - 1)
                load(sp, j, b, bass.ds(expert, 1))
            overflow(sp, body)

        @block.tensor
        def _(pe):
            def body(i, j, b):
                gather(pe, j, b)
                turn_rows(pe, j, b)
                expand(pe, j, b, i + PAIRS + 1)
                turn_act(pe, j, b)
                contract(pe, j, b, i + PAIRS + 1)
            overflow(pe, body)

        @block.vector
        def _(dve):
            def body(i, j, b):
                pick_tokens(dve, (i, N_EXPERTS + b + 1), 1 - b)
                take_tokens(dve, j, b)
                gate_hidden(dve, j, b)
            overflow(dve, body)

        @block.scalar
        def _(act):
            act.wait_ge(*cleared_dma.now())

            def body(i, j, b):
                keep_rows(act, j, b)
                take_silu(act, j, b)
                keep_act(act, j, b)
                store_rows(act, j, b, i + PAIRS + 1)
                act.wait_ge(stored[b].sem, (i + PAIRS + 2) * 32)
                if b == 1:
                    nc.scalar.copy(landed_mark[:], iota[0:1, 0:1])
            overflow(act, body)
    inner.close()

    inner = ExitStack()
    got = [core.sb(inner, f"got{b}", [P, D]) for b in range(2 * NT)]
    fetched = [core.sig(f"expert_rows_fetched{t}") for t in range(NT)]
    added = core.sig("expert_rows_added")
    with core.block() as block:
        @block.gpsimd
        def _(pool):
            for t in range(NT):
                for c in range(2):
                    pool.indirect_dma_start(got[2 * t + c][:], None, expert_rows,
                                            bass.IndirectOffsetOnAxis(ap=slot_rows[:, t, c:c + 1], axis=0)
                                            ).then_inc(*fetched[t].up(16))

        @block.vector
        def _(dve):
            for t in range(NT):
                dve.wait_ge(*fetched[t].at(32))
                for c in range(2):
                    nc.vector.scalar_tensor_tensor(out=x[:, t, :], in0=got[2 * t + c][:], scalar=gates[:, t, c:c + 1],
                                                   in1=x[:, t, :], op0=ALU.mult, op1=ALU.add).then_inc(*added.up())
                    dve.wait_ge(*added.at(2 * t + c + 1))

        @block.sync
        def _(sp):
            for t in range(NT):
                sp.wait_ge(*added.at(2 * t + 2))
                sp.dma_start(core.out[0, t * P:(t + 1) * P, :], x[:, t, :]).then_inc(*core.stored.up(16))
            sp.wait_ge(*core.stored.at(16 * NT))
    inner.close()
    st.close()


def build_program(nc, ins, out):
    core = Core(nc, ins, out)
    core.const_at = CONST_AT
    top = ExitStack()
    ident = core.sb(top, "ident", [P, P])
    ones = core.sb(top, "ones", [P, P])
    upto_m = core.sb(top, "upto", [P, P])
    eps = core.sb(top, "eps", [P, 1])
    gn_eps = core.sb(top, "gn_eps", [P, 1])
    one = core.sb(top, "one", [P, 1])
    core.ident, core.ones, core.upto, core.eps, core.gn_eps, core.one = ident[:], ones[:], upto_m[:], eps, gn_eps, one
    gains = core.sb(top, "norm_gains", [P, 5, KD])
    x = core.sb(top, "x", [P, NT, D])

    w_in = ins["w_in"][0].rearrange("(k p) n -> p k n", p=P)
    w_in_2 = ins["w_in_2"][0].rearrange("(k p) n -> p k n", p=P)

    def cols(name, at, n, src=w_in):
        return (name, src[:, :, at:at + n], KD, n)

    def merge_items(n):
        gates = [cols(f"merge{n}_{h}", AT["merge_gate"] + n * D + h * SEQ, SEQ) for h in range(2)]
        return [gates[0], (f"w_br{n}", ins["w_br"][0, n].rearrange("(k p) n -> p k n", p=P), 4, D), gates[1]]

    def halves(name, src, base=0):
        w = src.rearrange("(k p) n -> p k n", p=P)
        return [cols(f"{name}{h}", base + h * SEQ, SEQ, w) for h in range(2)]

    items = [cols(f"gdn_{c}", AT[f"gdn_{c}"], 512) for c in "qkvz"] + merge_items(0)
    items += [cols("gla_qk", AT["gla_q"], 512), cols("gla_v", AT["gla_v"], 512), cols("gla_z", AT["gla_z"], 512)] + merge_items(1)
    items += [cols("ssd_x", AT["ssd_x"], 512), cols("ssd_bc", AT["ssd_b"], 512), cols("ssd_z", AT["ssd_z"], 512)] + merge_items(2)
    items += [cols("nsa_q", AT["nsa_q"], 512), cols("nsa_kv", AT["nsa_kc"], 512), cols("nsa_w", AT["nsa_kw"], 256),
              cols("nsa_z", AT["nsa_z"], 512)] + merge_items(3)
    items += halves("w_out", ins["w_out"][0])
    for n, name in enumerate(("mix_q", "mix_k", "mix_v", "mix_rqk", "mix_rv", "mix_rg")):
        items.append(cols(name, 512 * n, 512, w_in_2))
    items += halves("w_out_2", ins["w_out_2"][0])
    items += halves("mem_q", ins["w_mq_2"][0]) + halves("mem_k", ins["w_mkv_2"][0]) + halves("mem_v", ins["w_mkv_2"][0], D)
    items += halves("mem_o", ins["w_mo_2"][0])

    xin = ins["x"][0].rearrange("(t p) d -> p t d", p=P)
    body = ExitStack()
    stream = Stream(core, body, 3, items)
    b1 = ExitStack()
    merged = core.sb(b1, "merged", [P, NT, D])
    w_small = merged[:, 0, 0:KD * 56].rearrange("p (k n) -> p k n", k=KD)
    head_par = merged[:, 1, 0:24]
    small_of = {n: core.sb(b1, n, s) for n, s in (
        ("conv_a", [P, 12, 4]), ("conv_c", [P, 8, 4]), ("conv_bias_c", [P, 8]), ("d_skip_c", [P, 8]))}
    small_landed = core.sig("small_weights_landed")
    small_loads = [(w_small[:, :, a:a + n], w_in[:, :, AT[c]:AT[c] + n]) for a, n, c in (
        (0, 16, "gla_gk"), (16, 8, "gdn_beta"), (24, 8, "ssd_dt"), (32, 24, "nsa_gate"))]
    small_loads += [(head_par[:, a:a + n], ins[c].to_broadcast([P, n])) for a, n, c in (
        (0, 4, "a_log_a"), (4, 8, "a_log_c"), (12, 4, "dt_bias_a"), (16, 8, "dt_bias_c"))]
    small_loads += [(small_of[n][:], ins[n]) for n in ("conv_a", "conv_c", "conv_bias_c")]
    small_loads += [(small_of["d_skip_c"][:], ins["d_skip_c"].to_broadcast([P, 8]))]
    with core.block() as block:
        @block.sync
        def _(sp):
            loads = [(x[:], xin), (ident[:], core.const("ident")), (ones[:], core.const("ones")),
                     (upto_m[:], core.const("upto")), (gains[:], ins["norm_gains"])]
            for dst, src in loads:
                sp.dma_start(dst, src).then_inc(*core.dma.up(16))
            for dst, src in small_loads:
                sp.dma_start(dst, src).then_inc(*small_landed.up(16))
            for _ in range(stream.slots):
                stream.load(sp)
            sp.wait_ge(*core.dma.at(16 * len(loads)))

        @block.vector
        def _(dve):
            nc.vector.memset(eps[:], EPS)
            nc.vector.memset(gn_eps[:], GN_EPS)
            nc.vector.memset(one[:], 1.0)

    hT = core.sb(b1, "hT", [P, 2, KD, SEQ], F32R)
    norm_to_channels(core, x, NT, gains[:, 0, :], hT)
    dec = {n: core.sb(b1, n, [P, NT, w]) for n, w in (("rate", 12), ("dt", 12), ("cum", 12), ("e_cum", 12),
                                                      ("e_rest", 12), ("e_total", 12), ("beta", 4), ("gates", 24))}
    gkT = core.sb(b1, "gkT", [16, SEQ])
    inner = ExitStack()
    small = core.sb(inner, "small", [P, NT, 40])
    w_pair = core.sb(inner, "w_small_split", [P, 2, KD, 56], F32R)
    with core.block() as block:
        @block.sync
        def _(sp):
            sp.wait_ge(*small_landed.now())

        @block.scalar
        def _(act):
            act.wait_ge(*small_landed.now())
            nc.scalar.copy(w_pair[:, 0], w_small).then_inc(*core.rounded.up())

        @block.vector
        def _(dve):
            dve.wait_ge(*core.rounded.at(1))
            nc.vector.tensor_tensor(w_pair[:, 1], w_small, w_pair[:, 0], ALU.subtract)
    small_products(core, stream, hT, w_pair, small, gkT)
    decay_rates(core, small, head_par, dec["rate"], dec["dt"], dec["gates"], dec["beta"])
    decay_sums(core, dec["rate"], core.upto, dec["cum"], dec["e_cum"], dec["e_rest"], dec["e_total"])
    inner.close()

    norm_landed = core.sig("head_gain_landed")

    def finish_branch(n, y, head_norm, z, order):
        heads, width, gain = head_norm
        if heads:
            with core.block() as block:
                @block.sync
                def _(sp):
                    sp.wait_ge(*norm_landed.now())
        if order == ("norm", "gate"):
            gate_with_z(core, stream, hT, z, y, (heads, width, gain[:]))
        else:
            gate_with_z(core, stream, hT, z, y)
            if "norm" in order:
                head_rms(core, y, heads, width, gain[:])
        st = ExitStack()
        yT = core.sb(st, "yT", [P, 2, 4, SEQ], F32R)
        to_channels(core, y, yT, 4)
        merge_branch(core, stream, hT, yT, n, merged)
        st.close()

    branches = (
        (lambda y: gdn(core, stream, hT, dec, y, small_of), (4, P, ins["onorm_a"]), "gdn_z", ("norm", "gate")),
        (lambda y: gla(core, stream, hT, gkT, y), (4, P, ins["onorm_b"]), "gla_z", ("norm", "gate")),
        (lambda y: ssd(core, stream, hT, dec, y, small_of), (1, SEQ, ins["onorm_c"]), "ssd_z", ("gate", "norm")),
        (lambda y: nsa(core, stream, hT, dec["gates"], y), (0, 0, None), "nsa_z", ("gate",)),
    )
    for n, (run, norm, z, order) in enumerate(branches):
        st = ExitStack()
        y = core.sb(st, "y", [P, NT, SEQ])
        heads, width, src = norm
        if heads:
            gain = core.sb(st, "head_gain", [P, width])
            norm = heads, width, gain
            with core.block() as block:
                @block.sync
                def _(sp):
                    sp.dma_start(gain[:], src.to_broadcast([P, width])).then_inc(*norm_landed.up(16))
        run(y)
        finish_branch(n, y, norm, z, order)
        st.close()
    inner = ExitStack()
    gain = core.sb(inner, "gain", [P, D])
    post_gain = core.sig("post_gain_landed")
    with core.block() as block:
        @block.sync
        def _(sp):
            sp.dma_start(gain[:], ins["norm_post"].to_broadcast([P, D])).then_inc(*post_gain.up(16))
    to_channels(core, merged, hT, KD)
    project_out(core, stream, hT, ("w_out0", "w_out1"), merged, False)
    with core.block() as block:
        @block.sync
        def _(sp):
            sp.wait_ge(*post_gain.now())
    post_norm_residual(core, x, merged, gain[:])
    inner.close()
    b1.close()

    b2 = ExitStack()
    hT = core.sb(b2, "hT", [P, 2, KD, SEQ], F32R)
    y = core.sb(b2, "y", [P, NT, D])
    mem = core.sb(b2, "mem", [P, 2, D])
    mem_landed = core.sig("memory_landed")
    with core.block() as block:
        @block.sync
        def _(sp):
            sp.dma_start(mem[:], ins["mem_2"][0].rearrange("(t p) d -> p t d", p=P)).then_inc(*mem_landed.up(16))
    norm_to_channels(core, x, NT, gains[:, 1, :], hT)
    mixer(core, stream, hT, y)
    to_channels(core, y, hT, KD)
    project_out(core, stream, hT, ("w_out_20", "w_out_21"), x, True)
    norm_to_channels(core, x, NT, gains[:, 2, :], hT)
    inner = ExitStack()
    memT = core.sb(inner, "memT", [P, 2, KD, N_MEM], F32R)
    with core.block() as block:
        @block.sync
        def _(sp):
            sp.wait_ge(*mem_landed.now())
    norm_to_channels(core, mem, 2, gains[:, 3, :], memT)
    cross_attention(core, stream, hT, memT, y)
    inner.close()
    to_channels(core, y, hT, KD)
    project_out(core, stream, hT, ("mem_o0", "mem_o1"), x, True)
    b2.close()
    body.close()
    moe(core, x, gains[:, 4, :])


CONST_AT, CONSTANTS = shape_constants()


def lay_out(inputs):
    a = {k: np.ascontiguousarray(v) for k, v in inputs.items()}
    by_channel = lambda v: np.ascontiguousarray(v.reshape(-1, P).T)
    for name in ("conv_a", "conv_c"):
        w = a[name][0]
        a[name] = np.ascontiguousarray(w.T.reshape(-1, P, w.shape[0]).transpose(1, 0, 2))
    a["conv_bias_c"] = by_channel(a["conv_bias_c"])
    a["norm_gains"] = np.ascontiguousarray(np.stack([by_channel(a.pop(n)) for n in (
        "norm_pre", "norm_mix_w_2", "norm_mem_w_2", "norm_memkv_w_2", "norm_moe_w_2")], axis=1))
    q, k = a.pop("attn_q_norm_w_2")[0], a.pop("attn_k_norm_w_2")[0]
    a["mix_qk_gain"] = np.ascontiguousarray(np.stack([np.concatenate([q, q]), np.concatenate([k, k])], axis=1))
    q, k = a.pop("mem_q_norm_w_2")[0], a.pop("mem_k_norm_w_2")[0]
    a["mem_qk_gain"] = np.ascontiguousarray(np.stack([q[:P], q[P:], k[:P], k[P:]], axis=1))
    for c in "kv":
        a[f"w_c{c}1"] = np.ascontiguousarray(a[f"w_c{c}1"][0].reshape(16, P, 64).transpose(1, 0, 2))
        a[f"cmp_pos_{c}"] = np.ascontiguousarray(a[f"cmp_pos_{c}"][0].reshape(16, P).T)
    a["w_router_2"] = np.ascontiguousarray(a["w_router_2"][0].transpose(1, 0, 2).reshape(D, N_EXPERTS))
    q = slice(AT["nsa_q"], AT["nsa_q"] + 512)
    w = a["w_in"].copy()
    w[..., q] = w[..., q].reshape(1, D, 2, 4, 64).transpose(0, 1, 3, 2, 4).reshape(1, D, 512)
    a["w_in"] = w
    a["shape_constants"] = CONSTANTS
    return a


def kernel(**inputs):
    import concourse.bacc as bacc
    from concourse.bass_utils import run_bass_kernel_spmd as run

    nc = bacc.Bacc("TRN2", target_bir_lowering=False, num_devices=1)
    arrays = lay_out(inputs)
    ins = {n: nc.dram_tensor(n, a.shape, mybir.dt.from_np(a.dtype), kind="ExternalInput").ap() for n, a in arrays.items()}
    out = nc.dram_tensor("out", (1, SEQ, D), F32, kind="ExternalOutput").ap()
    build_program(nc, ins, out)
    return run(nc, [arrays], core_ids=[0]).results[0]["out"]
```
